# Optimizing a Trainium2 kernel written in Bass

```python
import jax
import jax.numpy as jnp
from jax import lax
import numpy as np
import math

D_MODEL = 1024
BATCH = 1
SEQ = 512
DEPTH = 1

ATT_HEADS = 8
ATT_KV_HEADS = 2
ATT_HEAD_DIM = 128
ATT_GROUP = ATT_HEADS // ATT_KV_HEADS
ROPE_THETA = 500000.0
ROPE_FRACTION = 4
IDX_HEADS = 4
IDX_DIM = 64
TOPK_MAX = 256
Q_BLOCK = 128
SSM_EXPAND = 2
SSM_D_INNER = SSM_EXPAND * D_MODEL
SSM_HEAD_DIM = 64
SSM_HEADS = SSM_D_INNER // SSM_HEAD_DIM
SSM_GROUPS = 4
SSM_STATE = 128
SSM_CONV = 4
SSM_CHUNK = 128
N_BRANCHES = 2
EPS = 1e-6

ATT_Q_DIM = ATT_HEADS * ATT_HEAD_DIM
ATT_KV_DIM = ATT_KV_HEADS * ATT_HEAD_DIM
ATT_ROT_DIM = ATT_HEAD_DIM // ROPE_FRACTION
IDX_ROT_DIM = IDX_DIM // ROPE_FRACTION
SSM_CONV_DIM = SSM_D_INNER + 2 * SSM_GROUPS * SSM_STATE
IN_SPLITS = (ATT_Q_DIM, ATT_KV_DIM, ATT_KV_DIM, ATT_Q_DIM, IDX_HEADS * IDX_DIM, IDX_DIM, IDX_HEADS,
             SSM_D_INNER, SSM_CONV_DIM, SSM_HEADS, N_BRANCHES * D_MODEL)
IN_DIM = sum(IN_SPLITS)


def _split_points():
    pts, acc = [], 0
    for s in IN_SPLITS[:-1]:
        acc += s
        pts.append(acc)
    return pts

def rms_norm(x, g):
    xf = x.astype(jnp.float32)
    y = xf * lax.rsqrt(jnp.mean(xf * xf, axis=-1, keepdims=True) + EPS)
    return y.astype(x.dtype) * g

def layer_norm(x, g, b):
    xf = x.astype(jnp.float32)
    mu = jnp.mean(xf, axis=-1, keepdims=True)
    var = jnp.mean(jnp.square(xf - mu), axis=-1, keepdims=True)
    return ((xf - mu) * lax.rsqrt(var + EPS)).astype(x.dtype) * g + b

def rope_tables(positions, rot_dim):
    inv = jnp.power(ROPE_THETA, -(jnp.arange(0, rot_dim, 2, dtype=jnp.float32) / rot_dim))
    ang = positions.astype(jnp.float32)[..., None] * inv
    return jnp.cos(ang)[:, :, None, :], jnp.sin(ang)[:, :, None, :]

def partial_rope(x, cos, sin):
    half = cos.shape[-1]
    rot = 2 * half
    x1 = x[..., :half].astype(jnp.float32)
    x2 = x[..., half:rot].astype(jnp.float32)
    r1 = x1 * cos - x2 * sin
    r2 = x2 * cos + x1 * sin
    return jnp.concatenate([r1.astype(x.dtype), r2.astype(x.dtype), x[..., rot:]], axis=-1)

def causal_depthwise_conv(u, w, b):
    ch = u.shape[-1]
    y = lax.conv_general_dilated(u, w[:, None, :].astype(u.dtype), window_strides=(1,),
                                 padding=[(SSM_CONV - 1, 0)],
                                 dimension_numbers=("NWC", "WIO", "NWC"),
                                 feature_group_count=ch)
    return y + b

def segsum(a):
    n = a.shape[-1]
    ar = jnp.broadcast_to(a[..., :, None], a.shape + (n,))
    ar = jnp.where(jnp.tril(jnp.ones((n, n), dtype=bool), -1), ar, 0.0)
    cs = jnp.cumsum(ar, axis=-2)
    return jnp.where(jnp.tril(jnp.ones((n, n), dtype=bool)), cs, -jnp.inf)

def ssd(xh, dt, a, bm, cm):
    bsz, s, h, p = xh.shape
    g, n = bm.shape[2], bm.shape[3]
    r = h // g
    nc, ln = s // SSM_CHUNK, SSM_CHUNK
    xc = (xh * dt[..., None]).reshape(bsz, nc, ln, g, r, p)
    adt = (dt * a).reshape(bsz, nc, ln, g, r).transpose(0, 1, 3, 4, 2)
    a_cum = jnp.cumsum(adt, axis=-1)
    bc = bm.reshape(bsz, nc, ln, g, n)
    cc = cm.reshape(bsz, nc, ln, g, n)
    decay = jnp.exp(segsum(adt))
    cb = jnp.einsum("bclgn,bcsgn->bcgls", cc, bc)
    y_diag = jnp.einsum("bcgls,bcgrls,bcsgrp->bclgrp", cb, decay, xc)
    decay_states = jnp.exp(a_cum[..., -1:] - a_cum)
    states = jnp.einsum("bclgn,bcgrl,bclgrp->bcgrpn", bc, decay_states, xc)
    chunk_decay = jnp.exp(a_cum[..., -1])

    def step(hstate, inp):
        st, dec = inp
        return dec[..., None, None] * hstate + st, hstate

    h0 = jnp.zeros((bsz, g, r, p, n), dtype=xc.dtype)
    _, prev = lax.scan(step, h0, (states.swapaxes(0, 1), chunk_decay.swapaxes(0, 1)))
    prev = prev.swapaxes(0, 1)
    y_off = jnp.einsum("bclgn,bcgrpn,bcgrl->bclgrp", cc, prev, jnp.exp(a_cum))
    return (y_diag + y_off).reshape(bsz, s, h, p)

def sparse_attention(q, k, v, q_idx, k_idx, w_idx):
    bsz, s = q.shape[0], q.shape[1]
    topk = min(TOPK_MAX, s // 4)
    nblk = s // Q_BLOCK
    scale = ATT_HEAD_DIM ** -0.5
    key_pos = jnp.arange(s)
    gather = jax.vmap(lambda arr, idx: arr[idx])

    def to_blocks(arr):
        return arr.reshape((bsz, nblk, Q_BLOCK) + arr.shape[2:]).swapaxes(0, 1)

    qg = q.reshape(bsz, s, ATT_KV_HEADS, ATT_GROUP, ATT_HEAD_DIM)

    def block(args):
        blk, qb, qib, wb = args
        qpos = blk * Q_BLOCK + jnp.arange(Q_BLOCK)
        causal = key_pos[None, :] <= qpos[:, None]
        logits = jnp.einsum("bthd,bsd->bths", qib, k_idx)
        score = jnp.einsum("bth,bths->bts", wb, jax.nn.relu(logits))
        score = jnp.where(causal[None], score, -jnp.inf)
        _, sel = lax.top_k(score, topk)
        valid = sel <= qpos[None, :, None]
        ks = gather(k, sel)
        vs = gather(v, sel)
        sc = jnp.einsum("btgrd,btjgd->btgrj", qb, ks).astype(jnp.float32) * scale
        sc = jnp.where(valid[:, :, None, None, :], sc, -jnp.inf)
        pr = jax.nn.softmax(sc, axis=-1).astype(vs.dtype)
        return jnp.einsum("btgrj,btjgd->btgrd", pr, vs)

    out = lax.map(block, (jnp.arange(nblk), to_blocks(qg), to_blocks(q_idx), to_blocks(w_idx)))
    return out.swapaxes(0, 1).reshape(bsz, s, ATT_Q_DIM)

def first_inputs(seed: int = 0) -> dict:
    key = jax.random.key(seed)
    ks = jax.random.split(key, 24)
    nrm = jax.random.normal
    f32 = jnp.float32
    dt0 = jnp.exp(jax.random.uniform(ks[14], (DEPTH, SSM_HEADS), dtype=f32)
                  * (np.log(0.1) - np.log(0.001)) + np.log(0.001))
    return {
        "x": nrm(ks[0], (BATCH, SEQ, D_MODEL), f32),
        "c": nrm(ks[1], (BATCH, D_MODEL), f32),
        "positions": jnp.broadcast_to(jnp.arange(SEQ, dtype=jnp.int32)[None, :], (BATCH, SEQ)),
        "ada_w": nrm(ks[2], (DEPTH, D_MODEL, 3 * D_MODEL), f32) * (0.5 * D_MODEL ** -0.5),
        "ada_b": nrm(ks[3], (DEPTH, 3 * D_MODEL), f32) * 0.01,
        "norm_g": 1.0 + 0.1 * nrm(ks[4], (DEPTH, D_MODEL), f32),
        "w_in": nrm(ks[5], (DEPTH, D_MODEL, IN_DIM), f32) * D_MODEL ** -0.5,
        "q_norm_g": 1.0 + 0.1 * nrm(ks[6], (DEPTH, ATT_HEAD_DIM), f32),
        "k_norm_g": 1.0 + 0.1 * nrm(ks[7], (DEPTH, ATT_HEAD_DIM), f32),
        "idx_k_ln_g": 1.0 + 0.1 * nrm(ks[8], (DEPTH, IDX_DIM), f32),
        "idx_k_ln_b": 0.01 * nrm(ks[9], (DEPTH, IDX_DIM), f32),
        "conv_w": nrm(ks[10], (DEPTH, SSM_CONV, SSM_CONV_DIM), f32) * SSM_CONV ** -0.5,
        "conv_b": 0.01 * nrm(ks[11], (DEPTH, SSM_CONV_DIM), f32),
        "dt_bias": dt0 + jnp.log(-jnp.expm1(-dt0)),
        "a_log": jnp.log(jax.random.uniform(ks[12], (DEPTH, SSM_HEADS), f32, 1.0, 16.0)),
        "d_skip": 1.0 + 0.1 * nrm(ks[13], (DEPTH, SSM_HEADS), f32),
        "ssm_norm_g": 1.0 + 0.1 * nrm(ks[15], (DEPTH, SSM_D_INNER), f32),
        "w_branch_att": nrm(ks[16], (DEPTH, ATT_Q_DIM, D_MODEL), f32) * ATT_Q_DIM ** -0.5,
        "w_branch_ssm": nrm(ks[17], (DEPTH, SSM_D_INNER, D_MODEL), f32) * SSM_D_INNER ** -0.5,
        "w_out": nrm(ks[18], (DEPTH, D_MODEL, D_MODEL), f32) * D_MODEL ** -0.5,
    }

def first_block(x, c, positions, ada_w, ada_b, norm_g, w_in, q_norm_g, k_norm_g, idx_k_ln_g, idx_k_ln_b,
              conv_w, conv_b, dt_bias, a_log, d_skip, ssm_norm_g, w_branch_att, w_branch_ssm, w_out):
    f32 = jnp.float32
    bsz, s, _ = x.shape
    cos_a, sin_a = rope_tables(positions, ATT_ROT_DIM)
    cos_i, sin_i = rope_tables(positions, IDX_ROT_DIM)
    pts = _split_points()
    for l in range(DEPTH):
        mod = jax.nn.silu(c) @ ada_w[l] + ada_b[l]
        shift, scale, gate = jnp.split(mod, 3, axis=-1)
        h = rms_norm(x, norm_g[l]) * (1.0 + scale[:, None, :]) + shift[:, None, :]
        proj = h @ w_in[l]
        (q, k, v, z_att, q_idx, k_idx, w_idx, z_ssm, xbc, dt_raw, gate_logits) = jnp.split(proj, pts, axis=-1)

        q = partial_rope(rms_norm(q.reshape(bsz, s, ATT_HEADS, ATT_HEAD_DIM), q_norm_g[l]), cos_a, sin_a)
        k = partial_rope(rms_norm(k.reshape(bsz, s, ATT_KV_HEADS, ATT_HEAD_DIM), k_norm_g[l]), cos_a, sin_a)
        v = v.reshape(bsz, s, ATT_KV_HEADS, ATT_HEAD_DIM)
        q_idx = partial_rope(q_idx.reshape(bsz, s, IDX_HEADS, IDX_DIM), cos_i, sin_i) * (IDX_DIM ** -0.5)
        k_idx = partial_rope(layer_norm(k_idx, idx_k_ln_g[l], idx_k_ln_b[l])[:, :, None, :], cos_i, sin_i)[:, :, 0, :]
        w_idx = w_idx * (IDX_HEADS ** -0.5)
        o_att = sparse_attention(q, k, v, q_idx, k_idx, w_idx) * jax.nn.silu(z_att)
        y_att = o_att @ w_branch_att[l]

        xbc = jax.nn.silu(causal_depthwise_conv(xbc, conv_w[l], conv_b[l]))
        xs, bm, cm = jnp.split(xbc, [SSM_D_INNER, SSM_D_INNER + SSM_GROUPS * SSM_STATE], axis=-1)
        xs = xs.reshape(bsz, s, SSM_HEADS, SSM_HEAD_DIM).astype(f32)
        dt = jax.nn.softplus(dt_raw.astype(f32) + dt_bias[l].astype(f32))
        a = -jnp.exp(a_log[l].astype(f32))
        y = ssd(xs, dt, a,
                bm.reshape(bsz, s, SSM_GROUPS, SSM_STATE).astype(f32),
                cm.reshape(bsz, s, SSM_GROUPS, SSM_STATE).astype(f32))
        y = y + d_skip[l].astype(f32)[:, None] * xs
        y = y.reshape(bsz, s, SSM_D_INNER).astype(x.dtype) * jax.nn.silu(z_ssm)
        y = rms_norm(y.reshape(bsz, s, SSM_GROUPS, SSM_D_INNER // SSM_GROUPS),
                     ssm_norm_g[l].reshape(SSM_GROUPS, SSM_D_INNER // SSM_GROUPS)).reshape(bsz, s, SSM_D_INNER)
        y_ssm = y @ w_branch_ssm[l]

        g_att, g_ssm = jnp.split(gate_logits, 2, axis=-1)
        merged = jax.nn.sigmoid(g_att) * y_att + jax.nn.sigmoid(g_ssm) * y_ssm
        x = x + gate[:, None, :] * (merged @ w_out[l])
    return x


CHUNK = 64

ATTN_HEAD_DIM = 64
ATTN_WIDTH = D_MODEL // 2
ATTN_HEADS = ATTN_WIDTH // ATTN_HEAD_DIM
LEFT_CHUNKS = 8
BAND = (LEFT_CHUNKS + 1) * CHUNK
REL_CLIP = 128
N_REL = 2 * REL_CLIP + 1

DN_HEAD_DIM = 128
DN_WIDTH = D_MODEL - ATTN_WIDTH
DN_HEADS = DN_WIDTH // DN_HEAD_DIM
CONV_WIDTH = 4

MIX_WIDTH = ATTN_WIDTH + DN_WIDTH
IN_PROJ_WIDTH = 3 * ATTN_WIDTH + 4 * DN_WIDTH + 2 * DN_HEADS

PEER_HEADS = 8
PEER_KEY_DIM = 256
PEER_HALF = PEER_KEY_DIM // 2
N_KEYS = 128
N_EXPERTS = N_KEYS * N_KEYS
PEER_TOPK = 16
PEER_BLOCK = 128


def rms_norm_2(x, gain):
    xf = x.astype(jnp.float32)
    y = xf * lax.rsqrt(jnp.mean(xf * xf, axis=-1, keepdims=True) + EPS)
    return (y * gain.astype(jnp.float32)).astype(x.dtype)

def l2_norm(x):
    xf = x.astype(jnp.float32)
    return xf * lax.rsqrt(jnp.sum(xf * xf, axis=-1, keepdims=True) + EPS)

def modulate(h, shift, scale):
    return h * (1.0 + scale) + shift

def chunked_band_attention(q, k, v, q_gain, k_gain, rel_bias):
    B, S = q.shape[:2]
    nc = S // CHUNK
    shp = (B, nc, CHUNK, ATTN_HEADS, ATTN_HEAD_DIM)
    pad = ((0, 0), (LEFT_CHUNKS, 0), (0, 0), (0, 0), (0, 0))
    q = rms_norm_2(q, q_gain).reshape(shp)
    k = jnp.pad(rms_norm_2(k, k_gain).reshape(shp), pad)
    v = jnp.pad(v.reshape(shp), pad)
    band_idx = np.arange(nc)[:, None] + np.arange(LEFT_CHUNKS + 1)[None, :]
    kb = k[:, band_idx].reshape(B, nc, BAND, ATTN_HEADS, ATTN_HEAD_DIM)
    vb = v[:, band_idx].reshape(B, nc, BAND, ATTN_HEADS, ATTN_HEAD_DIM)
    scores = jnp.einsum("bnqhd,bnkhd->bhnqk", q, kb,
                        preferred_element_type=jnp.float32) * (ATTN_HEAD_DIM ** -0.5)
    rel = np.arange(CHUNK)[:, None] + LEFT_CHUNKS * CHUNK - np.arange(BAND)[None, :]
    rel_idx = np.clip(rel, -REL_CLIP, REL_CLIP) + REL_CLIP
    bias = rel_bias.astype(jnp.float32)[:, rel_idx]
    valid = (np.arange(nc)[:, None] + np.arange(BAND)[None, :] // CHUNK) >= LEFT_CHUNKS
    scores = jnp.where(valid[None, None, :, None, :], scores + bias[None, :, None], -jnp.inf)
    p = jax.nn.softmax(scores, axis=-1).astype(vb.dtype)
    o = jnp.einsum("bhnqk,bnkhd->bnqhd", p, vb)
    return o.reshape(B, S, ATTN_WIDTH)

def causal_depthwise_conv_2(x, w):
    S = x.shape[1]
    xp = jnp.pad(x, ((0, 0), (CONV_WIDTH - 1, 0), (0, 0)))
    y = xp[:, 0:S] * w[0]
    for i in range(1, CONV_WIDTH):
        y = y + xp[:, i:i + S] * w[i]
    return jax.nn.silu(y)

def gated_delta_rule(q, k, v, g, beta):
    B, S, H, Dk = q.shape
    Dv = v.shape[-1]
    nc = S // CHUNK

    def to_chunks(t):
        return t.astype(jnp.float32).reshape(B, nc, CHUNK, H, -1).transpose(1, 0, 3, 2, 4)

    q = to_chunks(q) * (Dk ** -0.5)
    k = to_chunks(k)
    v = to_chunks(v)
    g = g.astype(jnp.float32).reshape(B, nc, CHUNK, H).transpose(1, 0, 3, 2)
    beta = beta.astype(jnp.float32).reshape(B, nc, CHUNK, H).transpose(1, 0, 3, 2)
    gc = jnp.cumsum(g, axis=-1)
    tri = np.tril(np.ones((CHUNK, CHUNK), dtype=bool))
    strict = np.tril(np.ones((CHUNK, CHUNK), dtype=bool), -1)
    decay = jnp.exp(jnp.where(tri, gc[..., :, None] - gc[..., None, :], -jnp.inf))
    k_beta = k * beta[..., None]
    v_beta = v * beta[..., None]
    lower = jnp.where(strict, jnp.einsum("nbhid,nbhjd->nbhij", k_beta, k) * decay, 0.0)
    rhs = jnp.concatenate([v_beta, k_beta * jnp.exp(gc)[..., None]], axis=-1)
    sol = lax.linalg.triangular_solve(jnp.eye(CHUNK, dtype=jnp.float32) + lower, rhs,
                                      left_side=True, lower=True, unit_diagonal=True)
    u = sol[..., :Dv]
    w = sol[..., Dv:]
    intra = jnp.einsum("nbhid,nbhjd->nbhij", q, k) * decay

    def step(state, xs):
        q_c, k_c, u_c, w_c, a_c, g_c = xs
        v_new = u_c - jnp.einsum("bhcd,bhde->bhce", w_c, state)
        o = (jnp.einsum("bhcd,bhde->bhce", q_c * jnp.exp(g_c)[..., None], state)
             + jnp.einsum("bhij,bhje->bhie", a_c, v_new))
        g_last = g_c[..., -1]
        k_dec = k_c * jnp.exp(g_last[..., None] - g_c)[..., None]
        state = state * jnp.exp(g_last)[..., None, None] + jnp.einsum("bhcd,bhce->bhde", k_dec, v_new)
        return state, o

    state0 = jnp.zeros((B, H, Dk, Dv), jnp.float32)
    _, o = lax.scan(step, state0, (q, k, u, w, intra, gc))
    return o.transpose(1, 0, 3, 2, 4).reshape(B, S, H, Dv)

def peer(h, w_query, query_gain, sub_keys_1, sub_keys_2, expert_down, expert_up):
    B, S, D = h.shape
    n_blocks = (B * S) // PEER_BLOCK

    def block(hb):
        qry = (hb @ w_query).reshape(PEER_BLOCK, PEER_HEADS, PEER_KEY_DIM)
        qry = rms_norm_2(qry, query_gain)
        s1 = jnp.einsum("thd,nd->thn", qry[..., :PEER_HALF], sub_keys_1, preferred_element_type=jnp.float32)
        s2 = jnp.einsum("thd,nd->thn", qry[..., PEER_HALF:], sub_keys_2, preferred_element_type=jnp.float32)
        v1, i1 = lax.top_k(s1, PEER_TOPK)
        v2, i2 = lax.top_k(s2, PEER_TOPK)
        cand_s = (v1[..., :, None] + v2[..., None, :]).reshape(PEER_BLOCK, PEER_HEADS, PEER_TOPK * PEER_TOPK)
        cand_i = (i1[..., :, None] * N_KEYS + i2[..., None, :]).reshape(PEER_BLOCK, PEER_HEADS, PEER_TOPK * PEER_TOPK)
        top_s, pos = lax.top_k(cand_s, PEER_TOPK)
        experts = jnp.take_along_axis(cand_i, pos, axis=-1)
        gates = jax.nn.softmax(top_s, axis=-1)
        u = expert_down[experts]
        vv = expert_up[experts]
        act = jax.nn.gelu(jnp.einsum("thkd,td->thk", u, hb, preferred_element_type=jnp.float32),
                          approximate=False)
        return jnp.einsum("thk,thkd->td", (gates * act).astype(vv.dtype), vv)

    out = lax.map(block, h.reshape(n_blocks, PEER_BLOCK, D))
    return out.reshape(B, S, D)

def hybrid_layer(x, c, w_ada, b_ada, norm1_gain, w_in, attn_q_gain, attn_k_gain, attn_rel_bias,
                 attn_out_gain, dn_conv_w, dn_a_log, dn_dt_bias, dn_out_gain, w_out, norm2_gain,
                 peer_w_query, peer_query_gain, peer_sub_keys_1, peer_sub_keys_2,
                 peer_expert_down, peer_expert_up):
    B, S, _ = x.shape
    mod = jax.nn.silu(c) @ w_ada + b_ada
    shift1, scale1, gate1, shift2, scale2, gate2 = [m[:, None, :] for m in jnp.split(mod, 6, axis=-1)]

    h = modulate(rms_norm_2(x, norm1_gain), shift1, scale1)
    proj = h @ w_in
    cuts = [ATTN_WIDTH, 2 * ATTN_WIDTH, 3 * ATTN_WIDTH, 3 * ATTN_WIDTH + 3 * DN_WIDTH,
            3 * ATTN_WIDTH + 4 * DN_WIDTH, 3 * ATTN_WIDTH + 4 * DN_WIDTH + DN_HEADS]
    qa, ka, va, qkv_b, z_b, b_raw, a_raw = jnp.split(proj, cuts, axis=-1)

    hd_a = (B, S, ATTN_HEADS, ATTN_HEAD_DIM)
    o_a = chunked_band_attention(qa.reshape(hd_a), ka.reshape(hd_a), va.reshape(hd_a),
                                 attn_q_gain, attn_k_gain, attn_rel_bias)
    o_a = rms_norm_2(o_a, attn_out_gain)

    qkv_b = causal_depthwise_conv_2(qkv_b, dn_conv_w)
    q_b, k_b, v_b = jnp.split(qkv_b, 3, axis=-1)
    hd_b = (B, S, DN_HEADS, DN_HEAD_DIM)
    q_b = l2_norm(q_b.reshape(hd_b))
    k_b = l2_norm(k_b.reshape(hd_b))
    beta = jax.nn.sigmoid(b_raw.astype(jnp.float32))
    g = -jnp.exp(dn_a_log.astype(jnp.float32)) * jax.nn.softplus(
        a_raw.astype(jnp.float32) + dn_dt_bias.astype(jnp.float32))
    o_b = gated_delta_rule(q_b, k_b, v_b.reshape(hd_b), g, beta)
    o_b = rms_norm_2(o_b, dn_out_gain) * jax.nn.silu(z_b.reshape(hd_b).astype(jnp.float32))
    o_b = o_b.reshape(B, S, DN_WIDTH).astype(x.dtype)

    mix = jnp.concatenate([o_a, o_b], axis=-1) @ w_out
    x = x + gate1 * mix

    h2 = modulate(rms_norm_2(x, norm2_gain), shift2, scale2)
    y = peer(h2, peer_w_query, peer_query_gain, peer_sub_keys_1, peer_sub_keys_2,
             peer_expert_down, peer_expert_up)
    return x + gate2 * y

def second_inputs(seed: int = 0) -> dict:
    key = jax.random.key(seed)
    ks = iter(jax.random.split(key, 32))
    L = DEPTH

    def nrm(shape, scale):
        return scale * jax.random.normal(next(ks), shape, jnp.float32)

    def gain(shape):
        return 1.0 + nrm(shape, 0.02)

    x = nrm((BATCH, SEQ, D_MODEL), 1.0)
    c = nrm((BATCH, D_MODEL), 1.0)
    w_ada = nrm((L, D_MODEL, 6 * D_MODEL), 0.5 * D_MODEL ** -0.5)
    b_ada = nrm((L, 6 * D_MODEL), 0.02)
    norm1_gain = gain((L, D_MODEL))
    w_in = nrm((L, D_MODEL, IN_PROJ_WIDTH), D_MODEL ** -0.5)
    attn_q_gain = gain((L, ATTN_HEAD_DIM))
    attn_k_gain = gain((L, ATTN_HEAD_DIM))
    attn_rel_bias = nrm((L, ATTN_HEADS, N_REL), 0.5)
    attn_out_gain = gain((L, ATTN_WIDTH))
    dn_conv_w = nrm((L, CONV_WIDTH, 3 * DN_WIDTH), CONV_WIDTH ** -0.5)
    dn_a_log = jnp.log(jax.random.uniform(next(ks), (L, DN_HEADS), jnp.float32, 1.0, 16.0))
    dt = jnp.exp(jax.random.uniform(next(ks), (L, DN_HEADS), jnp.float32,
                                    math.log(1e-3), math.log(1e-1)))
    dn_dt_bias = dt + jnp.log(-jnp.expm1(-dt))
    dn_out_gain = gain((L, DN_HEAD_DIM))
    w_out = nrm((L, MIX_WIDTH, D_MODEL), MIX_WIDTH ** -0.5)
    norm2_gain = gain((L, D_MODEL))
    peer_w_query = nrm((L, D_MODEL, PEER_HEADS * PEER_KEY_DIM), D_MODEL ** -0.5)
    peer_query_gain = gain((L, PEER_KEY_DIM))
    peer_sub_keys_1 = nrm((L, N_KEYS, PEER_HALF), PEER_HALF ** -0.5)
    peer_sub_keys_2 = nrm((L, N_KEYS, PEER_HALF), PEER_HALF ** -0.5)
    peer_expert_down = nrm((L, N_EXPERTS, D_MODEL), D_MODEL ** -0.5)
    peer_expert_up = nrm((L, N_EXPERTS, D_MODEL), 0.5)
    return {"x": x, "c": c, "w_ada": w_ada, "b_ada": b_ada, "norm1_gain": norm1_gain,
            "w_in": w_in, "attn_q_gain": attn_q_gain, "attn_k_gain": attn_k_gain,
            "attn_rel_bias": attn_rel_bias, "attn_out_gain": attn_out_gain,
            "dn_conv_w": dn_conv_w, "dn_a_log": dn_a_log, "dn_dt_bias": dn_dt_bias,
            "dn_out_gain": dn_out_gain, "w_out": w_out, "norm2_gain": norm2_gain,
            "peer_w_query": peer_w_query, "peer_query_gain": peer_query_gain,
            "peer_sub_keys_1": peer_sub_keys_1, "peer_sub_keys_2": peer_sub_keys_2,
            "peer_expert_down": peer_expert_down, "peer_expert_up": peer_expert_up}

def second_block(x, c, w_ada, b_ada, norm1_gain, w_in, attn_q_gain, attn_k_gain, attn_rel_bias,
              attn_out_gain, dn_conv_w, dn_a_log, dn_dt_bias, dn_out_gain, w_out, norm2_gain,
              peer_w_query, peer_query_gain, peer_sub_keys_1, peer_sub_keys_2,
              peer_expert_down, peer_expert_up):
    for layer in range(DEPTH):
        x = hybrid_layer(x, c, w_ada[layer], b_ada[layer], norm1_gain[layer], w_in[layer],
                         attn_q_gain[layer], attn_k_gain[layer], attn_rel_bias[layer],
                         attn_out_gain[layer], dn_conv_w[layer], dn_a_log[layer], dn_dt_bias[layer],
                         dn_out_gain[layer], w_out[layer], norm2_gain[layer], peer_w_query[layer],
                         peer_query_gain[layer], peer_sub_keys_1[layer], peer_sub_keys_2[layer],
                         peer_expert_down[layer], peer_expert_up[layer])
    return x


def setup_inputs(seed=0):
    out = dict(first_inputs(seed))
    for name, value in second_inputs(seed + 1).items():
        if name != "x":
            out[name + "_2"] = value
    return out


def reference(
    x, c, positions, ada_w, ada_b, norm_g, w_in, q_norm_g, k_norm_g, idx_k_ln_g, idx_k_ln_b,
    conv_w, conv_b, dt_bias, a_log, d_skip, ssm_norm_g, w_branch_att, w_branch_ssm, w_out, c_2,
    w_ada_2, b_ada_2, norm1_gain_2, w_in_2, attn_q_gain_2, attn_k_gain_2, attn_rel_bias_2,
    attn_out_gain_2, dn_conv_w_2, dn_a_log_2, dn_dt_bias_2, dn_out_gain_2, w_out_2,
    norm2_gain_2, peer_w_query_2, peer_query_gain_2, peer_sub_keys_1_2, peer_sub_keys_2_2,
    peer_expert_down_2, peer_expert_up_2,
):
    x = first_block(
        x, c, positions, ada_w, ada_b, norm_g, w_in, q_norm_g, k_norm_g, idx_k_ln_g, idx_k_ln_b,
        conv_w, conv_b, dt_bias, a_log, d_skip, ssm_norm_g, w_branch_att, w_branch_ssm, w_out,
    )
    return second_block(
        x, c_2, w_ada_2, b_ada_2, norm1_gain_2, w_in_2, attn_q_gain_2, attn_k_gain_2,
        attn_rel_bias_2, attn_out_gain_2, dn_conv_w_2, dn_a_log_2, dn_dt_bias_2, dn_out_gain_2,
        w_out_2, norm2_gain_2, peer_w_query_2, peer_query_gain_2, peer_sub_keys_1_2,
        peer_sub_keys_2_2, peer_expert_down_2, peer_expert_up_2,
    )


_drawn_inputs = setup_inputs


def setup_inputs(seed=0):
    import zlib

    import numpy as np

    out = dict(_drawn_inputs(seed))
    spreads = {}
    factors = {'ada_b': 5.642,
     'q_norm_g': 8.0,
     'k_norm_g': 8.0,
     'idx_k_ln_g': 8.0,
     'idx_k_ln_b': 8.0,
     'conv_b': 8.0,
     'd_skip': 4.357,
     'ssm_norm_g': 2.681,
     'norm1_gain_2': 7.149,
     'attn_q_gain_2': 8.0,
     'attn_k_gain_2': 8.0,
     'attn_out_gain_2': 64.0,
     'dn_a_log_2': 3.39,
     'dn_out_gain_2': 22.613,
     'norm2_gain_2': 38.056,
     'peer_query_gain_2': 36.248,
     'attn_rel_bias_2': 4.335}
    for name, (base, spread) in spreads.items():
        noise = np.random.default_rng([zlib.crc32(name.encode()), seed]).standard_normal(out[name].shape)
        drawn = base * np.exp(spread * noise) if base else spread * noise
        out[name] = jnp.asarray(drawn.astype(out[name].dtype))
    for name, factor in factors.items():
        out[name] = (out[name] * factor).astype(out[name].dtype)
    return out
```

```python
from contextlib import ExitStack

import concourse.bass as bass
from concourse import mybir
import numpy as np

F32 = mybir.dt.float32
I32 = mybir.dt.int32
U32 = mybir.dt.uint32
ALU = mybir.AluOpType
ACT = mybir.ActivationFunctionType
AX = mybir.AxisListType.X

P = 128
D = 1024
KD = D // P
T = 512
NT = T // P
EPS = 1e-6
NEG = -1.0e30
SLOTS = 3
TWO_PI = 2.0 * np.pi

Q0, KV0, ZA0, IX0 = 0, 1024, 1536, 2560
ZS0, XBC0, DT0, GA0, GS0 = 2884, 4932, 8004, 8036, 9060
IDX_COLS = 4 * 64 + 64 + 4
AH, AKV, IH = 8, 2, 4
TOPK = 128
SH, SG, SP_ = 32, 4, 64
QA0, KA0, VA0, QKV0, ZB0, BA0 = 0, 512, 1024, 1536, 3072, 3584
BH, BD = 8, 64
DH, CH = 4, 64
RH, RK, NKEY = 8, 16, 128
NSEL = RH * RK

COLS = [("c", 8), ("c_2", 8), ("ada_b", 24), ("norm_g", 8), ("conv_b", 24), ("conv_w", 96),
        ("ssm_norm_g", 16), ("b_ada_2", 48), ("norm1_gain_2", 8), ("dn_conv_w_2", 48),
        ("attn_out_gain_2", 4), ("dn_out_gain_2", 1), ("norm2_gain_2", 8), ("peer_query_gain_2", 2),
        ("dt_bias", 1), ("a_log", 1), ("dn_dt_bias_2", 1), ("dn_a_log_2", 1)]
ROWS = [("q_norm_g", 128), ("k_norm_g", 128), ("idx_k_ln_g", 64), ("idx_k_ln_b", 64), ("d_skip", 32),
        ("attn_q_gain_2", 64), ("attn_k_gain_2", 64), ("gate2_b", 1024), ("rel_far", 8)]
CONSTS = [("ident", 128), ("ones", 128), ("causal_add", 128), ("s_le_l", 128), ("strict64", 128),
          ("upper64", 128), ("inv_freq", 24), ("iota16", 16), ("eps", 1), ("band_add", 128),
          ("lvl1", 128), ("lvl1T", 128), ("lvlT2", 128), ("lvlT4", 128), ("lvlT8", 128),
          ("lvlT16", 128), ("lvlT32", 128), ("flip", 128)]


def offsets(table):
    at, out = 0, {}
    for name, n in table:
        out[name] = (at, n)
        at += n
    return out, at


COL_AT, NCOL = offsets(COLS)
ROW_AT, NROW = offsets(ROWS)
CONST_AT, NCONST = offsets(CONSTS)


class Signal:

    def __init__(self, ctx, nc, name):
        self.sem = ctx.enter_context(nc.semaphore(name))
        self.n = 0


def post(eng, ins, sig):
    ins.then_inc(sig.sem, 1)
    sig.n += 1
    eng.wait_ge(sig.sem, sig.n)


class Kernel:

    def __init__(self, nc, ctx, dram, out):
        self.nc, self.ctx, self.dram, self.out = nc, ctx, dram, out
        sb = self.keep
        self.consts = sb("consts", [P, NCONST])
        self.cols = sb("cols", [P, NCOL])
        self.rows = sb("rows", [P, NROW])
        self.xT = sb("xT", [P, KD, T])
        self.hT = sb("hT", [P, KD, T])
        self.mod1 = sb("mod1", [P, 24])
        self.mod2 = sb("mod2", [P, 48])
        self.gate2 = sb("gate2", [P, D])
        self.ring = [sb(f"ring{i}", [P, KD, 512]) for i in range(SLOTS)]
        self.bank = [ctx.enter_context(nc.psum_tensor(f"bank{i}", [P, 512], F32)) for i in range(8)]
        self.vstep = Signal(ctx, nc, "vector_step")
        self.astep = Signal(ctx, nc, "scalar_step")
        self.gstep = Signal(ctx, nc, "gpsimd_step")
        self.loaded = [ctx.enter_context(nc.semaphore(f"weights_loaded{i}")) for i in range(SLOTS)]
        self.used = Signal(ctx, nc, "weights_used")
        self.output_stored = ctx.enter_context(nc.semaphore("output_stored"))
        self.issued = 0
        self.chunks = self.weight_chunks()

    def keep(self, name, shape, dt=F32):
        return self.ctx.enter_context(self.nc.sbuf_tensor(name, shape, dt))

    def const(self, name, n=None, p=P):
        at, w = CONST_AT[name]
        return self.consts[0:p, at:at + (n or w)]

    def col(self, name, i=0, n=1, p=P):
        at, _ = COL_AT[name]
        return self.cols[0:p, at + i:at + i + n]

    def row(self, name, p=P):
        at, w = ROW_AT[name]
        return self.rows[0:p, at:at + w]

    def weight_chunks(self):
        d = self.dram

        def cut(name, c0, n, k0=0):
            w = d[name][k0:k0 + D, :]
            return [(name, c, k0, w[:, c:min(c + 512, c0 + n)].rearrange("(k p) n -> p k n", p=P), min(512, c0 + n - c))
                    for c in range(c0, c0 + n, 512)]

        out = cut("ada_w", 0, 3072)
        out += cut("w_ada_2", 0, 6144)
        out += cut("w_in", Q0, 1024) + cut("w_in", KV0, 512) + cut("w_in", IX0, IDX_COLS)
        out += cut("w_in", ZA0, 1024)
        out += cut("w_in", GA0, 1024) + cut("w_branch_att", 0, 1024)
        out += cut("w_in", XBC0, 3072) + cut("w_in", DT0, 32) + cut("w_in", ZS0, 2048)
        out += cut("w_in", GS0, 1024)
        for c in (0, 512):
            out += cut("w_branch_ssm", c, 512) + cut("w_branch_ssm", c, 512, D)
        out += cut("w_out", 0, 1024)
        out += cut("w_in_2", QA0, 512) + cut("w_in_2", KA0, 512) + cut("w_in_2", VA0, 512)
        out += cut("w_in_2", QKV0, 1536) + cut("w_in_2", ZB0, 512) + cut("w_in_2", BA0, 8)
        out += cut("w_out_2", 0, 1024) + cut("peer_w_query_2", 0, 2048)
        return out

    def stream(self, sp, last):
        upto = min(len(self.chunks), last + SLOTS)
        for g in range(self.issued, upto):
            if g >= SLOTS:
                sp.wait_ge(self.used.sem, g - SLOTS + 1)
            n = self.chunks[g][4]
            sp.dma_start(self.ring[g % SLOTS][:, :, 0:n], self.chunks[g][3]).then_inc(self.loaded[g % SLOTS], 16)
        self.issued = max(self.issued, upto)

    def take(self, pe, g):
        pe.wait_ge(self.loaded[g % SLOTS], 16 * (g // SLOTS + 1))
        return self.ring[g % SLOTS]


def load_stage(k):
    nc, d = k.nc, k.dram
    with ExitStack() as ctx:
        x = ctx.enter_context(nc.sbuf_tensor("x_rows", [P, NT, D], F32))
        small = ctx.enter_context(nc.semaphore("small_loaded"))
        x_in = ctx.enter_context(nc.semaphore("x_loaded"))
        turned = ctx.enter_context(nc.semaphore("x_turned"))
        block = ctx.enter_context(nc.Block())

        @block.sync
        def _(sp):
            sp.dma_start(k.consts[:], d["consts"]).then_inc(small, 16)
            sp.dma_start(x[:], d["x"].rearrange("(t p) d -> p t d", p=P)).then_inc(x_in, 16)
            k.stream(sp, -1)
            sp.wait_ge(small, 48)

        @block.scalar
        def _(act):
            act.dma_start(k.cols[:], d["cols"]).then_inc(small, 16)
            act.dma_start(k.rows[:], d["rows"].to_broadcast([P, NROW])).then_inc(small, 16)
            for i in range(KD):
                act.wait_ge(turned, i + 1)
                post(act, nc.scalar.activation(k.xT[:, i, :], k.bank[i][:], ACT.Copy), k.astep)

        @block.tensor
        def _(pe):
            pe.wait_ge(small, 48)
            pe.wait_ge(x_in, 16)
            for i in range(KD):
                for t in range(NT):
                    last = nc.tensor.transpose(k.bank[i][:, t * P:(t + 1) * P], x[:, t, i * P:(i + 1) * P],
                                               k.const("ident"))
                last.then_inc(turned, 1)


def modulation_stage(k):
    nc = k.nc
    with ExitStack() as ctx:
        sc = ctx.enter_context(nc.sbuf_tensor("silu_c", [P, 2, 8], F32))
        sc_b = ctx.enter_context(nc.sbuf_tensor("silu_c_wide", [P, 8, P], F32))
        silu = ctx.enter_context(nc.semaphore("silu_c_ready"))
        wide = ctx.enter_context(nc.semaphore("silu_c_wide_ready"))
        done = ctx.enter_context(nc.semaphore("mod_products"))
        block = ctx.enter_context(nc.Block())
        n_g1, n_g2 = 6, 12

        @block.sync
        def _(sp):
            k.stream(sp, n_g1 + n_g2 - 1)

        @block.scalar
        def _(act):
            act.activation(sc[:, 0, :], k.col("c", 0, 8), ACT.Silu).then_inc(silu, 1)
            act.activation(sc[:, 1, :], k.col("c_2", 0, 8), ACT.Silu).then_inc(silu, 1)

        @block.tensor
        def _(pe):
            pe.wait_ge(silu, 2)
            for g in range(n_g1 + n_g2):
                w = k.take(pe, g)
                which, first = (0, 0) if g < n_g1 else (1, n_g1)
                for b in range(4):
                    j = (g - first) * 4 + b
                    for kk in range(KD):
                        last = pe.matmul(k.bank[which][:, j:j + 1], w[:, kk, b * P:(b + 1) * P],
                                         sc[:, which, kk:kk + 1], start=(kk == 0), stop=(kk == KD - 1))
                if g >= n_g1 + n_g2 - 2:
                    if g == n_g1 + n_g2 - 2:
                        pe.wait_ge(wide, 1)
                    half = g - (n_g1 + n_g2 - 2)
                    for kk in range(KD):
                        last = pe.matmul(k.bank[2 + half][:], sc_b[:, kk, :], w[:, kk, :],
                                         start=(kk == 0), stop=(kk == KD - 1))
                last.then_inc(k.used.sem, 1)
                k.used.n += 1

        @block.vector
        def _(dve):
            dve.wait_ge(silu, 2)
            dve.tensor_copy(sc_b[:], sc[:, 1, :].unsqueeze(2).broadcast_to([P, 8, P])).then_inc(wide, 1)
            dve.wait_ge(k.used.sem, n_g1)
            post(dve, dve.tensor_tensor(k.mod1[:], k.bank[0][:, 0:24], k.col("ada_b", 0, 24), ALU.add), k.vstep)
            dve.wait_ge(k.used.sem, n_g1 + n_g2)
            post(dve, dve.tensor_tensor(k.mod2[:], k.bank[1][:, 0:48], k.col("b_ada_2", 0, 48), ALU.add), k.vstep)
            at, _w = ROW_AT["gate2_b"]
            for half in range(2):
                post(dve, dve.tensor_tensor(k.gate2[:, half * 512:(half + 1) * 512], k.bank[2 + half][:],
                                            k.rows[:, at + half * 512:at + (half + 1) * 512], ALU.add), k.vstep)


def norm_stage(k, name, gain, mod, shift, scale):
    nc = k.nc
    with ExitStack() as ctx:
        sq = ctx.enter_context(nc.sbuf_tensor(f"{name}_squares", [P, KD, T], F32))
        rstd = ctx.enter_context(nc.sbuf_tensor(f"{name}_rstd", [P, T], F32))
        gs = ctx.enter_context(nc.sbuf_tensor(f"{name}_gain", [P, KD], F32))
        squared = Signal(ctx, nc, f"{name}_squared")
        summed = ctx.enter_context(nc.semaphore(f"{name}_summed"))
        rooted = Signal(ctx, nc, f"{name}_rooted")
        block = ctx.enter_context(nc.Block())

        @block.vector
        def _(dve):
            for i in range(KD):
                post(dve, dve.tensor_tensor(sq[:, i, :], k.xT[:, i, :], k.xT[:, i, :], ALU.mult), squared)
            post(dve, dve.tensor_scalar(gs[:], mod[:, scale:scale + KD], 1.0, None, ALU.add), k.vstep)
            post(dve, dve.tensor_tensor(gs[:], gs[:], k.col(gain, 0, KD), ALU.mult), k.vstep)
            dve.wait_ge(rooted.sem, 1)
            post(dve, dve.reciprocal(rstd[:], rstd[:]), k.vstep)
            for i in range(KD):
                post(dve, dve.tensor_tensor(k.hT[:, i, :], k.xT[:, i, :], rstd[:], ALU.mult), k.vstep)
                post(dve, dve.tensor_scalar(k.hT[:, i, :], k.hT[:, i, :], gs[:, i:i + 1],
                                            mod[:, shift + i:shift + i + 1], ALU.mult, ALU.add), k.vstep)

        @block.tensor
        def _(pe):
            for i in range(KD):
                pe.wait_ge(squared.sem, i + 1)
                last = pe.matmul(k.bank[0][:], k.const("ones"), sq[:, i, :], start=(i == 0), stop=(i == KD - 1))
            last.then_inc(summed, 1)

        @block.scalar
        def _(act):
            act.wait_ge(summed, 1)
            post(act, act.activation(rstd[:], k.bank[0][:], ACT.Sqrt, bias=k.const("eps"), scale=1.0 / D), rooted)


class Projection:

    def __init__(self, k, ctx, name, plan, banks=range(8)):
        self.k, self.banks, self.plan = k, list(banks), plan
        self.done = ctx.enter_context(k.nc.semaphore(f"{name}_product"))
        self.freed = Signal(ctx, k.nc, f"{name}_freed")
        self.made = self.taken = 0
        self.there = []
        count = 0
        for kind, gs, _, _ in plan:
            outs = NT if kind == "rows" else max(1, k.chunks[gs[-1]][4] // P)
            for i in range(outs):
                if i == outs - 1:
                    self.there.append((k.used.sem, gs[-1] + 1))
                else:
                    count += 1
                    self.there.append((self.done, count))

    def _bank(self, pe):
        n = len(self.banks)
        if self.made >= n:
            pe.wait_ge(self.freed.sem, self.made - n + 1)
        self.made += 1
        return self.k.bank[self.banks[(self.made - 1) % n]]

    def run(self, pe, items=None):
        k = self.k
        for kind, gs, fixed, part in (self.plan if items is None else self.plan[items]):
            outs = NT if kind == "rows" else max(1, k.chunks[gs[-1]][4] // P)
            held = [None] * outs
            for which, g in enumerate(gs):
                w = k.take(pe, g)
                n = k.chunks[g][4]
                wide = min(n, P)
                for i in range(outs):
                    if which == 0:
                        held[i] = self._bank(pe)
                    for kk in range(KD):
                        flags = dict(start=(which == 0 and kk == 0), stop=(which == len(gs) - 1 and kk == KD - 1))
                        if kind == "rows":
                            last = pe.matmul(held[i][:, 0:n], fixed[:, kk, i * P:(i + 1) * P], w[:, kk, 0:n], **flags)
                        else:
                            last = pe.matmul(held[i][0:wide, :], w[:, kk, i * P:i * P + wide],
                                             fixed[:, which * KD + kk, :], **flags)
                    if i == outs - 1:
                        last.then_inc(k.used.sem, 1)
                        k.used.n += 1
                    elif which == len(gs) - 1:
                        last.then_inc(self.done, 1)

    def next(self, eng):
        sem, value = self.there[self.taken]
        eng.wait_ge(sem, value)
        self.taken += 1
        return self.k.bank[self.banks[(self.taken - 1) % len(self.banks)]]


def columns(gs, rhs):
    return [("columns", (g,), rhs, None) for g in gs]


def token_rows(gs, lhs):
    return [("rows", (g,), lhs, None) for g in gs]


def find(k, name, c0, n, k0=0):
    return [g for g, (w, c, kk, _, _) in enumerate(k.chunks) if w == name and c0 <= c < c0 + n and kk == k0]


def attention_projection_stage(k, t):
    nc = k.nc
    with ExitStack() as ctx:
        plan = token_rows(find(k, "w_in", Q0, 1024) + find(k, "w_in", KV0, 512) + find(k, "w_in", IX0, IDX_COLS), k.hT)
        plan += columns(find(k, "w_in", ZA0, 1024), k.hT)
        pj = Projection(k, ctx, "attention_in", plan)
        block = ctx.enter_context(nc.Block())

        @block.sync
        def _(sp):
            k.stream(sp, plan[-1][1][-1])

        @block.tensor
        def _(pe):
            pj.run(pe)

        @block.scalar
        def _(act):
            for c, (dst, c0, n) in enumerate([(t.q, 0, 512), (t.q, 512, 512), (t.kv, 0, 512), (t.ix, 0, IDX_COLS)]):
                for i in range(NT):
                    bank = pj.next(act)
                    post(act, act.activation(dst[:, i, c0:c0 + n], bank[:, 0:n], ACT.Copy), pj.freed)
            for j in range(8):
                bank = pj.next(act)
                post(act, act.activation(t.zT[:, j, :], bank[:], ACT.Silu), pj.freed)


def bc(ap, axis, shape):
    return ap.unsqueeze(axis).broadcast_to(shape)


def rotate(k, dve, x, cos, sin, tmp, half, heads):
    shape = [P, NT, heads, half]
    x1, x2 = x[:, :, :, 0:half], x[:, :, :, half:2 * half]
    c, s = bc(cos, 2, shape), bc(sin, 2, shape)
    a, b, e, f = (tmp[:, i, 0:NT * heads * half].rearrange("p (t h d) -> p t h d", t=NT, h=heads) for i in range(4))
    post(dve, dve.tensor_tensor(a, x1, c, ALU.mult), k.vstep)
    post(dve, dve.tensor_tensor(b, x2, s, ALU.mult), k.vstep)
    post(dve, dve.tensor_tensor(e, x2, c, ALU.mult), k.vstep)
    post(dve, dve.tensor_tensor(f, x1, s, ALU.mult), k.vstep)
    post(dve, dve.tensor_tensor(x1, a, b, ALU.subtract), k.vstep)
    post(dve, dve.tensor_tensor(x2, e, f, ALU.add), k.vstep)


def attention_rotary_stage(k, t):
    nc, d = k.nc, k.dram
    with ExitStack() as ctx:
        def sb(name, shape, dt=F32):
            return ctx.enter_context(nc.sbuf_tensor(name, shape, dt))

        pos = sb("positions", [P, NT], I32)
        posf = sb("positions_f", [P, NT])
        ang = sb("angle", [P, NT, 24])
        turns = sb("turns", [P, NT, 24])
        red = sb("angle_reduced", [P, 2, NT, 24])
        trig = sb("sin_cos", [P, 2, NT, 24])
        sq = k.merged[:].rearrange("p k t -> p (k t)")
        ssum = sb("head_sums", [P, 44])
        rstd = sb("head_rstd", [P, 44])
        mean = sb("idx_mean", [P, NT])
        tmp = sb("rope_products", [P, 4, NT * AH * 16])
        kdup = sb("idx_k_twice", [P, NT, 2, 64])
        pos_in = ctx.enter_context(nc.semaphore("positions_loaded"))
        reduced = Signal(ctx, nc, "angles_reduced")
        trig_ok = Signal(ctx, nc, "trig_ready")
        summed = Signal(ctx, nc, "head_squares_summed")
        rooted = Signal(ctx, nc, "head_roots")
        ready = Signal(ctx, nc, "rows_rotated")
        turned = ctx.enter_context(nc.semaphore("rows_turned"))
        block = ctx.enter_context(nc.Block())
        q4 = t.q[:].rearrange("p t (h d) -> p t h d", h=AH)
        k4 = t.kv[:, :, 0:256].rearrange("p t (h d) -> p t h d", h=AKV)
        v2 = None
        qi4 = t.ix[:, :, 0:256].rearrange("p t (h d) -> p t h d", h=IH)
        ki = t.ix[:, :, 256:320]

        @block.sync
        def _(sp):
            sp.dma_start(pos[:], d["positions"]).then_inc(pos_in, 16)

        @block.vector
        def _(dve):
            def v(ins):
                post(dve, ins, k.vstep)

            dve.wait_ge(pos_in, 16)
            v(dve.tensor_copy(posf[:], pos[:]))
            v(dve.tensor_tensor(ang[:], bc(posf[:], 2, [P, NT, 24]), bc(k.const("inv_freq"), 1, [P, NT, 24]), ALU.mult))
            magic = 12582912.0
            hi, mid, lo = 6.28125, 0.0019340515136718750, 1.2556659146e-06
            hi_mid_lo = (hi, mid, lo)
            for w, quarter in ((0, 0.0), (1, 0.25)):
                v(dve.tensor_scalar(turns[:], ang[:], 1.0 / TWO_PI, quarter, ALU.mult, ALU.add))
                v(dve.tensor_scalar(turns[:], turns[:], magic, None, ALU.add))
                v(dve.tensor_scalar(turns[:], turns[:], magic, None, ALU.subtract))
                src = ang[:]
                for part in hi_mid_lo:
                    v(dve.scalar_tensor_tensor(red[:, w], turns[:], -part, src, ALU.mult, ALU.add))
                    src = red[:, w]
                if quarter:
                    v(dve.tensor_scalar(red[:, w], red[:, w], TWO_PI / 4, None, ALU.add))
                v(dve.tensor_scalar(red[:, w], red[:, w], 3.1415925, None, ALU.min))
                ins = dve.tensor_scalar(red[:, w], red[:, w], -3.1415925, None, ALU.max)
                post(dve, ins, reduced)

            v(dve.tensor_tensor(sq, t.q[:].rearrange("p t n -> p (t n)"), t.q[:].rearrange("p t n -> p (t n)"), ALU.mult))
            v(dve.tensor_reduce(ssum[:, 0:32], sq.rearrange("p (a d) -> p a d", d=P), AX, ALU.add))
            ksq = sq[:, 0:1024].rearrange("p (t h d) -> p t h d", t=NT, h=AKV)
            v(dve.tensor_tensor(ksq, k4, k4, ALU.mult))
            v(dve.tensor_reduce(ssum[:, 32:40], sq[:, 0:1024].rearrange("p (a d) -> p a d", d=P), AX, ALU.add))
            v(dve.tensor_reduce(mean[:], ki, AX, ALU.add))
            v(dve.tensor_scalar(mean[:], mean[:], 1.0 / 64, None, ALU.mult))
            v(dve.tensor_tensor(ki, ki, bc(mean[:], 2, [P, NT, 64]), ALU.subtract))
            kisq = sq[:, 0:256].rearrange("p (t d) -> p t d", t=NT)
            v(dve.tensor_tensor(kisq, ki, ki, ALU.mult))
            v(dve.tensor_reduce(ssum[:, 40:44], kisq, AX, ALU.add))
            post(dve, dve.tensor_scalar(ssum[:, 40:44], ssum[:, 40:44], 2.0, None, ALU.mult), summed)
            dve.wait_ge(rooted.sem, 1)
            v(dve.reciprocal(rstd[:], rstd[:]))
            for x4, at, heads, gain in ((q4, 0, AH, "q_norm_g"), (k4, 32, AKV, "k_norm_g")):
                r = rstd[:, at:at + NT * heads].rearrange("p (t h) -> p t h", t=NT)
                v(dve.tensor_tensor(x4, x4, bc(r, 3, [P, NT, heads, P]), ALU.mult))
                g = k.row(gain).unsqueeze(1).unsqueeze(1).broadcast_to([P, NT, heads, P])
                v(dve.tensor_tensor(x4, x4, g, ALU.mult))
            v(dve.tensor_tensor(ki, ki, bc(rstd[:, 40:44], 2, [P, NT, 64]), ALU.mult))
            v(dve.tensor_tensor(ki, ki, bc(k.row("idx_k_ln_g"), 1, [P, NT, 64]), ALU.mult))
            v(dve.tensor_tensor(ki, ki, bc(k.row("idx_k_ln_b"), 1, [P, NT, 64]), ALU.add))
            v(dve.tensor_scalar(t.ix[:, :, 320:324], t.ix[:, :, 320:324], 0.125 * 0.5, None, ALU.mult))
            dve.wait_ge(trig_ok.sem, 2)
            sa, ca = trig[:, 0, :, 0:16], trig[:, 1, :, 0:16]
            si, ci = trig[:, 0, :, 16:24], trig[:, 1, :, 16:24]
            rotate(k, dve, q4, ca, sa, tmp, 16, AH)
            rotate(k, dve, k4, ca, sa, tmp, 16, AKV)
            rotate(k, dve, qi4, ci, si, tmp, 8, IH)
            rotate(k, dve, ki.unsqueeze(2), ci, si, tmp, 8, 1)
            post(dve, dve.tensor_copy(kdup[:], bc(ki, 2, [P, NT, 2, 64])), ready)

        @block.scalar
        def _(act):
            for w in range(2):
                act.wait_ge(reduced.sem, w + 1)
                post(act, act.activation(trig[:, w], red[:, w], ACT.Sin), trig_ok)
            act.wait_ge(summed.sem, 1)
            post(act, act.activation(rstd[:], ssum[:], ACT.Sqrt, bias=k.const("eps"), scale=1.0 / P), rooted)
            for n, dst in enumerate([t.qT[:, h, :] for h in range(AH)] + [t.kT[:, h, :] for h in range(AKV)]
                                    + [t.qiT[:, h, :] for h in range(2)] + [t.kiT[:]]):
                act.wait_ge(turned, n + 1)
                post(act, act.activation(dst, k.bank[n % 8][:], ACT.Copy), k.astep)
                if n == 0:
                    t.turn_base = k.astep.n - 1

        @block.tensor
        def _(pe):
            srcs = [t.q[:, :, h * P:(h + 1) * P] for h in range(AH)]
            srcs += [t.kv[:, :, h * P:(h + 1) * P] for h in range(AKV)]
            srcs += [t.ix[:, :, h * P:(h + 1) * P] for h in range(2)]
            srcs += [kdup[:].rearrange("p t a d -> p t (a d)")]
            pe.wait_ge(ready.sem, 1)
            for n, src in enumerate(srcs):
                if n >= 8:
                    pe.wait_ge(k.astep.sem, t.turn_base + n - 7)
                for i in range(NT):
                    last = pe.transpose(k.bank[n % 8][:, i * P:(i + 1) * P], src[:, i, :], k.const("ident"))
                last.then_inc(turned, 1)


def selection_stage(k, t):
    nc = k.nc
    with ExitStack() as ctx:
        def sb(name, shape):
            return ctx.enter_context(nc.sbuf_tensor(name, shape, F32))

        relu = sb("relu_logits", [P, IH, T])
        score = sb("index_scores", [P, T])
        work = sb("scores_left", [P, T])
        m8 = sb("best8", [P, 8])
        eq = sb("tied", [P, T])
        seen = sb("ties_so_far", [P, T])
        need = sb("ties_to_keep", [P, 1])
        ones = sb("ones_wide", [P, T])
        logits = ctx.enter_context(nc.semaphore("index_logits"))
        rect = Signal(ctx, nc, "index_relu")
        summed = Signal(ctx, nc, "index_scores_summed")
        block = ctx.enter_context(nc.Block())

        @block.tensor
        def _(pe):
            for i in range(1, NT):
                w = (i + 1) * P
                if i > 1:
                    pe.wait_ge(rect.sem, IH * (i - 1))
                for h in range(IH):
                    p0 = 64 * (h % 2)
                    pe.matmul(k.bank[h][:, 0:w], t.qiT[p0:p0 + 64, h // 2, i * P:(i + 1) * P],
                              t.kiT[p0:p0 + 64, 0:w], start=True, stop=True).then_inc(logits, 1)

        @block.scalar
        def _(act):
            for i in range(1, NT):
                w = (i + 1) * P
                if i > 1:
                    act.wait_ge(summed.sem, i - 1)
                for h in range(IH):
                    act.wait_ge(logits, IH * (i - 1) + h + 1)
                    post(act, act.activation(relu[:, h, 0:w], k.bank[h][:, 0:w], ACT.Relu), rect)

        @block.vector
        def _(dve):
            def v(ins):
                post(dve, ins, k.vstep)

            v(dve.memset(ones[:], 1.0))
            v(dve.memset(t.madd[:], NEG))
            v(dve.tensor_copy(t.madd[:, 0, 0:P], k.const("causal_add")))
            for i in range(1, NT):
                w = (i + 1) * P
                for h in range(IH):
                    dve.wait_ge(rect.sem, IH * (i - 1) + h + 1)
                    wh = t.ix[:, i, 320 + h:321 + h]
                    if h == 0:
                        v(dve.tensor_scalar(score[:, 0:w], relu[:, h, 0:w], wh, None, ALU.mult))
                    else:
                        ins = dve.scalar_tensor_tensor(score[:, 0:w], relu[:, h, 0:w], wh, score[:, 0:w],
                                                       ALU.mult, ALU.add)
                        post(dve, ins, summed if h == IH - 1 else k.vstep)
                v(dve.tensor_tensor(score[:, w - P:w], score[:, w - P:w], k.const("causal_add"), ALU.add))
                for r in range(TOPK // 8):
                    src = score if r == 0 else work
                    v(dve.max(m8[:], src[:, 0:w]))
                    if r < TOPK // 8 - 1:
                        v(dve.match_replace(work[:, 0:w], m8[:], src[:, 0:w], -3.0e38))
                m = t.madd[:, i, 0:w]
                v(dve.tensor_scalar(eq[:, 0:w], score[:, 0:w], m8[:, 7:8], None, ALU.is_equal))
                v(dve.tensor_scalar(m, score[:, 0:w], m8[:, 7:8], None, ALU.is_gt))
                v(dve.tensor_reduce(need[:], m, AX, ALU.add))
                v(dve.tensor_scalar(need[:], need[:], -1.0, float(TOPK), ALU.mult, ALU.add))
                v(dve.tensor_tensor_scan(seen[:, 0:w], ones[:, 0:w], eq[:, 0:w], 0.0, ALU.mult, ALU.add))
                v(dve.scalar_tensor_tensor(eq[:, 0:w], seen[:, 0:w], need[:], eq[:, 0:w], ALU.is_le, ALU.mult))
                v(dve.tensor_tensor(m, m, eq[:, 0:w], ALU.add))
                v(dve.tensor_scalar(m, m, 1.0, -NEG, ALU.subtract, ALU.mult))


def attention_stage(k, t):
    nc = k.nc
    scale = float(P) ** -0.5
    with ExitStack() as ctx:
        def sb(name, shape):
            return ctx.enter_context(nc.sbuf_tensor(name, shape, F32))

        s_at, p_at = [0, P, 3 * P, 6 * P], [0, 4 * P, 7 * P, 9 * P]
        s = sb("scores", [P, 2, 10 * P])
        pT = sb("probsT", [P, 2, 10 * P])
        top = sb("row_top", [P, 2, NT])
        den = sb("row_sum", [P, 2, NT])
        scored = ctx.enter_context(nc.semaphore("scores_made"))
        read = Signal(ctx, nc, "scores_read")
        topped = Signal(ctx, nc, "row_tops")
        exped = Signal(ctx, nc, "exps_made")
        normed = Signal(ctx, nc, "probs_normed")
        flipped = ctx.enter_context(nc.semaphore("probs_flipped"))
        copied = Signal(ctx, nc, "probsT_copied")
        valued = ctx.enter_context(nc.semaphore("values_mixed"))
        gated = Signal(ctx, nc, "outputs_gated")
        block = ctx.enter_context(nc.Block())
        place = [(4, 0), (5, 0), (6, 0), (6, 256)]

        @block.tensor
        def _(pe):
            def scores(h):
                for i in range(NT):
                    if h > 0:
                        pe.wait_ge(read.sem, NT * (h - 1) + i + 1)
                    w = (i + 1) * P
                    pe.matmul(k.bank[i][:, 0:w], t.qT[:, h, i * P:w], t.kT[:, h // 4, 0:w],
                              start=True, stop=True).then_inc(scored, 1)

            scores(0)
            for h in range(AH):
                if h + 1 < AH:
                    scores(h + 1)
                for i in range(NT):
                    pe.wait_ge(normed.sem, NT * h + i + 1)
                    if h > 0 and i == 0:
                        pe.wait_ge(copied.sem, NT * h)
                    for j in range(i + 1):
                        b, c = place[j]
                        c += (i - j) * P
                        last = pe.transpose(k.bank[b][:, c:c + P], s[:, h % 2, s_at[i] + j * P:s_at[i] + (j + 1) * P], k.const("ident"))
                last.then_inc(flipped, 1)
                if h > 0:
                    pe.wait_ge(gated.sem, h)
                for j in range(NT):
                    pe.wait_ge(copied.sem, NT * h + j + 1)
                    v = t.kv[:, j, 256 + (h // 4) * P:256 + (h // 4 + 1) * P]
                    last = pe.matmul(k.bank[7][:, j * P:T], v, pT[:, h % 2, p_at[j]:p_at[j] + T - j * P], start=(j == 0), stop=(j == NT - 1))
                last.then_inc(valued, 1)

        @block.vector
        def _(dve):
            def softmax_in(h):
                for i in range(NT):
                    w = (i + 1) * P
                    dve.wait_ge(scored, NT * h + i + 1)
                    if h >= 2:
                        dve.wait_ge(flipped, h - 1)
                    post(dve, dve.scalar_tensor_tensor(s[:, h % 2, s_at[i]:s_at[i] + w], k.bank[i][:, 0:w], scale,
                                                       t.madd[:, i, 0:w], ALU.mult, ALU.add), read)
                    post(dve, dve.tensor_reduce(top[:, h % 2, i:i + 1], s[:, h % 2, s_at[i]:s_at[i] + w], AX, ALU.max, negate=True), topped)

            def softmax_out(h):
                dve.wait_ge(exped.sem, NT * (h + 1))
                post(dve, dve.reciprocal(den[:, h % 2, :], den[:, h % 2, :]), k.vstep)
                for i in range(NT):
                    w = (i + 1) * P
                    post(dve, dve.tensor_scalar(s[:, h % 2, s_at[i]:s_at[i] + w], s[:, h % 2, s_at[i]:s_at[i] + w], den[:, h % 2, i:i + 1],
                                                None, ALU.mult), normed)

            def gate(h):
                dve.wait_ge(valued, h + 1)
                post(dve, dve.tensor_tensor(t.oT[:, h, :], k.bank[7][:], t.zT[:, h, :], ALU.mult), gated)

            softmax_in(0)
            for h in range(AH):
                if h + 1 < AH:
                    softmax_in(h + 1)
                softmax_out(h)
                if h > 0:
                    gate(h - 1)
            gate(AH - 1)

        @block.scalar
        def _(act):
            def exps(h):
                for i in range(NT):
                    w = (i + 1) * P
                    act.wait_ge(topped.sem, NT * h + i + 1)
                    if h >= 2 and i == 0:
                        act.wait_ge(normed.sem, NT * (h - 1))
                    post(act, act.activation(s[:, h % 2, s_at[i]:s_at[i] + w], s[:, h % 2, s_at[i]:s_at[i] + w], ACT.Exp,
                                             bias=top[:, h % 2, i:i + 1], accum_out=den[:, h % 2, i:i + 1]), exped)

            exps(0)
            for h in range(AH):
                if h + 1 < AH:
                    exps(h + 1)
                act.wait_ge(flipped, h + 1)
                if h >= 2:
                    act.wait_ge(valued, h - 1)
                for j in range(NT):
                    b, c = place[j]
                    post(act, act.activation(pT[:, h % 2, p_at[j]:p_at[j] + T - j * P], k.bank[b][:, c:c + T - j * P], ACT.Copy), copied)


def attention_out_stage(k, t):
    nc = k.nc
    with ExitStack() as ctx:
        plan = columns(find(k, "w_in", GA0, 1024), k.hT) + columns(find(k, "w_branch_att", 0, 1024), t.oT)
        pj = Projection(k, ctx, "attention_out", plan)
        gated = Signal(ctx, nc, "attention_gates")
        block = ctx.enter_context(nc.Block())

        @block.sync
        def _(sp):
            k.stream(sp, plan[-1][1][-1])

        @block.tensor
        def _(pe):
            pj.run(pe)

        @block.scalar
        def _(act):
            for j in range(8):
                bank = pj.next(act)
                post(act, act.activation(t.merged[:, j, :], bank[:], ACT.Sigmoid), pj.freed)

        @block.vector
        def _(dve):
            pj.taken = 8
            dve.wait_ge(pj.freed.sem, 8)
            for j in range(8):
                bank = pj.next(dve)
                post(dve, dve.tensor_tensor(t.merged[:, j, :], bank[:], t.merged[:, j, :], ALU.mult), pj.freed)


class Part:
    pass


def attention_branch(k):
    with ExitStack() as ctx:
        def sb(name, shape):
            return ctx.enter_context(k.nc.sbuf_tensor(name, shape, F32))

        t = Part()
        t.merged = k.merged
        t.zT = sb("silu_zT", [P, 8, T])
        t.kv = sb("k_v_rows", [P, NT, 512])
        t.ix = sb("index_rows", [P, NT, IDX_COLS])
        t.kT, t.qiT, t.kiT = sb("kT", [P, AKV, T]), sb("index_qT", [P, 2, T]), sb("index_kT", [P, T])
        t.qT = sb("qT", [P, AH, T])
        with k.nc.sbuf_tensor("q_rows", [P, NT, D], F32) as t.q:
            attention_projection_stage(k, t)
            attention_rotary_stage(k, t)
        t.madd = sb("selected_add", [P, NT, T])
        selection_stage(k, t)
        t.oT = t.zT
        attention_stage(k, t)
        attention_out_stage(k, t)


def ssm_projection_stage(k, t):
    nc = k.nc
    with ExitStack() as ctx:
        def sb(name, shape):
            return ctx.enter_context(nc.sbuf_tensor(name, shape, F32))

        neg = sb("minus_abs", [SH, T])
        e = sb("exp_minus_abs", [SH, T])
        u = sb("one_plus_exp", [SH, T])
        ln = sb("log_one_plus", [SH, T])
        a_neg = sb("exp_a_log", [SH, 1])
        ones = sb("ones_row", [SH, P])
        dt_plan = columns(find(k, "w_in", DT0, 32), k.hT)
        plan = columns(find(k, "w_in", XBC0, 3072), k.hT) + dt_plan
        pj = Projection(k, ctx, "ssm_in", plan)
        first_tap = Signal(ctx, nc, "conv_first_tap")
        convolved = Signal(ctx, nc, "convolved")
        absed = Signal(ctx, nc, "dt_minus_abs")
        exped = Signal(ctx, nc, "dt_exps")
        summed = Signal(ctx, nc, "dt_one_plus")
        logged = Signal(ctx, nc, "dt_logs")
        block = ctx.enter_context(nc.Block())

        @block.sync
        def _(sp):
            k.stream(sp, plan[-1][1][-1])

        @block.tensor
        def _(pe):
            pj.run(pe)

        @block.scalar
        def _(act):
            post(act, act.activation(a_neg[:], k.col("a_log", 0, 1, SH), ACT.Exp), k.astep)
            a_done = k.astep.n
            t.a_done = a_done
            for j in range(24):
                sem, value = pj.there[j]
                act.wait_ge(sem, value)
                post(act, act.activation(t.xbcT[:, j, :], k.bank[j % 8][:], ACT.Identity,
                                         bias=k.col("conv_b", j), scale=k.col("conv_w", 3 * 24 + j)), first_tap)
                if j > 0:
                    act.wait_ge(convolved.sem, j)
                    post(act, act.activation(t.xbcT[:, j - 1, :], t.xbcT[:, j - 1, :], ACT.Silu), k.astep)
            act.wait_ge(convolved.sem, 24)
            post(act, act.activation(t.xbcT[:, 23, :], t.xbcT[:, 23, :], ACT.Silu), k.astep)
            act.wait_ge(absed.sem, 1)
            post(act, act.activation(e[:], neg[:], ACT.Exp), exped)
            act.wait_ge(summed.sem, 1)
            post(act, act.activation(ln[:], u[:], ACT.Ln), logged)

        @block.vector
        def _(dve):
            def v(ins):
                post(dve, ins, k.vstep)

            v(dve.memset(ones[:], 1.0))
            for j in range(24):
                bank = pj.next(dve)
                dve.wait_ge(first_tap.sem, j + 1)
                for back in (1, 2, 3):
                    ins = dve.scalar_tensor_tensor(t.xbcT[:, j, back:T], bank[:, 0:T - back],
                                                   k.col("conv_w", (3 - back) * 24 + j), t.xbcT[:, j, back:T],
                                                   ALU.mult, ALU.add)
                    post(dve, ins, convolved if back == 3 else k.vstep)
                dve.sem_inc(pj.freed.sem, 1)
                pj.freed.n += 1
            bank = pj.next(dve)
            v(dve.tensor_scalar(t.dtT[:], bank[0:SH, :], k.col("dt_bias", 0, 1, SH), None, ALU.add))
            v(dve.tensor_scalar(neg[:], t.dtT[:], -1.0, None, ALU.mult))
            post(dve, dve.tensor_tensor(neg[:], neg[:], t.dtT[:], ALU.min), absed)
            dve.wait_ge(exped.sem, 1)
            post(dve, dve.tensor_scalar(u[:], e[:], 1.0, None, ALU.add), summed)
            v(dve.scalar_tensor_tensor(e[:], u[:], -1.0, e[:], ALU.add, ALU.subtract))
            v(dve.reciprocal(neg[:], u[:]))
            v(dve.scalar_tensor_tensor(e[:], e[:], -1.0, neg[:], ALU.mult, ALU.mult))
            dve.wait_ge(logged.sem, 1)
            v(dve.tensor_tensor(e[:], e[:], ln[:], ALU.add))
            v(dve.scalar_tensor_tensor(t.dtT[:], t.dtT[:], 0.0, e[:], ALU.max, ALU.add))
            dve.wait_ge(k.astep.sem, t.a_done)
            v(dve.tensor_scalar(e[:], t.dtT[:], a_neg[:], -1.0, ALU.mult, ALU.mult))
            for c in range(NT):
                cs = slice(c * P, (c + 1) * P)
                v(dve.tensor_tensor_scan(t.acumT[:, cs], ones[:], e[:, cs], 0.0, ALU.mult, ALU.add))


def ssd_stage(k, t):
    nc = k.nc
    HG = SH // SG
    with ExitStack() as ctx:
        def sb(name, shape):
            return ctx.enter_context(nc.sbuf_tensor(name, shape, F32))

        z = sb("silu_z_rows", [P, NT, 512])
        dt_row = sb("dt_rows", [P, NT, SH])
        ac_row = sb("acum_rows", [P, NT, SH])
        ea_row = sb("exp_acum_rows", [P, NT, SH])
        xs = sb("xs_rows", [P, 512])
        b_row = sb("b_rows", [P, P])
        xdt = sb("xs_dt", [P, HG, SP_])
        xdec = sb("xs_dt_decay", [P, HG, SP_])
        dec = sb("decay", [P, HG, P])
        cbm = sb("cb_causal", [P, P])
        ds = sb("decay_to_end", [P, HG])
        cd = sb("chunk_decay", [P, HG])
        y = sb("y_rows", [P, 512])
        tmp = sb("y_terms", [P, 512])
        state = sb("state", [P, HG, SP_])
        ss = sb("group_squares", [P, 1])
        plan = token_rows(find(k, "w_in", ZS0, 2048), k.hT)
        pj = Projection(k, ctx, "ssm_z", plan, banks=(0, 1, 2, 3))
        smalls = ctx.enter_context(nc.semaphore("dt_acum_turned"))
        small_in = Signal(ctx, nc, "dt_acum_rows")
        turned = ctx.enter_context(nc.semaphore("unit_turned"))
        bcast = ctx.enter_context(nc.semaphore("acum_spread"))
        rows_in = Signal(ctx, nc, "unit_rows")
        subbed = Signal(ctx, nc, "decay_exponents")
        exped = Signal(ctx, nc, "decays_made")
        weighted = Signal(ctx, nc, "decay_weighted")
        multiplied = ctx.enter_context(nc.semaphore("unit_products"))
        stated = Signal(ctx, nc, "state_updated")
        squared = Signal(ctx, nc, "unit_gated")
        rooted = Signal(ctx, nc, "unit_root")
        normed = Signal(ctx, nc, "unit_normed")
        back = ctx.enter_context(nc.semaphore("unit_turned_back"))
        stored = Signal(ctx, nc, "unit_stored")
        block = ctx.enter_context(nc.Block())
        units = [(g, c) for g in range(SG) for c in range(NT)]

        @block.sync
        def _(sp):
            k.stream(sp, plan[-1][1][-1])

        @block.tensor
        def _(pe):
            for c in range(NT):
                pe.transpose(k.bank[4][:, c * 64:c * 64 + SH], t.dtT[:, c * P:(c + 1) * P], k.const("ident", SH, SH))
                last = pe.transpose(k.bank[4][:, c * 64 + SH:c * 64 + 64], t.acumT[:, c * P:(c + 1) * P],
                                    k.const("ident", SH, SH))
            last.then_inc(smalls, 1)
            pe.wait_ge(small_in.sem, 2)
            for n, (g, c) in enumerate(units):
                cs = slice(c * P, (c + 1) * P)
                if c == 0:
                    if g > 0:
                        pe.wait_ge(stored.sem, n)
                        pe.wait_ge(stated.sem, n)
                    pj.run(pe, slice(g, g + 1))
                    pe.wait_ge(pj.freed.sem, 4 * (g + 1))
                if n > 0:
                    pe.wait_ge(normed.sem, n)
                    pe.wait_ge(stated.sem, n)
                for j in range(4):
                    pe.transpose(k.bank[0][:, j * P:(j + 1) * P], t.xbcT[:, 4 * g + j, cs], k.const("ident"))
                pe.transpose(k.bank[1][:, 0:P], t.xbcT[:, 16 + g, cs], k.const("ident"))
                pe.matmul(k.bank[1][:, P:2 * P], t.xbcT[:, 16 + g, cs], t.xbcT[:, 20 + g, cs],
                          start=True, stop=True).then_inc(turned, 1)
                for h in range(HG):
                    sel = k.const("ident", SH, SH)[:, g * HG + h:g * HG + h + 1].broadcast_to([SH, P])
                    last = pe.matmul(k.bank[4 + h // 4][:, (h % 4) * P:(h % 4 + 1) * P], sel, t.acumT[:, cs],
                                     start=True, stop=True)
                last.then_inc(bcast, 1)
                pe.wait_ge(weighted.sem, n + 1)
                for h in range(HG):
                    pe.matmul(k.bank[2][:, h * SP_:(h + 1) * SP_], dec[:, h, :], xdt[:, h, :], start=True, stop=True)
                pe.matmul(k.bank[3][:], t.xbcT[:, 20 + g, cs], state[:].rearrange("p h d -> p (h d)"),
                          start=True, stop=True)
                pe.matmul(k.bank[6][:], b_row[:], xdec[:].rearrange("p h d -> p (h d)"),
                          start=True, stop=True).then_inc(multiplied, 1)
                pe.wait_ge(normed.sem, n + 1)
                if n > 0:
                    pe.wait_ge(stored.sem, n)
                for j in range(4):
                    last = pe.transpose(k.bank[7][:, j * P:(j + 1) * P], y[:, j * P:(j + 1) * P], k.const("ident"))
                last.then_inc(back, 1)

        @block.scalar
        def _(act):
            def a(ins):
                post(act, ins, k.astep)

            act.wait_ge(smalls, 1)
            v4 = k.bank[4][:, 0:256].rearrange("p (c x) -> p c x", c=NT)
            a(act.activation(dt_row[:], v4[:, :, 0:SH], ACT.Copy))
            post(act, act.activation(ac_row[:], v4[:, :, SH:64], ACT.Copy), small_in)
            post(act, act.activation(ea_row[:], v4[:, :, SH:64], ACT.Exp), small_in)
            for n, (g, c) in enumerate(units):
                if c == 0:
                    for i in range(NT):
                        bank = pj.next(act)
                        if n > 0:
                            act.wait_ge(squared.sem, n)
                        post(act, act.activation(z[:, i, :], bank[:], ACT.Silu), pj.freed)
                act.wait_ge(turned, n + 1)
                if n > 0:
                    act.wait_ge(normed.sem, n)
                a(act.activation(b_row[:], k.bank[1][:, 0:P], ACT.Copy))
                post(act, act.activation(xs[:], k.bank[0][:], ACT.Copy), rows_in)
                act.wait_ge(subbed.sem, n + 1)
                a(act.activation(ds[:], ds[:], ACT.Exp))
                a(act.activation(cd[:], cd[:], ACT.Exp))
                post(act, act.activation(dec[:], dec[:], ACT.Exp), exped)
                act.wait_ge(squared.sem, n + 1)
                a(act.activation(tmp[:], y[:], ACT.Square, accum_out=ss[:]))
                post(act, act.activation(ss[:], ss[:], ACT.Sqrt, bias=k.const("eps"), scale=1.0 / 512), rooted)
                act.wait_ge(back, n + 1)
                for j in range(4):
                    ins = act.activation(t.xbcT[:, 4 * g + j, c * P:(c + 1) * P], k.bank[7][:, j * P:(j + 1) * P],
                                         ACT.Copy, scale=k.col("ssm_norm_g", 4 * g + j))
                    post(act, ins, stored if j == 3 else k.astep)

        @block.vector
        def _(dve):
            def v(ins):
                post(dve, ins, k.vstep)

            dve.wait_ge(small_in.sem, 2)
            for n, (g, c) in enumerate(units):
                hs = slice(g * HG, (g + 1) * HG)
                full, tall = [P, HG, P], [P, HG, SP_]
                dve.wait_ge(bcast, n + 1)
                spread = [k.bank[4 + i][:].rearrange("p (h l) -> p h l", h=4) for i in range(2)]
                for i in range(2):
                    mine = ac_row[:, c, g * HG + 4 * i:g * HG + 4 * i + 4]
                    v(dve.tensor_tensor(dec[:, 4 * i:4 * i + 4, :], spread[i], bc(mine, 2, [P, 4, P]), ALU.subtract))
                    v(dve.tensor_copy(cd[:, 4 * i:4 * i + 4], spread[i][:, :, P - 1]))
                v(dve.tensor_tensor(ds[:], cd[:], ac_row[:, c, hs], ALU.subtract))
                post(dve, dve.tensor_scalar(dec[:], dec[:], 0.0, None, ALU.min), subbed)
                dve.wait_ge(rows_in.sem, n + 1)
                v(dve.tensor_tensor(cbm[:], k.bank[1][:, P:2 * P], k.const("s_le_l"), ALU.mult))
                x3 = xs[:].rearrange("p (h d) -> p h d", h=HG)
                v(dve.tensor_tensor(xdt[:], x3, bc(dt_row[:, c, hs], 2, tall), ALU.mult))
                if c == 0:
                    if n > 0:
                        dve.wait_ge(multiplied, n)
                    v(dve.memset(state[:], 0.0))
                dve.wait_ge(exped.sem, n + 1)
                v(dve.tensor_tensor(xdec[:], xdt[:], bc(ds[:], 2, tall), ALU.mult))
                post(dve, dve.tensor_tensor(dec[:], dec[:], bc(cbm[:], 1, full), ALU.mult), weighted)
                dve.wait_ge(multiplied, n + 1)
                v(dve.tensor_tensor(state[:], state[:], bc(cd[:], 2, tall), ALU.mult))
                s3 = k.bank[6][:].rearrange("p (h d) -> p h d", h=HG)
                post(dve, dve.tensor_tensor(state[:], state[:], s3, ALU.add), stated)
                y3 = y[:].rearrange("p (h d) -> p h d", h=HG)
                t3 = tmp[:].rearrange("p (h d) -> p h d", h=HG)
                off = k.bank[3][:].rearrange("p (h d) -> p h d", h=HG)
                if n > 0:
                    dve.wait_ge(back, n)
                v(dve.tensor_tensor(y3, off, bc(ea_row[:, c, hs], 2, tall), ALU.mult))
                v(dve.tensor_tensor(y[:], y[:], k.bank[2][:], ALU.add))
                v(dve.tensor_tensor(t3, x3, bc(k.row("d_skip")[:, hs], 2, tall), ALU.mult))
                v(dve.tensor_tensor(y[:], y[:], tmp[:], ALU.add))
                post(dve, dve.tensor_tensor(y[:], y[:], z[:, c, :], ALU.mult), squared)
                dve.wait_ge(rooted.sem, n + 1)
                v(dve.reciprocal(ss[:], ss[:]))
                post(dve, dve.tensor_scalar(y[:], y[:], ss[:], None, ALU.mult), normed)


def ssm_out_stage(k, t):
    nc = k.nc
    with ExitStack() as ctx:
        sig = ctx.enter_context(nc.sbuf_tensor("ssm_gate", [P, 8, T], F32))
        term = ctx.enter_context(nc.sbuf_tensor("ssm_term", [P, T], F32))
        plan = columns(find(k, "w_in", GS0, 1024), k.hT)
        for c in (0, 512):
            pair = (find(k, "w_branch_ssm", c, 512)[0], find(k, "w_branch_ssm", c, 512, D)[0])
            plan.append(("columns", pair, t.xbcT, None))
        n_branch = len(plan)
        plan += columns(find(k, "w_out", 0, 1024), k.merged)
        pj = Projection(k, ctx, "ssm_out", plan)
        merged = Signal(ctx, nc, "branches_merged")
        block = ctx.enter_context(nc.Block())

        @block.sync
        def _(sp):
            k.stream(sp, plan[-1][1][-1])

        @block.tensor
        def _(pe):
            pj.run(pe, slice(0, n_branch))
            pe.wait_ge(merged.sem, 8)
            pj.run(pe, slice(n_branch, None))

        @block.scalar
        def _(act):
            for j in range(8):
                bank = pj.next(act)
                post(act, act.activation(sig[:, j, :], bank[:], ACT.Sigmoid), pj.freed)

        @block.vector
        def _(dve):
            dve.wait_ge(pj.freed.sem, 8)
            for j in range(8):
                bank = pj.next(dve)
                post(dve, dve.tensor_tensor(term[:], bank[:], sig[:, j, :], ALU.mult), pj.freed)
                post(dve, dve.tensor_tensor(k.merged[:, j, :], k.merged[:, j, :], term[:], ALU.add), merged)
            for j in range(8):
                bank = pj.next(dve)
                post(dve, dve.scalar_tensor_tensor(k.xT[:, j, :], bank[:], k.mod1[:, 16 + j:17 + j], k.xT[:, j, :],
                                                   ALU.mult, ALU.add), pj.freed)


def ssm_branch(k):
    with ExitStack() as ctx:
        def sb(name, shape):
            return ctx.enter_context(k.nc.sbuf_tensor(name, shape, F32))

        t = Part()
        t.xbcT = sb("xbcT", [P, 24, T])
        t.dtT, t.acumT = sb("dtT", [SH, T]), sb("acumT", [SH, T])
        ssm_projection_stage(k, t)
        ssd_stage(k, t)
        ssm_out_stage(k, t)


def second_projection_stage(k, t):
    nc = k.nc
    with ExitStack() as ctx:
        def sb(name, shape):
            return ctx.enter_context(nc.sbuf_tensor(name, shape, F32))

        xa = sb("a_raw", [DH, T])
        neg = sb("a_minus_abs", [DH, T])
        e = sb("a_exp_minus_abs", [DH, T])
        u = sb("a_one_plus_exp", [DH, T])
        ln = sb("a_log_one_plus", [DH, T])
        a_neg = sb("dn_exp_a_log", [DH, 1])
        ones = sb("dn_ones_row", [DH, CH])
        raw = sb("conv_raw", [P, 2, T])
        ba = find(k, "w_in_2", BA0, 8)[0]
        plan = token_rows(find(k, "w_in_2", QA0, 512) + find(k, "w_in_2", KA0, 512) + find(k, "w_in_2", VA0, 512), k.hT)
        plan += columns(find(k, "w_in_2", QKV0, 1536), k.hT) + token_rows(find(k, "w_in_2", ZB0, 512), k.hT)
        pj = Projection(k, ctx, "second_in", plan)
        tapped = Signal(ctx, nc, "dn_first_tap")
        convolved = Signal(ctx, nc, "dn_convolved")
        gates_made = ctx.enter_context(nc.semaphore("dn_gate_products"))
        absed = Signal(ctx, nc, "a_minus_abs_ready")
        exped = Signal(ctx, nc, "a_exps")
        summed = Signal(ctx, nc, "a_one_plus")
        logged = Signal(ctx, nc, "a_logs")
        sig_ok = Signal(ctx, nc, "beta_ready")
        block = ctx.enter_context(nc.Block())

        @block.sync
        def _(sp):
            k.stream(sp, ba)

        @block.tensor
        def _(pe):
            pj.run(pe)
            w = k.take(pe, ba)
            pe.wait_ge(pj.freed.sem, 28)
            for which in range(2):
                for kk in range(KD):
                    last = pe.matmul(k.bank[which][0:DH, :], w[:, kk, which * DH:(which + 1) * DH], k.hT[:, kk, :],
                                     start=(kk == 0), stop=(kk == KD - 1))
                last.then_inc(gates_made if which == 0 else k.used.sem, 1)
            k.used.n += 1

        @block.scalar
        def _(act):
            for dst in (t.qa, t.ka, t.va):
                for i in range(NT):
                    bank = pj.next(act)
                    post(act, act.activation(dst[:, i, :], bank[:], ACT.Copy), pj.freed)
            for j in range(12):
                bank = pj.next(act)
                if j >= 2:
                    act.wait_ge(convolved.sem, j - 1)
                post(act, act.activation(raw[:, j % 2, :], bank[:], ACT.Copy), pj.freed)
                post(act, act.activation(t.dT[:, j, :], raw[:, j % 2, :], ACT.Copy,
                                         scale=k.col("dn_conv_w_2", 3 * 12 + j)), tapped)
                if j > 0:
                    act.wait_ge(convolved.sem, j)
                    post(act, act.activation(t.dT[:, j - 1, :], t.dT[:, j - 1, :], ACT.Silu), k.astep)
            act.wait_ge(convolved.sem, 12)
            post(act, act.activation(t.dT[:, 11, :], t.dT[:, 11, :], ACT.Silu), k.astep)
            for i in range(NT):
                bank = pj.next(act)
                post(act, act.activation(t.zb[:, i, :], bank[:], ACT.Silu), pj.freed)
            act.wait_ge(gates_made, 1)
            post(act, act.activation(t.betaT[:], k.bank[0][0:DH, :], ACT.Sigmoid), k.astep)
            post(act, act.activation(a_neg[:], k.col("dn_a_log_2", 0, 1, DH), ACT.Exp), sig_ok)
            act.wait_ge(absed.sem, 1)
            post(act, act.activation(e[:], neg[:], ACT.Exp), exped)
            act.wait_ge(summed.sem, 1)
            post(act, act.activation(ln[:], u[:], ACT.Ln), logged)

        @block.vector
        def _(dve):
            def v(ins):
                post(dve, ins, k.vstep)

            v(dve.memset(ones[:], 1.0))
            for j in range(12):
                dve.wait_ge(tapped.sem, j + 1)
                for b in (1, 2, 3):
                    ins = dve.scalar_tensor_tensor(t.dT[:, j, b:T], raw[:, j % 2, 0:T - b],
                                                   k.col("dn_conv_w_2", (3 - b) * 12 + j), t.dT[:, j, b:T],
                                                   ALU.mult, ALU.add)
                    post(dve, ins, convolved if b == 3 else k.vstep)
            dve.wait_ge(k.used.sem, ba + 1)
            v(dve.tensor_scalar(xa[:], k.bank[1][0:DH, :], k.col("dn_dt_bias_2", 0, 1, DH), None, ALU.add))
            v(dve.tensor_scalar(neg[:], xa[:], -1.0, None, ALU.mult))
            post(dve, dve.tensor_tensor(neg[:], neg[:], xa[:], ALU.min), absed)
            dve.wait_ge(exped.sem, 1)
            post(dve, dve.tensor_scalar(u[:], e[:], 1.0, None, ALU.add), summed)
            v(dve.scalar_tensor_tensor(e[:], u[:], -1.0, e[:], ALU.add, ALU.subtract))
            v(dve.reciprocal(neg[:], u[:]))
            v(dve.scalar_tensor_tensor(e[:], e[:], -1.0, neg[:], ALU.mult, ALU.mult))
            dve.wait_ge(logged.sem, 1)
            v(dve.tensor_tensor(e[:], e[:], ln[:], ALU.add))
            v(dve.scalar_tensor_tensor(xa[:], xa[:], 0.0, e[:], ALU.max, ALU.add))
            dve.wait_ge(sig_ok.sem, 1)
            v(dve.tensor_scalar(e[:], xa[:], a_neg[:], -1.0, ALU.mult, ALU.mult))
            for c in range(T // CH):
                cs = slice(c * CH, (c + 1) * CH)
                v(dve.tensor_tensor_scan(t.gcT[:, cs], ones[:], e[:, cs], 0.0, ALU.mult, ALU.add))


def band_setup_stage(k, t):
    nc, d = k.nc, k.dram
    with ExitStack() as ctx:
        def sb(name, shape):
            return ctx.enter_context(nc.sbuf_tensor(name, shape, F32))

        sq = sb("band_squares", [P, NT * 512])
        ssum = sb("band_sums", [P, 2, NT * BH])
        rb = sb("rel_bias_padded", [BH, 384])
        first = ctx.enter_context(nc.semaphore("rel_bias_in"))
        padded = Signal(ctx, nc, "rel_bias_padded_ready")
        stored = ctx.enter_context(nc.semaphore("rel_bias_stored"))
        spread = ctx.enter_context(nc.semaphore("near_bias_in"))
        summed = Signal(ctx, nc, "band_squares_summed")
        rooted = Signal(ctx, nc, "band_roots")
        ready = Signal(ctx, nc, "band_rows_ready")
        turned = ctx.enter_context(nc.semaphore("band_turned"))
        turned_in = Signal(ctx, nc, "band_turned_in")
        flipped = ctx.enter_context(nc.semaphore("near_bias_flipped"))
        flipped_in = Signal(ctx, nc, "near_bias_flipped_in")
        block = ctx.enter_context(nc.Block())
        rel = t.rel_scratch

        @block.sync
        def _(sp):
            sp.dma_start(rb[:, 127:384], d["rel_bias_reversed"]).then_inc(first, 16)
            sp.wait_ge(padded.sem, 1)
            sp.dma_start(rel, rb[:]).then_inc(stored, 16)
            sp.wait_ge(stored, 16)
            near = bass.AP(tensor=rel.tensor, offset=0, ap=[[1, P], [384, BH], [1, 256]])
            sp.dma_start(t.near[:], near).then_inc(spread, 16)

        @block.vector
        def _(dve):
            def v(ins):
                post(dve, ins, k.vstep)

            dve.wait_ge(first, 16)
            post(dve, dve.tensor_copy(rb[:, 0:127], rb[:, 127:128].broadcast_to([BH, 127])), padded)
            for w, x in enumerate((t.qa, t.ka)):
                flat = x[:].rearrange("p t n -> p (t n)")
                v(dve.tensor_tensor(sq[:], flat, flat, ALU.mult))
                ins = dve.tensor_reduce(ssum[:, w, :], sq[:].rearrange("p (a d) -> p a d", d=BD), AX, ALU.add)
                post(dve, ins, summed)
            dve.wait_ge(rooted.sem, 1)
            v(dve.reciprocal(ssum[:], ssum[:]))
            for w, (x, gain) in enumerate(((t.qa, "attn_q_gain_2"), (t.ka, "attn_k_gain_2"))):
                x3 = x[:].rearrange("p t (h d) -> p (t h) d", h=BH)
                v(dve.tensor_tensor(x3, x3, bc(ssum[:, w, :], 2, [P, NT * BH, BD]), ALU.mult))
                post(dve, dve.tensor_tensor(x3, x3, bc(k.row(gain), 1, [P, NT * BH, BD]), ALU.mult), ready)
            dve.wait_ge(flipped_in.sem, 4)
            diag = t.near[:, :, P:2 * P]
            v(dve.tensor_tensor(diag, diag, bc(k.const("band_add"), 1, [P, BH, P]), ALU.add))

        @block.scalar
        def _(act):
            act.wait_ge(summed.sem, 2)
            post(act, act.activation(ssum[:], ssum[:], ACT.Sqrt, bias=k.const("eps"), scale=1.0 / BD), rooted)
            for n, dst in enumerate([t.qaT[:, j, :] for j in range(4)] + [t.kaT[:, j, :] for j in range(4)]):
                act.wait_ge(turned, n + 1)
                post(act, act.activation(dst, k.bank[n][:], ACT.Copy), turned_in)
            act.wait_ge(flipped, 1)
            for j in range(4):
                post(act, act.activation(t.near[:, 2 * j:2 * j + 2, :], k.bank[j][:].rearrange("p (h s) -> p h s", h=2),
                                         ACT.Copy), flipped_in)

        @block.tensor
        def _(pe):
            for w, src in enumerate((t.qa, t.ka)):
                pe.wait_ge(ready.sem, w + 1)
                for j in range(4):
                    for i in range(NT):
                        last = pe.transpose(k.bank[4 * w + j][:, i * P:(i + 1) * P], src[:, i, j * P:(j + 1) * P],
                                            k.const("ident"))
                    last.then_inc(turned, 1)
            pe.wait_ge(turned_in.sem, 4)
            pe.wait_ge(spread, 16)
            for j in range(4):
                last = pe.matmul(k.bank[j][:], k.const("flip"), t.near[:, 2 * j:2 * j + 2, :].rearrange("p h s -> p (h s)"),
                                 start=True, stop=True)
            last.then_inc(flipped, 1)


def band_attention_stage(k, t):
    nc = k.nc
    scale = float(BD) ** -0.5
    with ExitStack() as ctx:
        def sb(name, shape):
            return ctx.enter_context(nc.sbuf_tensor(name, shape, F32))

        s_at, p_at = [0, P, 3 * P, 6 * P], [0, 4 * P, 7 * P, 9 * P]
        s = sb("band_scores", [P, 2, 10 * P])
        pT = sb("band_probsT", [P, 2, 10 * P])
        top = sb("band_top", [P, 2, NT])
        den = sb("band_sum", [P, 2, NT])
        scored = ctx.enter_context(nc.semaphore("band_scores_made"))
        read = Signal(ctx, nc, "band_scores_read")
        topped = Signal(ctx, nc, "band_tops")
        exped = Signal(ctx, nc, "band_exps")
        flipped = ctx.enter_context(nc.semaphore("band_probs_flipped"))
        copied = Signal(ctx, nc, "band_probsT_copied")
        valued = ctx.enter_context(nc.semaphore("band_values_mixed"))
        normed = Signal(ctx, nc, "band_outputs_normed")
        block = ctx.enter_context(nc.Block())
        place = [(4, 0), (5, 0), (6, 0), (6, 256)]

        @block.tensor
        def _(pe):
            def scores(h):
                p0 = BD * (h % 2)
                for i in range(NT):
                    if h > 0:
                        pe.wait_ge(read.sem, NT * (h - 1) + i + 1)
                    w = (i + 1) * P
                    pe.matmul(k.bank[i][:, 0:w], t.qaT[p0:p0 + BD, h // 2, i * P:w], t.kaT[p0:p0 + BD, h // 2, 0:w],
                              start=True, stop=True).then_inc(scored, 1)

            scores(0)
            for h in range(BH):
                if h + 1 < BH:
                    scores(h + 1)
                for i in range(NT):
                    pe.wait_ge(exped.sem, NT * h + i + 1)
                    if h > 0 and i == 0:
                        pe.wait_ge(copied.sem, NT * h)
                    for j in range(i + 1):
                        b, c = place[j]
                        c += (i - j) * P
                        last = pe.transpose(k.bank[b][:, c:c + P], s[:, h % 2, s_at[i] + j * P:s_at[i] + (j + 1) * P],
                                            k.const("ident"))
                last.then_inc(flipped, 1)
                if h > 0:
                    pe.wait_ge(normed.sem, h)
                pe.wait_ge(copied.sem, NT * (h + 1))
                for i in range(NT):
                    for j in range(i + 1):
                        last = pe.matmul(k.bank[7][:, i * BD:(i + 1) * BD],
                                         pT[:, h % 2, p_at[j] + (i - j) * P:p_at[j] + (i - j + 1) * P],
                                         t.va[:, j, h * BD:(h + 1) * BD], start=(j == 0), stop=(j == i))
                last.then_inc(valued, 1)

        @block.vector
        def _(dve):
            def softmax_in(h):
                for i in range(NT):
                    w = (i + 1) * P
                    dve.wait_ge(scored, NT * h + i + 1)
                    if h >= 2:
                        dve.wait_ge(flipped, h - 1)
                    at = s_at[i]
                    if i >= 2:
                        post(dve, dve.tensor_scalar(s[:, h % 2, at:at + w - 2 * P], k.bank[i][:, 0:w - 2 * P], scale,
                                                    k.row("rel_far")[:, h:h + 1], ALU.mult, ALU.add), k.vstep)
                    nw = min(w, 2 * P)
                    post(dve, dve.scalar_tensor_tensor(s[:, h % 2, at + w - nw:at + w], k.bank[i][:, w - nw:w], scale,
                                                       t.near[:, h, 2 * P - nw:2 * P], ALU.mult, ALU.add), read)
                    post(dve, dve.tensor_reduce(top[:, h % 2, i:i + 1], s[:, h % 2, at:at + w], AX, ALU.max,
                                                negate=True), topped)

            def out(h):
                dve.wait_ge(valued, h + 1)
                post(dve, dve.reciprocal(den[:, h % 2, :], den[:, h % 2, :]), k.vstep)
                o3 = k.bank[7][:, 0:NT * BD].rearrange("p (t d) -> p t d", t=NT)
                post(dve, dve.tensor_tensor(t.oa[:, :, h * BD:(h + 1) * BD], o3, bc(den[:, h % 2, :], 2, [P, NT, BD]),
                                            ALU.mult), normed)

            softmax_in(0)
            for h in range(BH):
                if h + 1 < BH:
                    softmax_in(h + 1)
                out(h)

        @block.scalar
        def _(act):
            def exps(h):
                for i in range(NT):
                    w = (i + 1) * P
                    act.wait_ge(topped.sem, NT * h + i + 1)
                    if h >= 2 and i == 0:
                        act.wait_ge(normed.sem, h - 1)
                    post(act, act.activation(s[:, h % 2, s_at[i]:s_at[i] + w], s[:, h % 2, s_at[i]:s_at[i] + w], ACT.Exp,
                                             bias=top[:, h % 2, i:i + 1], accum_out=den[:, h % 2, i:i + 1]), exped)

            exps(0)
            for h in range(BH):
                if h + 1 < BH:
                    exps(h + 1)
                act.wait_ge(flipped, h + 1)
                if h >= 2:
                    act.wait_ge(valued, h - 1)
                for j in range(NT):
                    b, c = place[j]
                    post(act, act.activation(pT[:, h % 2, p_at[j]:p_at[j] + T - j * P], k.bank[b][:, c:c + T - j * P],
                                             ACT.Copy), copied)


def delta_setup_stage(k, t):
    nc = k.nc
    with ExitStack() as ctx:
        def sb(name, shape):
            return ctx.enter_context(nc.sbuf_tensor(name, shape, F32))

        sq = sb("dn_squares", [P, 2, T])
        rstd = sb("dn_rstd", [P, 2, T])
        last_row = sb("dn_chunk_end_rows", [P, NT, DH])
        squared = Signal(ctx, nc, "dn_squared")
        summed = ctx.enter_context(nc.semaphore("dn_squares_summed"))
        rooted = Signal(ctx, nc, "dn_roots")
        scaled = Signal(ctx, nc, "dn_columns_scaled")
        spread = ctx.enter_context(nc.semaphore("dn_sums_spread"))
        spread_in = Signal(ctx, nc, "dn_sums_in")
        turned = ctx.enter_context(nc.semaphore("dn_turned"))
        rows_in = Signal(ctx, nc, "dn_rows_in")
        expo = Signal(ctx, nc, "dn_row_exponents")
        expd = Signal(ctx, nc, "dn_row_exps")
        block = ctx.enter_context(nc.Block())

        @block.tensor
        def _(pe):
            for h in range(DH):
                sel = k.const("ident", DH, DH)[:, h:h + 1].broadcast_to([DH, P])
                pe.matmul(k.bank[h][:], sel, t.gcT[:], start=True, stop=True).then_inc(spread, 1)
            for i in range(NT):
                pe.transpose(k.bank[4][:, 8 * i:8 * i + 4], t.gcT[:, i * P:(i + 1) * P], k.const("ident", DH, DH))
                last = pe.transpose(k.bank[4][:, 8 * i + 4:8 * i + 8], t.betaT[:, i * P:(i + 1) * P],
                                    k.const("ident", DH, DH))
            last.then_inc(spread, 1)
            for j in range(8):
                pe.wait_ge(squared.sem, j + 1)
                if j >= 2:
                    pe.wait_ge(rooted.sem, j - 1)
                pe.matmul(k.bank[5 + j % 2][:], k.const("ones"), sq[:, j % 2, :], start=True, stop=True).then_inc(summed, 1)
            pe.wait_ge(scaled.sem, 8)
            pe.wait_ge(spread_in.sem, 6)
            for n in range(8):
                i, first = n % 4, 8 if n < 4 else 4
                for h in range(DH):
                    last = pe.transpose(k.bank[[0, 1, 2, 3, 7, 4, 5, 6][n]][:, h * P:(h + 1) * P],
                                        t.dT[:, first + h, i * P:(i + 1) * P], k.const("ident"))
                last.then_inc(turned, 1)

        @block.scalar
        def _(act):
            for h in range(DH):
                act.wait_ge(spread, h + 1)
                post(act, act.activation(t.gcB[:, h, :], k.bank[h][:], ACT.Copy), spread_in)
            act.wait_ge(spread, 5)
            v4 = k.bank[4][:, 0:32].rearrange("p (t x) -> p t x", t=NT)
            post(act, act.activation(t.gc_row[:], v4[:, :, 0:4], ACT.Copy), spread_in)
            post(act, act.activation(t.beta_row[:], v4[:, :, 4:8], ACT.Copy), spread_in)
            for j in range(8):
                act.wait_ge(summed, j + 1)
                if j >= 2:
                    act.wait_ge(scaled.sem, j - 1)
                post(act, act.activation(rstd[:, j % 2, :], k.bank[5 + j % 2][:], ACT.Sqrt, bias=k.const("eps")), rooted)
            for n in range(8):
                act.wait_ge(turned, n + 1)
                dst = t.v_row if n < 4 else t.k_row
                post(act, act.activation(dst[:, n % 4, :], k.bank[[0, 1, 2, 3, 7, 4, 5, 6][n]][:], ACT.Copy), rows_in)
            act.wait_ge(expo.sem, 1)
            post(act, act.activation(t.egl[:], t.egl[:], ACT.Exp), k.astep)
            post(act, act.activation(last_row[:], last_row[:], ACT.Exp), k.astep)
            post(act, act.activation(t.eg_row[:], t.gc_row[:], ACT.Exp), expd)
            post(act, act.activation(t.qgT[:], t.gcB[:], ACT.Exp), expd)

        @block.vector
        def _(dve):
            def v(ins):
                post(dve, ins, k.vstep)

            for j in range(8):
                if j == 0:
                    for jj in range(2):
                        post(dve, dve.tensor_tensor(sq[:, jj, :], t.dT[:, jj, :], t.dT[:, jj, :], ALU.mult), squared)
                dve.wait_ge(rooted.sem, j + 1)
                v(dve.reciprocal(rstd[:, j % 2, :], rstd[:, j % 2, :]))
                if j < DH:
                    post(dve, dve.scalar_tensor_tensor(t.dT[:, j, :], t.dT[:, j, :], float(P) ** -0.5, rstd[:, j % 2, :],
                                                       ALU.mult, ALU.mult), scaled)
                else:
                    post(dve, dve.tensor_tensor(t.dT[:, j, :], t.dT[:, j, :], rstd[:, j % 2, :], ALU.mult), scaled)
                if j + 2 < 8:
                    post(dve, dve.tensor_tensor(sq[:, j % 2, :], t.dT[:, j + 2, :], t.dT[:, j + 2, :], ALU.mult), squared)
            dve.wait_ge(spread_in.sem, 6)
            ends = t.gcB[:].rearrange("p h (n c) -> p h n c", c=CH)[:, :, :, CH - 1]
            v(dve.tensor_copy(t.egl[:], ends))
            for half in range(2):
                ps = slice(CH * half, CH * (half + 1))
                mine = ends.rearrange("p h (t two) -> p t h two", two=2)[ps, :, :, half]
                ins = dve.tensor_tensor(last_row[ps], mine, t.gc_row[ps], ALU.subtract)
                post(dve, ins, expo if half else k.vstep)
            dve.wait_ge(rows_in.sem, 8)
            dve.wait_ge(expd.sem, 2)
            shape = [P, NT, DH, P]

            def heads(x):
                return x[:].rearrange("p t (h d) -> p t h d", h=DH)

            v(dve.tensor_tensor(heads(t.v_row), heads(t.v_row), bc(t.beta_row[:], 3, shape), ALU.mult))
            v(dve.tensor_tensor(heads(t.kdec), heads(t.k_row), bc(last_row[:], 3, shape), ALU.mult))
            v(dve.tensor_tensor(heads(t.k_row), heads(t.k_row), bc(t.beta_row[:], 3, shape), ALU.mult))
            v(dve.tensor_tensor(heads(t.k_row), heads(t.k_row), bc(t.eg_row[:], 3, shape), ALU.mult))
            v(dve.tensor_tensor(t.qgT[:], t.qgT[:], t.dT[:, 0:DH, :], ALU.mult))


def delta_solve_stage(k, t):
    nc = k.nc
    levels = ["lvlT2", "lvlT4", "lvlT8", "lvlT16", "lvlT32"]
    with ExitStack() as ctx:
        def sb(name, shape):
            return ctx.enter_context(nc.sbuf_tensor(name, shape, F32))

        full = [P, DH, P]
        dec = sb("dn_decay", full)
        low = sb("dn_lower", full)
        lowT = sb("dn_lowerT", full)
        x = sb("dn_inverse", full)
        xT = sb("dn_inverseT", full)
        part = sb("dn_level", full)
        yy = sb("dn_level_x", full)
        products = ctx.enter_context(nc.semaphore("dn_products"))
        diff = Signal(ctx, nc, "dn_decay_exponents")
        exped = Signal(ctx, nc, "dn_decays")
        lowered = Signal(ctx, nc, "dn_lower_ready")
        flipped = ctx.enter_context(nc.semaphore("dn_lower_flipped"))
        begun = Signal(ctx, nc, "dn_level_ready")
        first = ctx.enter_context(nc.semaphore("dn_level_first"))
        first_in = Signal(ctx, nc, "dn_level_first_in")
        second = ctx.enter_context(nc.semaphore("dn_level_second"))
        inverted = Signal(ctx, nc, "dn_inverted")
        solved = ctx.enter_context(nc.semaphore("dn_solved"))
        solved_in = Signal(ctx, nc, "dn_solved_in")
        block = ctx.enter_context(nc.Block())

        def b3(i):
            return k.bank[i][:].rearrange("p (h l) -> p h l", h=DH)

        @block.tensor
        def _(pe):
            n_lvl = len(levels)
            for i in range(NT):
                ts = slice(i * P, (i + 1) * P)
                if i > 0:
                    pe.wait_ge(solved_in.sem, 2 * i)
                for h in range(DH):
                    pe.matmul(b3(0)[:, h], t.dT[:, DH + h, ts], t.dT[:, DH + h, ts], start=True, stop=True)
                for h in range(DH):
                    last = pe.matmul(b3(1)[:, h], t.dT[:, DH + h, ts], t.dT[:, h, ts], start=True, stop=True)
                last.then_inc(products, 1)
                pe.wait_ge(lowered.sem, i + 1)
                for h in range(DH):
                    last = pe.transpose(b3(2)[:, h], low[:, h], k.const("ident"))
                last.then_inc(flipped, 1)
                for m in range(n_lvl):
                    pe.wait_ge(begun.sem, n_lvl * i + m + 1)
                    for h in range(DH):
                        last = pe.matmul(b3(3)[:, h], part[:, h], x[:, h], start=True, stop=True)
                    last.then_inc(first, 1)
                    pe.wait_ge(first_in.sem, n_lvl * i + m + 1)
                    for h in range(DH):
                        pe.matmul(b3(4)[:, h], xT[:, h], yy[:, h], start=True, stop=True)
                    for h in range(DH):
                        last = pe.matmul(b3(5)[:, h], yy[:, h], xT[:, h], start=True, stop=True)
                    last.then_inc(second, 1)
                pe.wait_ge(inverted.sem, i + 1)
                for h in range(DH):
                    hs = slice(h * P, (h + 1) * P)
                    pe.matmul(b3(6)[:, h], xT[:, h], t.v_row[:, i, hs], start=True, stop=True)
                for h in range(DH):
                    hs = slice(h * P, (h + 1) * P)
                    last = pe.matmul(b3(7)[:, h], t.k_row[:, i, hs], xT[:, h], start=True, stop=True)
                last.then_inc(solved, 1)

        @block.scalar
        def _(act):
            n_lvl = len(levels)
            for i in range(NT):
                for w in range(2):
                    act.wait_ge(diff.sem, 2 * i + w + 1)
                    post(act, act.activation(dec[:], dec[:], ACT.Exp), exped)
                for m in range(n_lvl):
                    act.wait_ge(first, n_lvl * i + m + 1)
                    post(act, act.activation(yy[:], b3(3), ACT.Copy), first_in)
                act.wait_ge(solved, i + 1)
                post(act, act.activation(t.u[:, i, :], k.bank[6][:], ACT.Copy), solved_in)
                post(act, act.activation(t.wT[:, :, i * P:(i + 1) * P], b3(7), ACT.Copy), solved_in)

        @block.vector
        def _(dve):
            def v(ins):
                post(dve, ins, k.vstep)

            n_lvl = len(levels)
            for i in range(NT):
                along = t.gcB[:, :, i * P:(i + 1) * P]
                mine = bc(t.gc_row[:, i, :], 2, full)
                v(dve.tensor_tensor(dec[:], mine, along, ALU.subtract))
                post(dve, dve.tensor_scalar(dec[:], dec[:], 0.0, None, ALU.min), diff)
                dve.wait_ge(exped.sem, 2 * i + 1)
                dve.wait_ge(products, i + 1)
                v(dve.tensor_tensor(low[:], b3(0), dec[:], ALU.mult))
                v(dve.tensor_tensor(low[:], low[:], bc(t.beta_row[:, i, :], 2, full), ALU.mult))
                post(dve, dve.tensor_tensor(low[:], low[:], bc(k.const("strict64"), 1, full), ALU.mult), lowered)
                v(dve.tensor_tensor(dec[:], along, mine, ALU.subtract))
                post(dve, dve.tensor_scalar(dec[:], dec[:], 0.0, None, ALU.min), diff)
                dve.wait_ge(exped.sem, 2 * i + 2)
                v(dve.tensor_tensor(t.at[:, i], b3(1), dec[:], ALU.mult))
                v(dve.tensor_tensor(t.at[:, i], t.at[:, i], bc(k.const("upper64"), 1, full), ALU.mult))
                dve.wait_ge(flipped, i + 1)
                v(dve.tensor_copy(lowT[:], b3(2)))
                for dst, src, mask in ((x, low, "lvl1"), (xT, lowT, "lvl1T")):
                    v(dve.scalar_tensor_tensor(dst[:], src[:], -1.0, bc(k.const(mask), 1, full), ALU.mult, ALU.mult))
                    v(dve.tensor_tensor(dst[:], dst[:], bc(k.const("ident"), 1, full), ALU.add))
                for m, mask in enumerate(levels):
                    post(dve, dve.tensor_tensor(part[:], lowT[:], bc(k.const(mask), 1, full), ALU.mult), begun)
                    dve.wait_ge(second, n_lvl * i + m + 1)
                    v(dve.tensor_tensor(x[:], x[:], b3(4), ALU.subtract))
                    post(dve, dve.tensor_tensor(xT[:], xT[:], b3(5), ALU.subtract),
                         inverted if m == n_lvl - 1 else k.vstep)


def delta_scan_stage(k, t):
    nc = k.nc
    with ExitStack() as ctx:
        state = ctx.enter_context(nc.sbuf_tensor("dn_state", [P, DH, P], F32))
        vnew = ctx.enter_context(nc.sbuf_tensor("dn_v_new", [P, DH, P], F32))
        kept = Signal(ctx, nc, "dn_state_ready")
        removed = ctx.enter_context(nc.semaphore("dn_state_read"))
        v_ok = Signal(ctx, nc, "dn_v_new_ready")
        added = ctx.enter_context(nc.semaphore("dn_chunk_products"))
        stored = Signal(ctx, nc, "dn_chunk_stored")
        block = ctx.enter_context(nc.Block())

        def b3(i):
            return k.bank[i][:].rearrange("p (h l) -> p h l", h=DH)

        @block.tensor
        def _(pe):
            for n in range(T // CH):
                i, ps = n // 2, slice(CH * (n % 2), CH * (n % 2 + 1))
                cs = slice(n * CH, (n + 1) * CH)
                pe.wait_ge(kept.sem, n + 1)
                for h in range(DH):
                    last = pe.matmul(b3(0)[ps, h], t.wT[:, h, cs], state[:, h], start=True, stop=True)
                last.then_inc(removed, 1)
                if n > 0:
                    pe.wait_ge(stored.sem, n)
                pe.wait_ge(v_ok.sem, n + 1)
                for h in range(DH):
                    pe.matmul(b3(1)[ps, h], t.qgT[:, h, cs], state[:, h], start=True, stop=False)
                    pe.matmul(b3(1)[ps, h], t.at[ps, i, h, ps], vnew[ps, h], start=False, stop=True)
                for h in range(DH):
                    last = pe.matmul(b3(2)[:, h], t.kdec[ps, i, h * P:(h + 1) * P], vnew[ps, h], start=True, stop=True)
                last.then_inc(added, 1)

        @block.vector
        def _(dve):
            post(dve, dve.memset(state[:], 0.0), kept)
            for n in range(T // CH):
                i, ps = n // 2, slice(CH * (n % 2), CH * (n % 2 + 1))
                dve.wait_ge(removed, n + 1)
                u3 = t.u[ps, i, :].rearrange("p (h d) -> p h d", h=DH)
                post(dve, dve.tensor_tensor(vnew[ps], u3, b3(0)[ps], ALU.subtract), v_ok)
                dve.wait_ge(added, n + 1)
                post(dve, dve.tensor_tensor(state[:], state[:], bc(t.egl[:, :, n], 2, [P, DH, P]), ALU.mult), k.vstep)
                post(dve, dve.tensor_tensor(state[:], state[:], b3(2), ALU.add), kept)

        @block.scalar
        def _(act):
            for n in range(T // CH):
                i, ps = n // 2, slice(CH * (n % 2), CH * (n % 2 + 1))
                act.wait_ge(added, n + 1)
                post(act, act.activation(t.ob[ps, i, :], k.bank[1][ps, :], ACT.Copy), stored)


def second_out_stage(k, t):
    nc = k.nc
    with ExitStack() as ctx:
        def sb(name, shape):
            return ctx.enter_context(nc.sbuf_tensor(name, shape, F32))

        sq = sb("mix_squares", [P, NT, 512])
        ss = sb("mix_sums", [P, NT + NT * DH])
        mixT = k.hT
        plan = columns(find(k, "w_out_2", 0, 1024), mixT)
        pj = Projection(k, ctx, "second_out", plan)
        summed = Signal(ctx, nc, "mix_squares_summed")
        rooted = Signal(ctx, nc, "mix_roots")
        ready = Signal(ctx, nc, "mix_rows_ready")
        turned = ctx.enter_context(nc.semaphore("mix_turned"))
        copied = Signal(ctx, nc, "mix_columns")
        block = ctx.enter_context(nc.Block())

        @block.sync
        def _(sp):
            k.stream(sp, plan[-1][1][-1])

        @block.vector
        def _(dve):
            def v(ins):
                post(dve, ins, k.vstep)

            ob4 = t.ob[:].rearrange("p t (h d) -> p t h d", h=DH)
            v(dve.tensor_tensor(sq[:], t.oa[:], t.oa[:], ALU.mult))
            v(dve.tensor_reduce(ss[:, 0:NT], sq[:], AX, ALU.add))
            v(dve.tensor_tensor(sq[:], t.ob[:], t.ob[:], ALU.mult))
            v(dve.tensor_reduce(ss[:, NT:], sq[:].rearrange("p t (h d) -> p (t h) d", h=DH), AX, ALU.add))
            post(dve, dve.tensor_scalar(ss[:, 0:NT], ss[:, 0:NT], 0.25, None, ALU.mult), summed)
            dve.wait_ge(rooted.sem, 1)
            v(dve.reciprocal(ss[:], ss[:]))
            v(dve.tensor_tensor(t.oa[:], t.oa[:], bc(ss[:, 0:NT], 2, [P, NT, 512]), ALU.mult))
            r = ss[:, NT:].rearrange("p (t h) -> p t h", t=NT)
            v(dve.tensor_tensor(ob4, ob4, bc(r, 3, [P, NT, DH, P]), ALU.mult))
            post(dve, dve.tensor_tensor(t.ob[:], t.ob[:], t.zb[:], ALU.mult), ready)
            for j in range(8):
                bank = pj.next(dve)
                post(dve, dve.scalar_tensor_tensor(k.xT[:, j, :], bank[:], k.mod2[:, 16 + j:17 + j], k.xT[:, j, :],
                                                   ALU.mult, ALU.add), pj.freed)

        @block.scalar
        def _(act):
            act.wait_ge(summed.sem, 1)
            post(act, act.activation(ss[:], ss[:], ACT.Sqrt, bias=k.const("eps"), scale=1.0 / P), rooted)
            for j in range(8):
                gain = k.col("attn_out_gain_2", j) if j < 4 else k.col("dn_out_gain_2")
                act.wait_ge(turned, j + 1)
                post(act, act.activation(mixT[:, j, :], k.bank[j][:], ACT.Copy, scale=gain), copied)

        @block.tensor
        def _(pe):
            pe.wait_ge(ready.sem, 1)
            for j in range(8):
                src = t.oa if j < 4 else t.ob
                for i in range(NT):
                    last = pe.transpose(k.bank[j][:, i * P:(i + 1) * P], src[:, i, (j % 4) * P:(j % 4 + 1) * P],
                                        k.const("ident"))
                last.then_inc(turned, 1)
            pe.wait_ge(copied.sem, 8)
            pj.run(pe)


def second_mixer(k):
    nc = k.nc
    with ExitStack() as ctx:
        def sb(name, shape):
            return ctx.enter_context(nc.sbuf_tensor(name, shape, F32))

        t = Part()
        t.rel_scratch = nc.dram_tensor("rel_bias_scratch", (BH, 384), F32, kind="Internal").ap()
        t.zb = sb("silu_z_b", [P, NT, 512])
        t.betaT, t.gcT = sb("betaT", [DH, T]), sb("gcT", [DH, T])
        t.oa = sb("band_out", [P, NT, 512])
        t.dT = sb("delta_qkvT", [P, 12, T])
        with ExitStack() as bctx:
            def bsb(name, shape):
                return bctx.enter_context(nc.sbuf_tensor(name, shape, F32))

            t.qa, t.ka, t.va = (bsb(n, [P, NT, 512]) for n in ("band_q", "band_k", "band_v"))
            second_projection_stage(k, t)
            t.qaT, t.kaT = k.hT[:, 0:4, :], k.hT[:, 4:8, :]
            t.near = bsb("near_bias", [P, BH, 256])
            band_setup_stage(k, t)
            band_attention_stage(k, t)
        t.gcB = sb("gc_spread", [P, DH, T])
        t.gc_row, t.beta_row, t.eg_row = (sb(n, [P, NT, DH]) for n in ("gc_rows", "beta_rows", "exp_gc_rows"))
        t.egl = sb("exp_gc_chunk_end", [P, DH, T // CH])
        t.k_row, t.v_row = (sb(n, [P, NT, 512]) for n in ("dn_k_rows", "dn_v_rows"))
        t.kdec, t.qgT = k.hT[:, 0:4, :], k.hT[:, 4:8, :]
        delta_setup_stage(k, t)
        t.u = sb("dn_u", [P, NT, 512])
        t.wT = sb("dn_wT", [P, DH, T])
        t.at = sb("dn_intraT", [P, NT, DH, P])
        delta_solve_stage(k, t)
        t.ob = sb("dn_out", [P, NT, 512])
        delta_scan_stage(k, t)
        second_out_stage(k, t)


def expert_rows_stage(k, t):
    nc = k.nc
    with ExitStack() as ctx:
        turned = ctx.enter_context(nc.semaphore("rows_back_turned"))
        copied = Signal(ctx, nc, "rows_back")
        block = ctx.enter_context(nc.Block())
        jobs = [(src, dst, i, half) for src, dst in ((k.hT, t.h_row), (k.xT, t.x_row)) for i in range(NT)
                for half in range(2)]

        @block.tensor
        def _(pe):
            for n, (src, _, i, half) in enumerate(jobs):
                if n >= 8:
                    pe.wait_ge(copied.sem, n - 7)
                for j in range(4):
                    last = pe.transpose(k.bank[n % 8][:, j * P:(j + 1) * P], src[:, 4 * half + j, i * P:(i + 1) * P],
                                        k.const("ident"))
                last.then_inc(turned, 1)

        @block.scalar
        def _(act):
            for n, (_, dst, i, half) in enumerate(jobs):
                act.wait_ge(turned, n + 1)
                post(act, act.activation(dst[:, i, half * 512:(half + 1) * 512], k.bank[n % 8][:], ACT.Copy), copied)


def query_stage(k, t):
    nc, d = k.nc, k.dram
    with ExitStack() as ctx:
        def sb(name, shape):
            return ctx.enter_context(nc.sbuf_tensor(name, shape, F32))

        qT = sb("queriesT", [P, 2 * RH, T])
        sq = sb("query_squares", [P, 2, 2, T])
        keys = sb("sub_keys", [P, 2, P])
        keyT = sb("sub_keysT", [P, 2, P])
        keys_in = ctx.enter_context(nc.semaphore("sub_keys_loaded"))
        keys_turned = ctx.enter_context(nc.semaphore("sub_keys_turned"))
        keys_ok = Signal(ctx, nc, "sub_keys_ready")
        squared = Signal(ctx, nc, "queries_squared")
        summed = ctx.enter_context(nc.semaphore("query_squares_summed"))
        rooted = Signal(ctx, nc, "query_roots")
        scored = ctx.enter_context(nc.semaphore("key_scores_made"))
        plan = columns(find(k, "peer_w_query_2", 0, 2048), k.hT)
        pj = Projection(k, ctx, "queries", plan, banks=range(6))
        block = ctx.enter_context(nc.Block())

        @block.sync
        def _(sp):
            sp.dma_start(keys[:, 0, :], d["peer_sub_keys_1_2"]).then_inc(keys_in, 16)
            sp.dma_start(keys[:, 1, :], d["peer_sub_keys_2_2"]).then_inc(keys_in, 16)
            k.stream(sp, plan[-1][1][-1])

        @block.tensor
        def _(pe):
            pe.wait_ge(keys_in, 32)
            for w in range(2):
                last = pe.transpose(k.bank[7][:, w * P:(w + 1) * P], keys[:, w, :], k.const("ident"))
            last.then_inc(keys_turned, 1)

            def sums(h):
                pe.wait_ge(squared.sem, 2 * (h + 1))
                for i in range(NT):
                    for half in range(2):
                        last = pe.matmul(k.bank[6][:, i * RH + h:i * RH + h + 1],
                                         sq[:, h % 2, half, i * P:(i + 1) * P], k.const("ones", 1),
                                         start=(half == 0), stop=(half == 1))
                last.then_inc(summed, 1)

            for n in range(4):
                pj.run(pe, slice(n, n + 1))
                for h in ((2 * n - 2, 2 * n - 1) if n else ()):
                    sums(h)
            sums(6)
            sums(7)
            pe.wait_ge(pj.freed.sem, 16)
            pe.wait_ge(keys_ok.sem, 2)
            for n in range(4 * NT):
                i, quarter = n // 4, n % 4
                bank = k.bank[n % 6]
                if n >= 6:
                    pe.wait_ge(t.scores_in.sem, n - 5)
                for j in range(4):
                    b = 4 * quarter + j
                    last = pe.matmul(bank[:, j * P:(j + 1) * P], qT[:, b, i * P:(i + 1) * P], keyT[:, b % 2, :],
                                     start=True, stop=True)
                last.then_inc(scored, 1)

        @block.scalar
        def _(act):
            act.wait_ge(keys_turned, 1)
            for w in range(2):
                post(act, act.activation(keyT[:, w, :], k.bank[7][:, w * P:(w + 1) * P], ACT.Copy,
                                         scale=k.col("peer_query_gain_2", w)), keys_ok)
            for b in range(2 * RH):
                bank = pj.next(act)
                post(act, act.activation(qT[:, b, :], bank[:], ACT.Copy), pj.freed)
            act.wait_ge(summed, RH)
            post(act, act.activation(t.q_rstd[:], k.bank[6][:, 0:NT * RH], ACT.Sqrt, bias=k.const("eps"),
                                     scale=1.0 / (2 * P)), rooted)
            for n in range(4 * NT):
                i, quarter = n // 4, n % 4
                act.wait_ge(scored, n + 1)
                post(act, act.activation(t.scores[:, i, quarter * 512:(quarter + 1) * 512], k.bank[n % 6][:], ACT.Copy),
                     t.scores_in)

        @block.vector
        def _(dve):
            for b in range(2 * RH):
                h, half = b // 2, b % 2
                dve.wait_ge(pj.freed.sem, b + 1)
                if h >= 2 and half == 0:
                    dve.wait_ge(summed, h - 1)
                post(dve, dve.tensor_tensor(sq[:, h % 2, half, :], qT[:, b, :], qT[:, b, :], ALU.mult), squared)
            dve.wait_ge(rooted.sem, 1)
            post(dve, dve.reciprocal(t.q_rstd[:], t.q_rstd[:]), k.vstep)


def expert_stage(k, t):
    nc, d = k.nc, k.dram
    GR = 16
    with ExitStack() as ctx:
        def sb(name, shape, dt=F32):
            return ctx.enter_context(nc.sbuf_tensor(name, shape, dt))

        more = sb("more_expert_rows", [P, GR - 4 * SLOTS, D])
        slot = [r[:, 2 * a:2 * a + 2, :].rearrange("p a b -> p (a b)") for r in k.ring for a in range(4)]
        slot += [more[:, a, :] for a in range(GR - 4 * SLOTS)]
        diag = sb("coef_diagonals", [P, 4, P])
        experts = sb("experts", [P, NT, NSEL], I32)
        gates = sb("expert_gates", [P, NT, NSEL])
        dots = sb("expert_dots", [P, NSEL])
        coef = sb("expert_coefs", [P, 2, NSEL])
        left = sb("scores_left_over", [P, 256])
        vals = sb("key_values", [P, 2 * RH, RK])
        kidx = sb("key_indices", [P, 2 * RH, RK], U32)
        kidx_f = sb("key_indices_f", [P, 2 * RH, RK])
        cand = sb("pair_scores", [P, RH, RK * RK])
        ctop = sb("pair_top", [P, RH, RK])
        cpos = sb("pair_positions", [P, RH, RK], U32)
        part = sb("pair_parts", [P, RH, RK], U32)
        part_f = sb("pair_parts_f", [P, RH, RK])
        picked = sb("key_picked", [P, 2, RH, RK])
        gsum = sb("gate_sums", [P, RH])
        here = [ctx.enter_context(nc.semaphore(f"expert_row_in{s}")) for s in range(GR)]
        routed = Signal(ctx, nc, "tile_routed")
        soft_in = Signal(ctx, nc, "gate_exponents")
        soft_out = Signal(ctx, nc, "gate_exps")
        dotted = Signal(ctx, nc, "expert_dots_made")
        gelued = Signal(ctx, nc, "expert_gelus")
        weighed = Signal(ctx, nc, "expert_coefs_ready")
        diag_ok = Signal(ctx, nc, "coef_diagonal_ready")
        summed = ctx.enter_context(nc.semaphore("expert_row_summed"))
        written = Signal(ctx, nc, "tile_result")
        out_ok = k.output_stored
        block = ctx.enter_context(nc.Block())
        QG = NSEL // 4
        out2 = k.out[0].rearrange("(t p) d -> p t d", p=P)

        @block.gpsimd
        def _(pool):
            n = 0
            for i in range(NT):
                pool.wait_ge(routed.sem, i + 1)
                for table in ("peer_expert_down_2", "peer_expert_up_2"):
                    for j in range(NSEL):
                        if n >= GR:
                            tile, r = divmod(n - GR, 2 * NSEL)
                            if r < NSEL:
                                pool.wait_ge(dotted.sem, tile * NSEL + r + 1)
                            else:
                                pool.wait_ge(summed, tile * NSEL + r - NSEL + 1)
                        pool.indirect_dma_start(
                            out=slot[n % GR], out_offset=None, in_=d[table],
                            in_offset=bass.IndirectOffsetOnAxis(ap=experts[:, i, j:j + 1], axis=0),
                        ).then_inc(here[n % GR], 16)
                        n += 1

        def arrived(eng, n):
            eng.wait_ge(here[n % GR], 16 * (n // GR + 1))

        @block.vector
        def _(dve):
            def v(ins):
                post(dve, ins, k.vstep)

            def top16(values, indices, source, width):
                v(dve.max(values[:, 0:8], source))
                v(dve.max_index(indices[:, 0:8], values[:, 0:8], source))
                v(dve.match_replace(left[:, 0:width], values[:, 0:8], source, -3.0e38))
                v(dve.max(values[:, 8:16], left[:, 0:width]))
                v(dve.max_index(indices[:, 8:16], values[:, 8:16], left[:, 0:width]))

            def route(i):
                for b in range(2 * RH):
                    top16(vals[:, b, :], kidx[:, b, :], t.scores[:, i, b * NKEY:(b + 1) * NKEY], NKEY)
                v2 = vals[:].rearrange("p (h two) s -> p two h s", two=2)
                shape = [P, RH, RK, RK]
                v(dve.tensor_tensor(cand[:].rearrange("p h (a b) -> p h a b", a=RK), bc(v2[:, 0], 3, shape),
                                    bc(v2[:, 1], 2, shape), ALU.add))
                for h in range(RH):
                    top16(ctop[:, h, :], cpos[:, h, :], cand[:, h, :], RK * RK)
                v(dve.tensor_copy(kidx_f[:], kidx[:]))
                i2 = kidx_f[:].rearrange("p (h two) s -> p two h s", two=2)
                hot = cand[:].rearrange("p h (a b) -> p h a b", a=RK)
                iota = k.const("iota16").unsqueeze(1).unsqueeze(1).broadcast_to(shape)
                for w, (op, by) in enumerate(((ALU.logical_shift_right, 4), (ALU.bitwise_and, 15))):
                    v(dve.tensor_scalar(part[:], cpos[:], by, None, op))
                    v(dve.tensor_copy(part_f[:], part[:]))
                    v(dve.tensor_tensor(hot, iota, bc(part_f[:], 3, shape), ALU.is_equal))
                    v(dve.tensor_tensor(hot, hot, bc(i2[:, w], 2, shape), ALU.mult))
                    v(dve.tensor_reduce(picked[:, w], hot, AX, ALU.add))
                e3 = experts[:, i, :].rearrange("p (h s) -> p h s", h=RH)
                v(dve.scalar_tensor_tensor(e3, picked[:, 0], float(NKEY), picked[:, 1], ALU.mult, ALU.add))
                g3 = gates[:, i, :].rearrange("p (h s) -> p h s", h=RH)
                sh = [P, RH, RK]
                v(dve.tensor_tensor(g3, ctop[:], ctop[:, :, 0:1].broadcast_to(sh), ALU.subtract))
                post(dve, dve.tensor_tensor(g3, g3, bc(t.q_rstd[:, i * RH:(i + 1) * RH], 2, sh), ALU.mult), soft_in)
                dve.wait_ge(soft_out.sem, i + 1)
                v(dve.tensor_reduce(gsum[:], g3, AX, ALU.add))
                v(dve.reciprocal(gsum[:], gsum[:]))
                post(dve, dve.tensor_tensor(g3, g3, bc(gsum[:], 2, sh), ALU.mult), routed)

            route(0)
            for i in range(NT):
                for j in range(NSEL):
                    n = 2 * NSEL * i + j
                    arrived(dve, n)
                    row = slot[n % GR]
                    if j % QG == 0 and (i or j):
                        dve.wait_ge(gelued.sem, 4 * i + j // QG)
                    post(dve, dve.tensor_tensor_reduce(row, row, t.h_row[:, i, :], 1.0, 0.0, ALU.mult, ALU.add,
                                                       dots[:, j:j + 1]), dotted)
                    if j % QG == QG - 1:
                        q = j // QG
                        dve.wait_ge(gelued.sem, 4 * i + q + 1)
                        cs = slice(q * QG, (q + 1) * QG)
                        if i >= 2 and q == 0:
                            dve.wait_ge(summed, (i - 1) * NSEL)
                        post(dve, dve.tensor_tensor(coef[:, i % 2, cs], dots[:, cs], gates[:, i, cs], ALU.mult), weighed)
                if i + 1 < NT:
                    route(i + 1)
                dve.wait_ge(summed, (i + 1) * NSEL)
                for half in range(2):
                    hs = slice(half * 512, (half + 1) * 512)
                    bank = k.bank[2 * (i % 2) + half]
                    v(dve.tensor_tensor(t.result[:, hs], bank[:], k.gate2[:, hs], ALU.mult))
                post(dve, dve.tensor_tensor(t.x_row[:, i, :], t.x_row[:, i, :], t.result[:], ALU.add), written)

        @block.scalar
        def _(act):
            def soft(i):
                act.wait_ge(soft_in.sem, i + 1)
                post(act, act.activation(gates[:, i, :], gates[:, i, :], ACT.Exp), soft_out)

            soft(0)
            for i in range(NT):
                for q in range(4):
                    act.wait_ge(dotted.sem, i * NSEL + (q + 1) * QG)
                    cs = slice(q * QG, (q + 1) * QG)
                    post(act, act.activation(dots[:, cs], dots[:, cs], ACT.Gelu), gelued)
                for j in range(NSEL):
                    m = i * NSEL + j
                    act.wait_ge(weighed.sem, 4 * i + j // QG + 1)
                    if m >= 4:
                        act.wait_ge(summed, m - 3)
                    post(act, act.activation(diag[:, m % 4, :], k.const("ident"), ACT.Copy,
                                             scale=coef[:, i % 2, j:j + 1]), diag_ok)
                    if j == NSEL // 2 and i + 1 < NT:
                        soft(i + 1)

        @block.tensor
        def _(pe):
            for i in range(NT):
                if i >= 2:
                    pe.wait_ge(written.sem, i - 1)
                for j in range(NSEL):
                    m, n = i * NSEL + j, 2 * NSEL * i + NSEL + j
                    arrived(pe, n)
                    pe.wait_ge(diag_ok.sem, m + 1)
                    for half in range(2):
                        last = pe.matmul(k.bank[2 * (i % 2) + half][:], diag[:, m % 4, :],
                                         slot[n % GR][:, half * 512:(half + 1) * 512],
                                         start=(j == 0), stop=(j == NSEL - 1))
                    last.then_inc(summed, 1)

        @block.sync
        def _(sp):
            for i in range(NT):
                sp.wait_ge(written.sem, i + 1)
                sp.dma_start(out2[:, i, :], t.x_row[:, i, :]).then_inc(out_ok, 16)
            sp.wait_ge(out_ok, 16 * NT)


def expert_branch(k):
    nc = k.nc
    with ExitStack() as ctx:
        def sb(name, shape):
            return ctx.enter_context(nc.sbuf_tensor(name, shape, F32))

        t = Part()
        t.h_row, t.x_row = sb("h_rows", [P, NT, D]), sb("x_out_rows", [P, NT, D])
        t.scores = sb("key_scores", [P, NT, 2 * RH * NKEY])
        t.q_rstd = sb("query_rstd", [P, NT * RH])
        t.scores_in = Signal(ctx, nc, "key_scores_in")
        expert_rows_stage(k, t)
        query_stage(k, t)
        t.result = k.xT[:, 0:2, :].rearrange("p a b -> p (a b)")
        expert_stage(k, t)


def recycle(nc):
    ids = sorted(set(nc.released_uncleared_semaphores))
    runs = []
    for n in ids:
        if runs and runs[-1][1] == n:
            runs[-1][1] = n + 1
        else:
            runs.append([n, n + 1])
    for first, end in runs:
        nc.gpsimd.sem_clear(range(first, end))
    nc.all_engine_barrier()


def build(nc, dram, out, upto=99):
    with ExitStack() as ctx:
        k = Kernel(nc, ctx, dram, out)
        load_stage(k)
        modulation_stage(k)
        norm_stage(k, "norm1", "norm_g", k.mod1, 0, 8)
        with nc.sbuf_tensor("merged", [P, KD, T], F32) as k.merged:
            attention_branch(k)
            if upto < 2:
                return
            recycle(nc)
            ssm_branch(k)
        recycle(nc)
        if upto < 3:
            return
        norm_stage(k, "norm2", "norm1_gain_2", k.mod2, 0, 8)
        second_mixer(k)
        if upto < 4:
            return
        recycle(nc)
        norm_stage(k, "norm3", "norm2_gain_2", k.mod2, 24, 32)
        expert_branch(k)


def _tables():
    p = np.arange(P)
    row, colm = p[:, None], p[None, :]
    same64 = (row // 64) == (colm // 64)
    m = {"ident": np.eye(P), "flip": np.eye(P)[::-1], "ones": np.ones((P, P)), "causal_add": np.where(colm <= row, 0.0, NEG),
         "s_le_l": (row <= colm), "strict64": same64 & (colm < row), "upper64": same64 & (row <= colm),
         "iota16": np.tile(np.arange(16), (P, 1)), "eps": np.full((P, 1), EPS),
         "band_add": np.where((colm // 64) <= (row // 64), 0.0, NEG)}
    f = np.float32

    def inv(n):
        return np.power(f(500000.0), -(np.arange(0, n, 2, dtype=f) / f(n))).astype(f)

    m["inv_freq"] = np.tile(np.concatenate([inv(32), inv(16)]), (P, 1))
    for size in (1, 2, 4, 8, 16, 32):
        low = ((row // (2 * size)) == (colm // (2 * size))) & (row % (2 * size) >= size) & (colm % (2 * size) < size)
        if size == 1:
            m["lvl1"], m["lvl1T"] = low, low.T
        else:
            m[f"lvlT{size}"] = low.T
    return np.concatenate([np.asarray(m[n], f).reshape(P, w) for n, w in CONSTS], axis=1)


_DIRECT = ["x", "positions", "ada_w", "w_in", "w_branch_att", "w_branch_ssm", "w_out", "w_ada_2", "w_in_2",
           "w_out_2", "attn_rel_bias_2", "peer_w_query_2", "peer_sub_keys_1_2", "peer_sub_keys_2_2",
           "peer_expert_down_2", "peer_expert_up_2"]


def _layout(inputs):
    a = {n: np.asarray(v) for n, v in inputs.items()}
    out = {"consts": _tables()}
    for n in _DIRECT:
        v = a[n]
        out[n] = np.ascontiguousarray(v[0] if v.ndim == 3 else v)
    for n in ("peer_sub_keys_1_2", "peer_sub_keys_2_2", "peer_expert_down_2", "peer_expert_up_2", "attn_rel_bias_2"):
        out[n] = np.ascontiguousarray(a[n][0])

    out["positions"] = np.ascontiguousarray(a["positions"].reshape(NT, P).T)

    out["rel_bias_reversed"] = np.ascontiguousarray(out.pop("attn_rel_bias_2")[:, ::-1])

    def columns_of(n, w):
        if n in ("conv_w", "dn_conv_w_2"):
            v = a[n][0]
            return v.reshape(4, -1, P).transpose(2, 0, 1).reshape(P, w)
        v = a[n].reshape(-1)
        if v.size < P:
            full = np.zeros(P, v.dtype)
            full[:v.size] = v
            v = full
        return v.reshape(w, P).T

    out["cols"] = np.ascontiguousarray(np.concatenate([columns_of(n, w) for n, w in COLS], axis=1))
    rows = {n: a[n].reshape(-1) for n, _ in ROWS if n in a}
    rows["gate2_b"] = a["b_ada_2"].reshape(-1)[5 * D:6 * D]
    rows["rel_far"] = a["attn_rel_bias_2"][0][:, 256]
    out["rows"] = np.ascontiguousarray(np.concatenate([rows[n] for n, _ in ROWS])[None, :])
    return out


def kernel(**inputs):
    import concourse.bacc as _bacc
    from concourse.bass_utils import run_bass_kernel_spmd as _run

    nc = _bacc.Bacc("TRN2", target_bir_lowering=False, num_devices=1)
    arrays = _layout(inputs)
    dram = {n: nc.dram_tensor(f"in_{n}", a.shape, mybir.dt.from_np(a.dtype), kind="ExternalInput").ap()
            for n, a in arrays.items()}
    out = nc.dram_tensor("out", (1, T, D), F32, kind="ExternalOutput").ap()
    build(nc, dram, out)
    r = _run(nc, [{f"in_{n}": a for n, a in arrays.items()}], core_ids=[0])
    return r.results[0]["out"]
```

```python
from contextlib import ExitStack

import concourse.bass as bass
from concourse import mybir
import numpy as np

F32 = mybir.dt.float32
I32 = mybir.dt.int32
U32 = mybir.dt.uint32
ALU = mybir.AluOpType
ACT = mybir.ActivationFunctionType
AX = mybir.AxisListType.X

P = 128
D = 1024
KD = D // P
T = 512
NT = T // P
EPS = 1e-6
NEG = -1.0e30
SLOTS = 3
TWO_PI = 2.0 * np.pi

Q0, KV0, ZA0, IX0 = 0, 1024, 1536, 2560
ZS0, XBC0, DT0, GA0, GS0 = 2884, 4932, 8004, 8036, 9060
IDX_COLS = 4 * 64 + 64 + 4
AH, AKV, IH = 8, 2, 4
TOPK = 128
SH, SG, SP_ = 32, 4, 64
QA0, KA0, VA0, QKV0, ZB0, BA0 = 0, 512, 1024, 1536, 3072, 3584
BH, BD = 8, 64
DH, CH = 4, 64
RH, RK, NKEY = 8, 16, 128
NSEL = RH * RK

COLS = [("c", 8), ("c_2", 8), ("ada_b", 24), ("norm_g", 8), ("conv_b", 24), ("conv_w", 96),
        ("ssm_norm_g", 16), ("b_ada_2", 48), ("norm1_gain_2", 8), ("dn_conv_w_2", 48),
        ("attn_out_gain_2", 4), ("dn_out_gain_2", 1), ("norm2_gain_2", 8), ("peer_query_gain_2", 2),
        ("dt_bias", 1), ("a_log", 1), ("dn_dt_bias_2", 1), ("dn_a_log_2", 1)]
ROWS = [("q_norm_g", 128), ("k_norm_g", 128), ("idx_k_ln_g", 64), ("idx_k_ln_b", 64), ("d_skip", 32),
        ("attn_q_gain_2", 64), ("attn_k_gain_2", 64), ("gate2_b", 1024), ("rel_far", 8)]
CONSTS = [("ident", 128), ("ones", 128), ("causal_add", 128), ("s_le_l", 128), ("strict64", 128),
          ("upper64", 128), ("inv_freq", 24), ("iota16", 16), ("eps", 1), ("band_add", 128),
          ("lvl1", 128), ("lvl1T", 128), ("lvlT2", 128), ("lvlT4", 128), ("lvlT8", 128),
          ("lvlT16", 128), ("lvlT32", 128), ("flip", 128)]


def offsets(table):
    at, out = 0, {}
    for name, n in table:
        out[name] = (at, n)
        at += n
    return out, at


COL_AT, NCOL = offsets(COLS)
ROW_AT, NROW = offsets(ROWS)
CONST_AT, NCONST = offsets(CONSTS)


class Signal:

    def __init__(self, ctx, nc, name):
        self.sem = ctx.enter_context(nc.semaphore(name))
        self.n = 0


def post(eng, ins, sig):
    ins.then_inc(sig.sem, 1)
    sig.n += 1
    eng.wait_ge(sig.sem, sig.n)


class Kernel:

    def __init__(self, nc, ctx, dram, out):
        self.nc, self.ctx, self.dram, self.out = nc, ctx, dram, out
        sb = self.keep
        self.consts = sb("consts", [P, NCONST])
        self.cols = sb("cols", [P, NCOL])
        self.rows = sb("rows", [P, NROW])
        self.xT = sb("xT", [P, KD, T])
        self.hT = sb("hT", [P, KD, T])
        self.mod1 = sb("mod1", [P, 24])
        self.mod2 = sb("mod2", [P, 48])
        self.gate2 = sb("gate2", [P, D])
        self.ring = [sb(f"ring{i}", [P, KD, 512]) for i in range(SLOTS)]
        self.bank = [ctx.enter_context(nc.psum_tensor(f"bank{i}", [P, 512], F32)) for i in range(8)]
        self.vstep = Signal(ctx, nc, "vector_step")
        self.astep = Signal(ctx, nc, "scalar_step")
        self.gstep = Signal(ctx, nc, "gpsimd_step")
        self.loaded = [ctx.enter_context(nc.semaphore(f"weights_loaded{i}")) for i in range(SLOTS)]
        self.used = Signal(ctx, nc, "weights_used")
        self.output_stored = ctx.enter_context(nc.semaphore("output_stored"))
        self.issued = 0
        self.chunks = self.weight_chunks()
        self.modulation = Modulation(self)

    def keep(self, name, shape, dt=F32):
        return self.ctx.enter_context(self.nc.sbuf_tensor(name, shape, dt))

    def const(self, name, n=None, p=P):
        at, w = CONST_AT[name]
        return self.consts[0:p, at:at + (n or w)]

    def col(self, name, i=0, n=1, p=P):
        at, _ = COL_AT[name]
        return self.cols[0:p, at + i:at + i + n]

    def row(self, name, p=P):
        at, w = ROW_AT[name]
        return self.rows[0:p, at:at + w]

    def weight_chunks(self):
        d = self.dram

        def cut(name, c0, n, k0=0):
            w = d[name][k0:k0 + D, :]
            return [(name, c, k0, w[:, c:min(c + 512, c0 + n)].rearrange("(k p) n -> p k n", p=P), min(512, c0 + n - c))
                    for c in range(c0, c0 + n, 512)]

        out = cut("ada_w", 0, 3072)
        out += cut("w_in", Q0, 1024) + cut("w_in", KV0, 512) + cut("w_in", IX0, IDX_COLS)
        out += cut("w_in", ZA0, 1024)
        out += cut("w_ada_2", 0, 6144)
        out += cut("w_in", GA0, 1024) + cut("w_branch_att", 0, 1024)
        out += cut("w_in", XBC0, 3072) + cut("w_in", DT0, 32) + cut("w_in", ZS0, 2048)
        out += cut("w_in", GS0, 1024)
        for c in (0, 512):
            out += cut("w_branch_ssm", c, 512) + cut("w_branch_ssm", c, 512, D)
        out += cut("w_out", 0, 1024)
        out += cut("w_in_2", QA0, 512) + cut("w_in_2", KA0, 512) + cut("w_in_2", VA0, 512)
        out += cut("w_in_2", QKV0, 1536) + cut("w_in_2", ZB0, 512) + cut("w_in_2", BA0, 8)
        out += cut("w_out_2", 0, 1024) + cut("peer_w_query_2", 0, 2048)
        return out

    def stream(self, sp, last):
        upto = min(len(self.chunks), last + SLOTS)
        for g in range(self.issued, upto):
            if g >= SLOTS:
                sp.wait_ge(self.used.sem, g - SLOTS + 1)
            n = self.chunks[g][4]
            sp.dma_start(self.ring[g % SLOTS][:, :, 0:n], self.chunks[g][3]).then_inc(self.loaded[g % SLOTS], 16)
        self.issued = max(self.issued, upto)

    def take(self, pe, g):
        pe.wait_ge(self.loaded[g % SLOTS], 16 * (g // SLOTS + 1))
        return self.ring[g % SLOTS]


def load_stage(k):
    nc, d = k.nc, k.dram
    with ExitStack() as ctx:
        x = ctx.enter_context(nc.sbuf_tensor("x_rows", [P, NT, D], F32))
        small = ctx.enter_context(nc.semaphore("small_loaded"))
        x_in = ctx.enter_context(nc.semaphore("x_loaded"))
        turned = ctx.enter_context(nc.semaphore("x_turned"))
        block = ctx.enter_context(nc.Block())

        @block.sync
        def _(sp):
            sp.dma_start(k.consts[:], d["consts"]).then_inc(small, 16)
            sp.dma_start(x[:], d["x"].rearrange("(t p) d -> p t d", p=P)).then_inc(x_in, 16)
            k.stream(sp, -1)
            sp.wait_ge(small, 48)

        @block.scalar
        def _(act):
            act.dma_start(k.cols[:], d["cols"]).then_inc(small, 16)
            act.dma_start(k.rows[:], d["rows"].to_broadcast([P, NROW])).then_inc(small, 16)
            for i in range(KD):
                act.wait_ge(turned, i + 1)
                post(act, nc.scalar.activation(k.xT[:, i, :], k.bank[i][:], ACT.Copy), k.astep)

        @block.tensor
        def _(pe):
            pe.wait_ge(small, 48)
            pe.wait_ge(x_in, 16)
            for i in range(KD):
                for t in range(NT):
                    last = nc.tensor.transpose(k.bank[i][:, t * P:(t + 1) * P], x[:, t, i * P:(i + 1) * P],
                                               k.const("ident"))
                last.then_inc(turned, 1)


class Modulation:

    def __init__(self, k):
        self.k = k
        self.silu_c = k.keep("silu_c", [P, 2, 8])
        self.gs = [find(k, "ada_w", 0, 3072), find(k, "w_ada_2", 0, 6144)]
        self.steps = [(which, i, g) for which in range(2) for i, g in enumerate(self.gs[which])]
        self.row_in = k.ctx.enter_context(k.nc.semaphore("mod_row_copied"))
        self.turned = k.ctx.enter_context(k.nc.semaphore("mod_row_turned"))
        self.columns_in = k.ctx.enter_context(k.nc.semaphore("mod_columns_copied"))

    def rows_buffer(self, ctx, name):
        self.rows = ctx.enter_context(self.k.nc.sbuf_tensor(name, [1, 2, 512], F32))

    def multiply(self, pe, n):
        which, _, g = self.steps[n]
        w = self.k.take(pe, g)
        if n > 1:
            pe.wait_ge(self.row_in, n - 1)
        for kk in range(KD):
            last = pe.matmul(self.k.bank[6 + n % 2][0:1, :], self.silu_c[:, which, kk:kk + 1], w[:, kk, :],
                             start=(kk == 0), stop=(kk == KD - 1))
        last.then_inc(self.k.used.sem, 1)
        self.k.used.n += 1

    def turn(self, pe, n):
        pe.wait_ge(self.row_in, n + 1)
        if n > 0:
            pe.wait_ge(self.columns_in, n)
        for b in range(4):
            last = pe.matmul(self.k.bank[5][:, b:b + 1], self.rows[:, n % 2, b * P:(b + 1) * P],
                             self.k.const("ones", 1, 1), start=True, stop=True)
        last.then_inc(self.turned, 1)

    def copy_row(self, act, n):
        act.wait_ge(self.k.used.sem, self.steps[n][2] + 1)
        if n > 1:
            act.wait_ge(self.turned, n - 1)
        act.activation(self.rows[:, n % 2, :], self.k.bank[6 + n % 2][0:1, :], ACT.Copy).then_inc(self.row_in, 1)

    def copy_columns(self, act, n):
        which, i, _ = self.steps[n]
        act.wait_ge(self.turned, n + 1)
        dst = (self.k.mod1, self.k.mod2)[which][:, 4 * i:4 * i + 4]
        act.activation(dst, self.k.bank[5][:, 0:4], ACT.Copy).then_inc(self.columns_in, 1)

    def on_tensor(self, pe, steps):
        for n in steps:
            self.multiply(pe, n)
            if n > steps[0]:
                self.turn(pe, n - 1)
        self.turn(pe, steps[-1])

    def on_scalar(self, act, steps):
        for n in steps:
            self.copy_row(act, n)
            if n > steps[0]:
                self.copy_columns(act, n - 1)
        self.copy_columns(act, steps[-1])


def modulation_stage(k):
    nc, m = k.nc, k.modulation
    with ExitStack() as ctx:
        m.rows_buffer(ctx, "mod1_rows")
        silu = ctx.enter_context(nc.semaphore("silu_c_ready"))
        block = ctx.enter_context(nc.Block())
        steps = range(len(m.gs[0]))

        @block.sync
        def _(sp):
            k.stream(sp, m.gs[0][-1])

        @block.scalar
        def _(act):
            act.activation(m.silu_c[:, 0, :], k.col("c", 0, 8), ACT.Silu).then_inc(silu, 1)
            act.activation(m.silu_c[:, 1, :], k.col("c_2", 0, 8), ACT.Silu).then_inc(silu, 1)
            m.on_scalar(act, steps)

        @block.tensor
        def _(pe):
            pe.wait_ge(silu, 2)
            m.on_tensor(pe, steps)

        @block.vector
        def _(dve):
            dve.wait_ge(m.columns_in, len(steps))
            post(dve, dve.tensor_tensor(k.mod1[:], k.mod1[:], k.col("ada_b", 0, 24), ALU.add), k.vstep)


def norm_stage(k, name, gain, mod, shift, scale):
    nc = k.nc
    with ExitStack() as ctx:
        sq = ctx.enter_context(nc.sbuf_tensor(f"{name}_squares", [P, KD, T], F32))
        rstd = ctx.enter_context(nc.sbuf_tensor(f"{name}_rstd", [P, T], F32))
        gs = ctx.enter_context(nc.sbuf_tensor(f"{name}_gain", [P, KD], F32))
        squared = Signal(ctx, nc, f"{name}_squared")
        summed = ctx.enter_context(nc.semaphore(f"{name}_summed"))
        rooted = Signal(ctx, nc, f"{name}_rooted")
        block = ctx.enter_context(nc.Block())

        @block.vector
        def _(dve):
            for i in range(KD):
                post(dve, dve.tensor_tensor(sq[:, i, :], k.xT[:, i, :], k.xT[:, i, :], ALU.mult), squared)
            post(dve, dve.tensor_scalar(gs[:], mod[:, scale:scale + KD], 1.0, None, ALU.add), k.vstep)
            post(dve, dve.tensor_tensor(gs[:], gs[:], k.col(gain, 0, KD), ALU.mult), k.vstep)
            dve.wait_ge(rooted.sem, 1)
            post(dve, dve.reciprocal(rstd[:], rstd[:]), k.vstep)
            for i in range(KD):
                post(dve, dve.tensor_tensor(k.hT[:, i, :], k.xT[:, i, :], rstd[:], ALU.mult), k.vstep)
                post(dve, dve.tensor_scalar(k.hT[:, i, :], k.hT[:, i, :], gs[:, i:i + 1],
                                            mod[:, shift + i:shift + i + 1], ALU.mult, ALU.add), k.vstep)

        @block.tensor
        def _(pe):
            for i in range(KD):
                pe.wait_ge(squared.sem, i + 1)
                last = pe.matmul(k.bank[0][:], k.const("ones"), sq[:, i, :], start=(i == 0), stop=(i == KD - 1))
            last.then_inc(summed, 1)

        @block.scalar
        def _(act):
            act.wait_ge(summed, 1)
            post(act, act.activation(rstd[:], k.bank[0][:], ACT.Sqrt, bias=k.const("eps"), scale=1.0 / D), rooted)


class Projection:

    def __init__(self, k, ctx, name, plan, banks=range(8)):
        self.k, self.banks, self.plan = k, list(banks), plan
        self.done = ctx.enter_context(k.nc.semaphore(f"{name}_product"))
        self.freed = Signal(ctx, k.nc, f"{name}_freed")
        self.made = self.taken = 0
        self.there = []
        count = 0
        for kind, gs, _, _ in plan:
            outs = NT if kind == "rows" else max(1, k.chunks[gs[-1]][4] // P)
            for i in range(outs):
                if i == outs - 1:
                    self.there.append((k.used.sem, gs[-1] + 1))
                else:
                    count += 1
                    self.there.append((self.done, count))

    def _bank(self, pe):
        n = len(self.banks)
        if self.made >= n:
            pe.wait_ge(self.freed.sem, self.made - n + 1)
        self.made += 1
        return self.k.bank[self.banks[(self.made - 1) % n]]

    def run(self, pe, items=None):
        k = self.k
        for kind, gs, fixed, part in (self.plan if items is None else self.plan[items]):
            outs = NT if kind == "rows" else max(1, k.chunks[gs[-1]][4] // P)
            held = [None] * outs
            for which, g in enumerate(gs):
                w = k.take(pe, g)
                n = k.chunks[g][4]
                wide = min(n, P)
                for i in range(outs):
                    if which == 0:
                        held[i] = self._bank(pe)
                    for kk in range(KD):
                        flags = dict(start=(which == 0 and kk == 0), stop=(which == len(gs) - 1 and kk == KD - 1))
                        if kind == "rows":
                            last = pe.matmul(held[i][:, 0:n], fixed[:, kk, i * P:(i + 1) * P], w[:, kk, 0:n], **flags)
                        else:
                            last = pe.matmul(held[i][0:wide, :], w[:, kk, i * P:i * P + wide],
                                             fixed[:, which * KD + kk, :], **flags)
                    if i == outs - 1:
                        last.then_inc(k.used.sem, 1)
                        k.used.n += 1
                    elif which == len(gs) - 1:
                        last.then_inc(self.done, 1)

    def next(self, eng):
        sem, value = self.there[self.taken]
        eng.wait_ge(sem, value)
        self.taken += 1
        return self.k.bank[self.banks[(self.taken - 1) % len(self.banks)]]


def columns(gs, rhs):
    return [("columns", (g,), rhs, None) for g in gs]


def token_rows(gs, lhs):
    return [("rows", (g,), lhs, None) for g in gs]


def find(k, name, c0, n, k0=0):
    return [g for g, (w, c, kk, _, _) in enumerate(k.chunks) if w == name and c0 <= c < c0 + n and kk == k0]


def attention_projection_stage(k, t):
    nc = k.nc
    with ExitStack() as ctx:
        plan = token_rows(find(k, "w_in", Q0, 1024) + find(k, "w_in", KV0, 512) + find(k, "w_in", IX0, IDX_COLS), k.hT)
        plan += columns(find(k, "w_in", ZA0, 1024), k.hT)
        pj = Projection(k, ctx, "attention_in", plan)
        block = ctx.enter_context(nc.Block())

        @block.sync
        def _(sp):
            k.stream(sp, plan[-1][1][-1])

        @block.tensor
        def _(pe):
            pj.run(pe)

        @block.scalar
        def _(act):
            for c, (dst, c0, n) in enumerate([(t.q, 0, 512), (t.q, 512, 512), (t.kv, 0, 512), (t.ix, 0, IDX_COLS)]):
                for i in range(NT):
                    bank = pj.next(act)
                    post(act, act.activation(dst[:, i, c0:c0 + n], bank[:, 0:n], ACT.Copy), pj.freed)
            for j in range(8):
                bank = pj.next(act)
                post(act, act.activation(t.zT[:, j, :], bank[:], ACT.Silu), pj.freed)


def bc(ap, axis, shape):
    return ap.unsqueeze(axis).broadcast_to(shape)


def rotate(k, dve, x, cos, sin, tmp, half, heads):
    shape = [P, NT, heads, half]
    x1, x2 = x[:, :, :, 0:half], x[:, :, :, half:2 * half]
    c, s = bc(cos, 2, shape), bc(sin, 2, shape)
    a, b, e, f = (tmp[:, i, 0:NT * heads * half].rearrange("p (t h d) -> p t h d", t=NT, h=heads) for i in range(4))
    post(dve, dve.tensor_tensor(a, x1, c, ALU.mult), k.vstep)
    post(dve, dve.tensor_tensor(b, x2, s, ALU.mult), k.vstep)
    post(dve, dve.tensor_tensor(e, x2, c, ALU.mult), k.vstep)
    post(dve, dve.tensor_tensor(f, x1, s, ALU.mult), k.vstep)
    post(dve, dve.tensor_tensor(x1, a, b, ALU.subtract), k.vstep)
    post(dve, dve.tensor_tensor(x2, e, f, ALU.add), k.vstep)


def attention_rotary_stage(k, t):
    nc, d = k.nc, k.dram
    with ExitStack() as ctx:
        def sb(name, shape, dt=F32):
            return ctx.enter_context(nc.sbuf_tensor(name, shape, dt))

        pos = sb("positions", [P, NT], I32)
        posf = sb("positions_f", [P, NT])
        ang = sb("angle", [P, NT, 24])
        turns = sb("turns", [P, NT, 24])
        red = sb("angle_reduced", [P, 2, NT, 24])
        trig = sb("sin_cos", [P, 2, NT, 24])
        sq = k.merged[:].rearrange("p k t -> p (k t)")
        ssum = sb("head_sums", [P, 44])
        rstd = sb("head_rstd", [P, 44])
        mean = sb("idx_mean", [P, NT])
        tmp = sb("rope_products", [P, 4, NT * AH * 16])
        kdup = sb("idx_k_twice", [P, NT, 2, 64])
        m = k.modulation
        m.rows_buffer(ctx, "mod2_rows_a")
        first = len(m.gs[0])
        steps = range(first, first + len(m.gs[1]) // 2)
        pos_in = ctx.enter_context(nc.semaphore("positions_loaded"))
        reduced = Signal(ctx, nc, "angles_reduced")
        trig_ok = Signal(ctx, nc, "trig_ready")
        summed = Signal(ctx, nc, "head_squares_summed")
        rooted = Signal(ctx, nc, "head_roots")
        ready = Signal(ctx, nc, "rows_rotated")
        turned = ctx.enter_context(nc.semaphore("rows_turned"))
        block = ctx.enter_context(nc.Block())
        q4 = t.q[:].rearrange("p t (h d) -> p t h d", h=AH)
        k4 = t.kv[:, :, 0:256].rearrange("p t (h d) -> p t h d", h=AKV)
        v2 = None
        qi4 = t.ix[:, :, 0:256].rearrange("p t (h d) -> p t h d", h=IH)
        ki = t.ix[:, :, 256:320]

        @block.sync
        def _(sp):
            sp.dma_start(pos[:], d["positions"]).then_inc(pos_in, 16)
            k.stream(sp, m.steps[steps[-1]][2])

        @block.vector
        def _(dve):
            def v(ins):
                post(dve, ins, k.vstep)

            dve.wait_ge(pos_in, 16)
            v(dve.tensor_copy(posf[:], pos[:]))
            v(dve.tensor_tensor(ang[:], bc(posf[:], 2, [P, NT, 24]), bc(k.const("inv_freq"), 1, [P, NT, 24]), ALU.mult))
            magic = 12582912.0
            hi, mid, lo = 6.28125, 0.0019340515136718750, 1.2556659146e-06
            hi_mid_lo = (hi, mid, lo)
            for w, quarter in ((0, 0.0), (1, 0.25)):
                v(dve.tensor_scalar(turns[:], ang[:], 1.0 / TWO_PI, quarter, ALU.mult, ALU.add))
                v(dve.tensor_scalar(turns[:], turns[:], magic, None, ALU.add))
                v(dve.tensor_scalar(turns[:], turns[:], magic, None, ALU.subtract))
                src = ang[:]
                for part in hi_mid_lo:
                    v(dve.scalar_tensor_tensor(red[:, w], turns[:], -part, src, ALU.mult, ALU.add))
                    src = red[:, w]
                if quarter:
                    v(dve.tensor_scalar(red[:, w], red[:, w], TWO_PI / 4, None, ALU.add))
                v(dve.tensor_scalar(red[:, w], red[:, w], 3.1415925, None, ALU.min))
                ins = dve.tensor_scalar(red[:, w], red[:, w], -3.1415925, None, ALU.max)
                post(dve, ins, reduced)

            v(dve.tensor_tensor(sq, t.q[:].rearrange("p t n -> p (t n)"), t.q[:].rearrange("p t n -> p (t n)"), ALU.mult))
            v(dve.tensor_reduce(ssum[:, 0:32], sq.rearrange("p (a d) -> p a d", d=P), AX, ALU.add))
            ksq = sq[:, 0:1024].rearrange("p (t h d) -> p t h d", t=NT, h=AKV)
            v(dve.tensor_tensor(ksq, k4, k4, ALU.mult))
            v(dve.tensor_reduce(ssum[:, 32:40], sq[:, 0:1024].rearrange("p (a d) -> p a d", d=P), AX, ALU.add))
            v(dve.tensor_reduce(mean[:], ki, AX, ALU.add))
            v(dve.tensor_scalar(mean[:], mean[:], 1.0 / 64, None, ALU.mult))
            v(dve.tensor_tensor(ki, ki, bc(mean[:], 2, [P, NT, 64]), ALU.subtract))
            kisq = sq[:, 0:256].rearrange("p (t d) -> p t d", t=NT)
            v(dve.tensor_tensor(kisq, ki, ki, ALU.mult))
            v(dve.tensor_reduce(ssum[:, 40:44], kisq, AX, ALU.add))
            post(dve, dve.tensor_scalar(ssum[:, 40:44], ssum[:, 40:44], 2.0, None, ALU.mult), summed)
            dve.wait_ge(rooted.sem, 1)
            v(dve.reciprocal(rstd[:], rstd[:]))
            for x4, at, heads, gain in ((q4, 0, AH, "q_norm_g"), (k4, 32, AKV, "k_norm_g")):
                r = rstd[:, at:at + NT * heads].rearrange("p (t h) -> p t h", t=NT)
                v(dve.tensor_tensor(x4, x4, bc(r, 3, [P, NT, heads, P]), ALU.mult))
                g = k.row(gain).unsqueeze(1).unsqueeze(1).broadcast_to([P, NT, heads, P])
                v(dve.tensor_tensor(x4, x4, g, ALU.mult))
            v(dve.tensor_tensor(ki, ki, bc(rstd[:, 40:44], 2, [P, NT, 64]), ALU.mult))
            v(dve.tensor_tensor(ki, ki, bc(k.row("idx_k_ln_g"), 1, [P, NT, 64]), ALU.mult))
            v(dve.tensor_tensor(ki, ki, bc(k.row("idx_k_ln_b"), 1, [P, NT, 64]), ALU.add))
            v(dve.tensor_scalar(t.ix[:, :, 320:324], t.ix[:, :, 320:324], 0.125 * 0.5, None, ALU.mult))
            dve.wait_ge(trig_ok.sem, 2)
            sa, ca = trig[:, 0, :, 0:16], trig[:, 1, :, 0:16]
            si, ci = trig[:, 0, :, 16:24], trig[:, 1, :, 16:24]
            rotate(k, dve, q4, ca, sa, tmp, 16, AH)
            rotate(k, dve, k4, ca, sa, tmp, 16, AKV)
            rotate(k, dve, qi4, ci, si, tmp, 8, IH)
            rotate(k, dve, ki.unsqueeze(2), ci, si, tmp, 8, 1)
            post(dve, dve.tensor_copy(kdup[:], bc(ki, 2, [P, NT, 2, 64])), ready)

        @block.scalar
        def _(act):
            for w in range(2):
                act.wait_ge(reduced.sem, w + 1)
                post(act, act.activation(trig[:, w], red[:, w], ACT.Sin), trig_ok)
            m.on_scalar(act, steps[:2])
            act.wait_ge(summed.sem, 1)
            post(act, act.activation(rstd[:], ssum[:], ACT.Sqrt, bias=k.const("eps"), scale=1.0 / P), rooted)
            m.on_scalar(act, steps[2:])
            for n, dst in enumerate([t.qT[:, h, :] for h in range(AH)] + [t.kT[:, h, :] for h in range(AKV)]
                                    + [t.qiT[:, h, :] for h in range(2)] + [t.kiT[:]]):
                act.wait_ge(turned, n + 1)
                post(act, act.activation(dst, k.bank[n % 8][:], ACT.Copy), k.astep)
                if n == 0:
                    t.turn_base = k.astep.n - 1

        @block.tensor
        def _(pe):
            srcs = [t.q[:, :, h * P:(h + 1) * P] for h in range(AH)]
            srcs += [t.kv[:, :, h * P:(h + 1) * P] for h in range(AKV)]
            srcs += [t.ix[:, :, h * P:(h + 1) * P] for h in range(2)]
            srcs += [kdup[:].rearrange("p t a d -> p t (a d)")]
            m.on_tensor(pe, steps[:2])
            m.on_tensor(pe, steps[2:])
            pe.wait_ge(ready.sem, 1)
            pe.wait_ge(m.columns_in, steps[-1] + 1)
            for n, src in enumerate(srcs):
                if n >= 8:
                    pe.wait_ge(k.astep.sem, t.turn_base + n - 7)
                for i in range(NT):
                    last = pe.transpose(k.bank[n % 8][:, i * P:(i + 1) * P], src[:, i, :], k.const("ident"))
                last.then_inc(turned, 1)


def selection_stage(k, t):
    nc = k.nc
    with ExitStack() as ctx:
        def sb(name, shape):
            return ctx.enter_context(nc.sbuf_tensor(name, shape, F32))

        relu = sb("relu_logits", [P, IH, T])
        score = sb("index_scores", [P, T])
        work = sb("scores_left", [P, T])
        m8 = sb("best8", [P, 8])
        eq = sb("tied", [P, T])
        seen = sb("ties_so_far", [P, T])
        need = sb("ties_to_keep", [P, 1])
        ones = sb("ones_wide", [P, T])
        m = k.modulation
        m.rows_buffer(ctx, "mod2_rows_b")
        first = len(m.gs[0]) + len(m.gs[1]) // 2
        steps = [range(first + 2 * i, first + 2 * i + 2) for i in range(3)]
        spread = ctx.enter_context(nc.semaphore("gate2_spread"))
        logits = ctx.enter_context(nc.semaphore("index_logits"))
        rect = Signal(ctx, nc, "index_relu")
        summed = Signal(ctx, nc, "index_scores_summed")
        block = ctx.enter_context(nc.Block())

        @block.sync
        def _(sp):
            k.stream(sp, m.gs[1][-1])

        @block.tensor
        def _(pe):
            for i in range(1, NT):
                w = (i + 1) * P
                if i > 1:
                    pe.wait_ge(rect.sem, IH * (i - 1))
                for h in range(IH):
                    p0 = 64 * (h % 2)
                    pe.matmul(k.bank[h][:, 0:w], t.qiT[p0:p0 + 64, h // 2, i * P:(i + 1) * P],
                              t.kiT[p0:p0 + 64, 0:w], start=True, stop=True).then_inc(logits, 1)
                m.on_tensor(pe, steps[i - 1])
            for half in range(2):
                last = pe.matmul(k.bank[4 + 2 * half][:], k.const("ones", P, 1), m.rows[:, half, :],
                                 start=True, stop=True)
            last.then_inc(spread, 1)

        @block.scalar
        def _(act):
            for i in range(1, NT):
                w = (i + 1) * P
                if i > 1:
                    act.wait_ge(summed.sem, i - 1)
                for h in range(IH):
                    act.wait_ge(logits, IH * (i - 1) + h + 1)
                    post(act, act.activation(relu[:, h, 0:w], k.bank[h][:, 0:w], ACT.Relu), rect)
                m.on_scalar(act, steps[i - 1])

        @block.vector
        def _(dve):
            def v(ins):
                post(dve, ins, k.vstep)

            v(dve.memset(ones[:], 1.0))
            v(dve.memset(t.madd[:], NEG))
            v(dve.tensor_copy(t.madd[:, 0, 0:P], k.const("causal_add")))
            for i in range(1, NT):
                w = (i + 1) * P
                for h in range(IH):
                    dve.wait_ge(rect.sem, IH * (i - 1) + h + 1)
                    wh = t.ix[:, i, 320 + h:321 + h]
                    if h == 0:
                        v(dve.tensor_scalar(score[:, 0:w], relu[:, h, 0:w], wh, None, ALU.mult))
                    else:
                        ins = dve.scalar_tensor_tensor(score[:, 0:w], relu[:, h, 0:w], wh, score[:, 0:w],
                                                       ALU.mult, ALU.add)
                        post(dve, ins, summed if h == IH - 1 else k.vstep)
                v(dve.tensor_tensor(score[:, w - P:w], score[:, w - P:w], k.const("causal_add"), ALU.add))
                for r in range(TOPK // 8):
                    src = score if r == 0 else work
                    v(dve.max(m8[:], src[:, 0:w]))
                    if r < TOPK // 8 - 1:
                        v(dve.match_replace(work[:, 0:w], m8[:], src[:, 0:w], -3.0e38))
                keep = t.madd[:, i, 0:w]
                v(dve.tensor_scalar(eq[:, 0:w], score[:, 0:w], m8[:, 7:8], None, ALU.is_equal))
                v(dve.tensor_scalar(keep, score[:, 0:w], m8[:, 7:8], None, ALU.is_gt))
                v(dve.tensor_reduce(need[:], keep, AX, ALU.add))
                v(dve.tensor_scalar(need[:], need[:], -1.0, float(TOPK), ALU.mult, ALU.add))
                v(dve.tensor_tensor_scan(seen[:, 0:w], ones[:, 0:w], eq[:, 0:w], 0.0, ALU.mult, ALU.add))
                v(dve.scalar_tensor_tensor(eq[:, 0:w], seen[:, 0:w], need[:], eq[:, 0:w], ALU.is_le, ALU.mult))
                v(dve.tensor_tensor(keep, keep, eq[:, 0:w], ALU.add))
                v(dve.tensor_scalar(keep, keep, 1.0, -NEG, ALU.subtract, ALU.mult))
            dve.wait_ge(m.columns_in, len(m.steps))
            v(dve.tensor_tensor(k.mod2[:], k.mod2[:], k.col("b_ada_2", 0, 48), ALU.add))
            dve.wait_ge(spread, 1)
            at, _w = ROW_AT["gate2_b"]
            for half in range(2):
                v(dve.tensor_tensor(k.gate2[:, half * 512:(half + 1) * 512], k.bank[4 + 2 * half][:],
                                    k.rows[:, at + half * 512:at + (half + 1) * 512], ALU.add))


def attention_stage(k, t):
    nc = k.nc
    scale = float(P) ** -0.5
    with ExitStack() as ctx:
        def sb(name, shape):
            return ctx.enter_context(nc.sbuf_tensor(name, shape, F32))

        s_at, p_at = [0, P, 3 * P, 6 * P], [0, 4 * P, 7 * P, 9 * P]
        s = sb("scores", [P, 2, 10 * P])
        pT = sb("probsT", [P, 2, 10 * P])
        top = sb("row_top", [P, 2, NT])
        den = sb("row_sum", [P, 2, NT])
        scored = ctx.enter_context(nc.semaphore("scores_made"))
        read = Signal(ctx, nc, "scores_read")
        topped = Signal(ctx, nc, "row_tops")
        exped = Signal(ctx, nc, "exps_made")
        normed = Signal(ctx, nc, "probs_normed")
        flipped = ctx.enter_context(nc.semaphore("probs_flipped"))
        copied = Signal(ctx, nc, "probsT_copied")
        valued = ctx.enter_context(nc.semaphore("values_mixed"))
        gated = Signal(ctx, nc, "outputs_gated")
        block = ctx.enter_context(nc.Block())
        place = [(4, 0), (5, 0), (6, 0), (6, 256)]

        @block.tensor
        def _(pe):
            def scores(h):
                for i in range(NT):
                    if h > 0:
                        pe.wait_ge(read.sem, NT * (h - 1) + i + 1)
                    w = (i + 1) * P
                    pe.matmul(k.bank[i][:, 0:w], t.qT[:, h, i * P:w], t.kT[:, h // 4, 0:w],
                              start=True, stop=True).then_inc(scored, 1)

            scores(0)
            for h in range(AH):
                if h + 1 < AH:
                    scores(h + 1)
                for i in range(NT):
                    pe.wait_ge(normed.sem, NT * h + i + 1)
                    if h > 0 and i == 0:
                        pe.wait_ge(copied.sem, NT * h)
                    for j in range(i + 1):
                        b, c = place[j]
                        c += (i - j) * P
                        last = pe.transpose(k.bank[b][:, c:c + P], s[:, h % 2, s_at[i] + j * P:s_at[i] + (j + 1) * P], k.const("ident"))
                last.then_inc(flipped, 1)
                if h > 0:
                    pe.wait_ge(gated.sem, h)
                for j in range(NT):
                    pe.wait_ge(copied.sem, NT * h + j + 1)
                    v = t.kv[:, j, 256 + (h // 4) * P:256 + (h // 4 + 1) * P]
                    last = pe.matmul(k.bank[7][:, j * P:T], v, pT[:, h % 2, p_at[j]:p_at[j] + T - j * P], start=(j == 0), stop=(j == NT - 1))
                last.then_inc(valued, 1)

        @block.vector
        def _(dve):
            def softmax_in(h):
                for i in range(NT):
                    w = (i + 1) * P
                    dve.wait_ge(scored, NT * h + i + 1)
                    if h >= 2:
                        dve.wait_ge(flipped, h - 1)
                    post(dve, dve.scalar_tensor_tensor(s[:, h % 2, s_at[i]:s_at[i] + w], k.bank[i][:, 0:w], scale,
                                                       t.madd[:, i, 0:w], ALU.mult, ALU.add), read)
                    post(dve, dve.tensor_reduce(top[:, h % 2, i:i + 1], s[:, h % 2, s_at[i]:s_at[i] + w], AX, ALU.max, negate=True), topped)

            def softmax_out(h):
                dve.wait_ge(exped.sem, NT * (h + 1))
                post(dve, dve.reciprocal(den[:, h % 2, :], den[:, h % 2, :]), k.vstep)
                for i in range(NT):
                    w = (i + 1) * P
                    post(dve, dve.tensor_scalar(s[:, h % 2, s_at[i]:s_at[i] + w], s[:, h % 2, s_at[i]:s_at[i] + w], den[:, h % 2, i:i + 1],
                                                None, ALU.mult), normed)

            def gate(h):
                dve.wait_ge(valued, h + 1)
                post(dve, dve.tensor_tensor(t.oT[:, h, :], k.bank[7][:], t.zT[:, h, :], ALU.mult), gated)

            softmax_in(0)
            for h in range(AH):
                if h + 1 < AH:
                    softmax_in(h + 1)
                softmax_out(h)
                if h > 0:
                    gate(h - 1)
            gate(AH - 1)

        @block.scalar
        def _(act):
            def exps(h):
                for i in range(NT):
                    w = (i + 1) * P
                    act.wait_ge(topped.sem, NT * h + i + 1)
                    if h >= 2 and i == 0:
                        act.wait_ge(normed.sem, NT * (h - 1))
                    post(act, act.activation(s[:, h % 2, s_at[i]:s_at[i] + w], s[:, h % 2, s_at[i]:s_at[i] + w], ACT.Exp,
                                             bias=top[:, h % 2, i:i + 1], accum_out=den[:, h % 2, i:i + 1]), exped)

            exps(0)
            for h in range(AH):
                if h + 1 < AH:
                    exps(h + 1)
                act.wait_ge(flipped, h + 1)
                if h >= 2:
                    act.wait_ge(valued, h - 1)
                for j in range(NT):
                    b, c = place[j]
                    post(act, act.activation(pT[:, h % 2, p_at[j]:p_at[j] + T - j * P], k.bank[b][:, c:c + T - j * P], ACT.Copy), copied)


def attention_out_stage(k, t):
    nc = k.nc
    with ExitStack() as ctx:
        plan = columns(find(k, "w_in", GA0, 1024), k.hT) + columns(find(k, "w_branch_att", 0, 1024), t.oT)
        pj = Projection(k, ctx, "attention_out", plan)
        gated = Signal(ctx, nc, "attention_gates")
        block = ctx.enter_context(nc.Block())

        @block.sync
        def _(sp):
            k.stream(sp, plan[-1][1][-1])

        @block.tensor
        def _(pe):
            pj.run(pe)

        @block.scalar
        def _(act):
            for j in range(8):
                bank = pj.next(act)
                post(act, act.activation(t.merged[:, j, :], bank[:], ACT.Sigmoid), pj.freed)

        @block.vector
        def _(dve):
            pj.taken = 8
            dve.wait_ge(pj.freed.sem, 8)
            for j in range(8):
                bank = pj.next(dve)
                post(dve, dve.tensor_tensor(t.merged[:, j, :], bank[:], t.merged[:, j, :], ALU.mult), pj.freed)


class Part:
    pass


def attention_branch(k):
    with ExitStack() as ctx:
        def sb(name, shape):
            return ctx.enter_context(k.nc.sbuf_tensor(name, shape, F32))

        t = Part()
        t.merged = k.merged
        t.zT = sb("silu_zT", [P, 8, T])
        t.kv = sb("k_v_rows", [P, NT, 512])
        t.ix = sb("index_rows", [P, NT, IDX_COLS])
        t.kT, t.qiT, t.kiT = sb("kT", [P, AKV, T]), sb("index_qT", [P, 2, T]), sb("index_kT", [P, T])
        t.qT = sb("qT", [P, AH, T])
        with k.nc.sbuf_tensor("q_rows", [P, NT, D], F32) as t.q:
            attention_projection_stage(k, t)
            attention_rotary_stage(k, t)
        t.madd = sb("selected_add", [P, NT, T])
        selection_stage(k, t)
        t.oT = t.zT
        attention_stage(k, t)
        attention_out_stage(k, t)


def ssm_projection_stage(k, t):
    nc = k.nc
    with ExitStack() as ctx:
        def sb(name, shape):
            return ctx.enter_context(nc.sbuf_tensor(name, shape, F32))

        neg = sb("minus_abs", [SH, T])
        e = sb("exp_minus_abs", [SH, T])
        u = sb("one_plus_exp", [SH, T])
        ln = sb("log_one_plus", [SH, T])
        a_neg = sb("exp_a_log", [SH, 1])
        ones = sb("ones_row", [SH, P])
        dt_plan = columns(find(k, "w_in", DT0, 32), k.hT)
        plan = columns(find(k, "w_in", XBC0, 3072), k.hT) + dt_plan
        pj = Projection(k, ctx, "ssm_in", plan)
        first_tap = Signal(ctx, nc, "conv_first_tap")
        convolved = Signal(ctx, nc, "convolved")
        absed = Signal(ctx, nc, "dt_minus_abs")
        exped = Signal(ctx, nc, "dt_exps")
        summed = Signal(ctx, nc, "dt_one_plus")
        logged = Signal(ctx, nc, "dt_logs")
        block = ctx.enter_context(nc.Block())

        @block.sync
        def _(sp):
            k.stream(sp, plan[-1][1][-1])

        @block.tensor
        def _(pe):
            pj.run(pe)

        @block.scalar
        def _(act):
            post(act, act.activation(a_neg[:], k.col("a_log", 0, 1, SH), ACT.Exp), k.astep)
            a_done = k.astep.n
            t.a_done = a_done
            for j in range(24):
                sem, value = pj.there[j]
                act.wait_ge(sem, value)
                post(act, act.activation(t.xbcT[:, j, :], k.bank[j % 8][:], ACT.Identity,
                                         bias=k.col("conv_b", j), scale=k.col("conv_w", 3 * 24 + j)), first_tap)
                if j > 0:
                    act.wait_ge(convolved.sem, j)
                    post(act, act.activation(t.xbcT[:, j - 1, :], t.xbcT[:, j - 1, :], ACT.Silu), k.astep)
            act.wait_ge(convolved.sem, 24)
            post(act, act.activation(t.xbcT[:, 23, :], t.xbcT[:, 23, :], ACT.Silu), k.astep)
            act.wait_ge(absed.sem, 1)
            post(act, act.activation(e[:], neg[:], ACT.Exp), exped)
            act.wait_ge(summed.sem, 1)
            post(act, act.activation(ln[:], u[:], ACT.Ln), logged)

        @block.vector
        def _(dve):
            def v(ins):
                post(dve, ins, k.vstep)

            v(dve.memset(ones[:], 1.0))
            for j in range(24):
                bank = pj.next(dve)
                dve.wait_ge(first_tap.sem, j + 1)
                for back in (1, 2, 3):
                    ins = dve.scalar_tensor_tensor(t.xbcT[:, j, back:T], bank[:, 0:T - back],
                                                   k.col("conv_w", (3 - back) * 24 + j), t.xbcT[:, j, back:T],
                                                   ALU.mult, ALU.add)
                    post(dve, ins, convolved if back == 3 else k.vstep)
                dve.sem_inc(pj.freed.sem, 1)
                pj.freed.n += 1
            bank = pj.next(dve)
            v(dve.tensor_scalar(t.dtT[:], bank[0:SH, :], k.col("dt_bias", 0, 1, SH), None, ALU.add))
            v(dve.tensor_scalar(neg[:], t.dtT[:], -1.0, None, ALU.mult))
            post(dve, dve.tensor_tensor(neg[:], neg[:], t.dtT[:], ALU.min), absed)
            dve.wait_ge(exped.sem, 1)
            post(dve, dve.tensor_scalar(u[:], e[:], 1.0, None, ALU.add), summed)
            v(dve.scalar_tensor_tensor(e[:], u[:], -1.0, e[:], ALU.add, ALU.subtract))
            v(dve.reciprocal(neg[:], u[:]))
            v(dve.scalar_tensor_tensor(e[:], e[:], -1.0, neg[:], ALU.mult, ALU.mult))
            dve.wait_ge(logged.sem, 1)
            v(dve.tensor_tensor(e[:], e[:], ln[:], ALU.add))
            v(dve.scalar_tensor_tensor(t.dtT[:], t.dtT[:], 0.0, e[:], ALU.max, ALU.add))
            dve.wait_ge(k.astep.sem, t.a_done)
            v(dve.tensor_scalar(e[:], t.dtT[:], a_neg[:], -1.0, ALU.mult, ALU.mult))
            for c in range(NT):
                cs = slice(c * P, (c + 1) * P)
                v(dve.tensor_tensor_scan(t.acumT[:, cs], ones[:], e[:, cs], 0.0, ALU.mult, ALU.add))


def ssd_stage(k, t):
    nc = k.nc
    HG = SH // SG
    with ExitStack() as ctx:
        def sb(name, shape):
            return ctx.enter_context(nc.sbuf_tensor(name, shape, F32))

        z = sb("silu_z_rows", [P, NT, 512])
        dt_row = sb("dt_rows", [P, NT, SH])
        ac_row = sb("acum_rows", [P, NT, SH])
        ea_row = sb("exp_acum_rows", [P, NT, SH])
        xs = sb("xs_rows", [P, 512])
        cbm = sb("cb_causal", [P, P])
        squares = ctx.enter_context(nc.sbuf_tensor("y_squares", [P, 512], mybir.dt.bfloat16))
        state = sb("state", [P, HG, SP_])
        b_row = sb("b_rows", [P, 2, P])
        xdt = sb("xs_dt", [P, 2, HG, SP_])
        xdec = sb("xs_dt_decay", [P, 2, HG, SP_])
        skip = sb("xs_skip", [P, HG, SP_])
        dec = sb("decay", [P, 2, HG, P])
        ends = sb("end_decays", [P, 2, 2, HG])
        y = sb("y_rows", [P, 2, 512])
        ss = sb("group_squares", [P, 2])
        diag = sb("rstd_diagonal", [P, 2, P])
        plan = token_rows(find(k, "w_in", ZS0, 2048), k.hT)
        pj = Projection(k, ctx, "ssm_z", plan, banks=(2, 3, 6, 7))
        smalls = ctx.enter_context(nc.semaphore("dt_acum_turned"))
        small_in = Signal(ctx, nc, "dt_acum_rows")
        turned = ctx.enter_context(nc.semaphore("unit_turned"))
        bcast = ctx.enter_context(nc.semaphore("acum_spread"))
        rows_in = Signal(ctx, nc, "unit_rows")
        subbed = Signal(ctx, nc, "decay_exponents")
        exped = Signal(ctx, nc, "decays_made")
        scaled = Signal(ctx, nc, "xs_scaled")
        weighted = Signal(ctx, nc, "decay_weighted")
        side = Signal(ctx, nc, "skip_and_decayed")
        multiplied = ctx.enter_context(nc.semaphore("unit_products"))
        faded = Signal(ctx, nc, "state_faded")
        stated = Signal(ctx, nc, "state_updated")
        summed = Signal(ctx, nc, "unit_summed")
        gated = Signal(ctx, nc, "unit_gated")
        rooted = Signal(ctx, nc, "unit_root")
        normed = Signal(ctx, nc, "unit_rstd_diagonal")
        back = ctx.enter_context(nc.semaphore("unit_turned_back"))
        stored = Signal(ctx, nc, "unit_stored")
        block = ctx.enter_context(nc.Block())
        units = [(g, c) for g in range(SG) for c in range(NT)]
        last_unit = len(units) - 1
        full, tall = [P, HG, P], [P, HG, SP_]

        def fades(n):
            return n + 1 - (n + 1) // NT


        @block.sync
        def _(sp):
            k.stream(sp, plan[-1][1][-1])

        @block.tensor
        def _(pe):
            def front(n):
                g, c = units[n]
                cs = slice(c * P, (c + 1) * P)
                if n > 0:
                    pe.wait_ge(weighted.sem, n)
                for h in range(HG):
                    sel = k.const("ident", SH, SH)[:, g * HG + h:g * HG + h + 1].broadcast_to([SH, P])
                    last = pe.matmul(k.bank[4 + h // 4][:, (h % 4) * P:(h % 4 + 1) * P], sel, t.acumT[:, cs],
                                     start=True, stop=True)
                last.then_inc(bcast, 1)
                for j in range(4):
                    pe.transpose(k.bank[0][:, j * P:(j + 1) * P], t.xbcT[:, 4 * g + j, cs], k.const("ident"))
                pe.transpose(k.bank[1][:, 0:P], t.xbcT[:, 16 + g, cs], k.const("ident"))
                pe.matmul(k.bank[1][:, P:2 * P], t.xbcT[:, 16 + g, cs], t.xbcT[:, 20 + g, cs],
                          start=True, stop=True).then_inc(turned, 1)

            def products(n):
                g, c = units[n]
                i = n % 2
                pe.wait_ge(weighted.sem, n + 1)
                pe.wait_ge(side.sem, n + 1)
                if n > 0:
                    pe.wait_ge(summed.sem, n)
                    pe.wait_ge(stated.sem, n)
                pe.wait_ge(pj.freed.sem, 4 * (g + 1))
                for h in range(HG):
                    out = k.bank[2][:, h * SP_:(h + 1) * SP_]
                    pe.matmul(out, dec[:, i, h, :], xdt[:, i, h, :], start=True, stop=False)
                    pe.matmul(out, k.const("ident"), skip[:, h, :], start=False, stop=True)
                pe.matmul(k.bank[3][:], t.xbcT[:, 20 + g, c * P:(c + 1) * P], state[:].rearrange("p h d -> p (h d)"),
                          start=True, stop=True)
                pe.matmul(k.bank[6][:], b_row[:, i, :], xdec[:, i].rearrange("p h d -> p (h d)"),
                          start=True, stop=True).then_inc(multiplied, 1)

            def turn_back(n):
                pe.wait_ge(normed.sem, n + 1)
                if n > 0:
                    pe.wait_ge(stored.sem, n)
                pe.wait_ge(pj.freed.sem, pj.made)
                for j in range(4):
                    last = pe.matmul(k.bank[7][:, j * P:(j + 1) * P], y[:, n % 2, j * P:(j + 1) * P],
                                     diag[:, n % 2, :], start=True, stop=True)
                last.then_inc(back, 1)

            for c in range(NT):
                pe.transpose(k.bank[4][:, c * 64:c * 64 + SH], t.dtT[:, c * P:(c + 1) * P], k.const("ident", SH, SH))
                last = pe.transpose(k.bank[4][:, c * 64 + SH:c * 64 + 64], t.acumT[:, c * P:(c + 1) * P],
                                    k.const("ident", SH, SH))
            last.then_inc(smalls, 1)
            pe.wait_ge(small_in.sem, 2)
            front(0)
            pj.run(pe, slice(0, 1))
            for n, (g, c) in enumerate(units):
                if n < last_unit:
                    front(n + 1)
                products(n)
                if n > 1:
                    turn_back(n - 2)
                if c == NT - 1 and n < last_unit:
                    pe.wait_ge(summed.sem, n + 1)
                    pe.wait_ge(stated.sem, n + 1)
                    pe.wait_ge(stored.sem, n - 1)
                    pj.run(pe, slice(g + 1, g + 2))
            turn_back(last_unit - 1)
            turn_back(last_unit)

        @block.scalar
        def _(act):
            def a(ins):
                post(act, ins, k.astep)

            def silu_z(g):
                for i in range(NT):
                    bank = pj.next(act)
                    if g > 0 and i == 0:
                        act.wait_ge(gated.sem, 4 * g)
                    post(act, act.activation(z[:, i, :], bank[:], ACT.Silu), pj.freed)

            def front(n):
                act.wait_ge(turned, n + 1)
                if n > 1:
                    act.wait_ge(multiplied, n - 1)
                a(act.activation(b_row[:, n % 2, :], k.bank[1][:, 0:P], ACT.Copy))
                if n > 0:
                    act.wait_ge(side.sem, n)
                post(act, act.activation(xs[:], k.bank[0][:], ACT.Copy), rows_in)
                act.wait_ge(subbed.sem, n + 1)
                a(act.activation(ends[:, n % 2], ends[:, n % 2], ACT.Exp))
                post(act, act.activation(dec[:, n % 2], dec[:, n % 2], ACT.Exp), exped)

            def root(n):
                act.wait_ge(gated.sem, n + 1)
                if n > 1:
                    act.wait_ge(normed.sem, n - 1)
                mine = ss[:, n % 2:n % 2 + 1]
                a(act.activation(squares[:], y[:, n % 2, :], ACT.Square, accum_out=mine))
                a(act.activation(mine, mine, ACT.Ln, bias=k.const("eps"), scale=1.0 / 512))
                post(act, act.activation(mine, mine, ACT.Exp, scale=-0.5), rooted)

            def store(n):
                g, c = units[n]
                act.wait_ge(back, n + 1)
                for j in range(4):
                    ins = act.activation(t.xbcT[:, 4 * g + j, c * P:(c + 1) * P], k.bank[7][:, j * P:(j + 1) * P],
                                         ACT.Copy, scale=k.col("ssm_norm_g", 4 * g + j))
                    if j == 3:
                        post(act, ins, stored)

            act.wait_ge(smalls, 1)
            v4 = k.bank[4][:, 0:256].rearrange("p (c x) -> p c x", c=NT)
            a(act.activation(dt_row[:], v4[:, :, 0:SH], ACT.Copy))
            post(act, act.activation(ac_row[:], v4[:, :, SH:64], ACT.Copy), small_in)
            post(act, act.activation(ea_row[:], v4[:, :, SH:64], ACT.Exp), small_in)
            front(0)
            silu_z(0)
            for n, (g, c) in enumerate(units):
                if n < last_unit:
                    front(n + 1)
                if n > 0:
                    root(n - 1)
                if n > 1:
                    store(n - 2)
                if c == NT - 1 and n < last_unit:
                    silu_z(g + 1)
            root(last_unit)
            store(last_unit - 1)
            store(last_unit)

        @block.vector
        def _(dve):
            def v(ins):
                post(dve, ins, k.vstep)

            def front(n):
                g, c = units[n]
                i, hs = n % 2, slice(g * HG, (g + 1) * HG)
                dve.wait_ge(bcast, n + 1)
                if n > 1:
                    dve.wait_ge(multiplied, n - 1)
                    dve.wait_ge(faded.sem, fades(n - 2))
                spread = [k.bank[4 + b][:].rearrange("p (h l) -> p h l", h=4) for b in range(2)]
                for b in range(2):
                    last = dve.tensor_copy(ends[:, i, 1, 4 * b:4 * b + 4], spread[b][:, :, P - 1])
                v(last)
                v(dve.tensor_tensor(ends[:, i, 0, :], ends[:, i, 1, :], ac_row[:, c, hs], ALU.subtract))
                for h in range(HG):
                    last = dve.tensor_scalar(dec[:, i, h, :], spread[h // 4][:, h % 4, :],
                                             ac_row[:, c, g * HG + h:g * HG + h + 1], 0.0, ALU.subtract, ALU.min)
                post(dve, last, subbed)
                dve.wait_ge(rows_in.sem, n + 1)
                dve.tensor_tensor(cbm[:], k.bank[1][:, P:2 * P], k.const("s_le_l"), ALU.mult)
                x3 = xs[:].rearrange("p (h d) -> p h d", h=HG)
                post(dve, dve.tensor_tensor(xdt[:, i], x3, bc(dt_row[:, c, hs], 2, tall), ALU.mult), scaled)
                dve.wait_ge(exped.sem, n + 1)
                post(dve, dve.tensor_tensor(dec[:, i], dec[:, i], bc(cbm[:], 1, full), ALU.mult), weighted)

            def sums(n):
                g, c = units[n]
                dve.wait_ge(multiplied, n + 1)
                if c == NT - 1:
                    post(dve, dve.memset(state[:], 0.0), stated)
                else:
                    dve.wait_ge(faded.sem, fades(n))
                    s3 = k.bank[6][:].rearrange("p (h d) -> p h d", h=HG)
                    post(dve, dve.tensor_tensor(state[:], state[:], s3, ALU.add), stated)
                if n > 1:
                    dve.wait_ge(back, n - 1)
                off = k.bank[3][:].rearrange("p (h d) -> p h d", h=HG)
                y3 = y[:, n % 2].rearrange("p (h d) -> p h d", h=HG)
                v(dve.tensor_tensor(y3, off, bc(ea_row[:, c, g * HG:(g + 1) * HG], 2, tall), ALU.mult))
                post(dve, dve.tensor_tensor(y[:, n % 2], y[:, n % 2], k.bank[2][:], ALU.add), summed)

            def norm(n):
                dve.wait_ge(rooted.sem, n + 1)
                if n > 1:
                    dve.wait_ge(back, n - 1)
                post(dve, dve.tensor_scalar(diag[:, n % 2, :], k.const("ident"), ss[:, n % 2:n % 2 + 1], None,
                                            ALU.mult), normed)

            dve.wait_ge(small_in.sem, 2)
            v(dve.memset(state[:], 0.0))
            front(0)
            for n in range(len(units)):
                if n < last_unit:
                    front(n + 1)
                sums(n)
                if n > 0:
                    norm(n - 1)
            norm(last_unit)

        @block.gpsimd
        def _(pool):
            def p(ins):
                post(pool, ins, k.gstep)

            def front(n):
                g, c = units[n]
                i, hs = n % 2, slice(g * HG, (g + 1) * HG)
                pool.wait_ge(rows_in.sem, n + 1)
                if n > 0:
                    pool.wait_ge(multiplied, n)
                x3 = xs[:].rearrange("p (h d) -> p h d", h=HG)
                pool.tensor_tensor(skip[:], x3, bc(k.row("d_skip")[:, hs], 2, tall), ALU.mult)
                pool.wait_ge(scaled.sem, n + 1)
                pool.wait_ge(exped.sem, n + 1)
                post(pool, pool.tensor_tensor(xdec[:, i], xdt[:, i], bc(ends[:, i, 0, :], 2, tall), ALU.mult), side)

            def fade(n):
                pool.wait_ge(multiplied, n + 1)
                if n > 0:
                    pool.wait_ge(stated.sem, n)
                post(pool, pool.tensor_tensor(state[:], state[:], bc(ends[:, n % 2, 1, :], 2, tall), ALU.mult), faded)

            def gate(n):
                pool.wait_ge(summed.sem, n + 1)
                pool.wait_ge(pj.freed.sem, 4 * (units[n][0] + 1))
                post(pool, pool.tensor_tensor(y[:, n % 2], y[:, n % 2], z[:, units[n][1], :], ALU.mult), gated)

            front(0)
            for n in range(len(units)):
                if n < last_unit:
                    front(n + 1)
                if units[n][1] < NT - 1:
                    fade(n)
                gate(n)


def ssm_out_stage(k, t):
    nc = k.nc
    with ExitStack() as ctx:
        sig = ctx.enter_context(nc.sbuf_tensor("ssm_gate", [P, 8, T], F32))
        term = ctx.enter_context(nc.sbuf_tensor("ssm_term", [P, T], F32))
        plan = columns(find(k, "w_in", GS0, 1024), k.hT)
        for c in (0, 512):
            pair = (find(k, "w_branch_ssm", c, 512)[0], find(k, "w_branch_ssm", c, 512, D)[0])
            plan.append(("columns", pair, t.xbcT, None))
        n_branch = len(plan)
        plan += columns(find(k, "w_out", 0, 1024), k.merged)
        pj = Projection(k, ctx, "ssm_out", plan)
        merged = Signal(ctx, nc, "branches_merged")
        block = ctx.enter_context(nc.Block())

        @block.sync
        def _(sp):
            k.stream(sp, plan[-1][1][-1])

        @block.tensor
        def _(pe):
            pj.run(pe, slice(0, n_branch))
            pe.wait_ge(merged.sem, 8)
            pj.run(pe, slice(n_branch, None))

        @block.scalar
        def _(act):
            for j in range(8):
                bank = pj.next(act)
                post(act, act.activation(sig[:, j, :], bank[:], ACT.Sigmoid), pj.freed)

        @block.vector
        def _(dve):
            dve.wait_ge(pj.freed.sem, 8)
            for j in range(8):
                bank = pj.next(dve)
                post(dve, dve.tensor_tensor(term[:], bank[:], sig[:, j, :], ALU.mult), pj.freed)
                post(dve, dve.tensor_tensor(k.merged[:, j, :], k.merged[:, j, :], term[:], ALU.add), merged)
            for j in range(8):
                bank = pj.next(dve)
                post(dve, dve.scalar_tensor_tensor(k.xT[:, j, :], bank[:], k.mod1[:, 16 + j:17 + j], k.xT[:, j, :],
                                                   ALU.mult, ALU.add), pj.freed)


def ssm_branch(k):
    with ExitStack() as ctx:
        def sb(name, shape):
            return ctx.enter_context(k.nc.sbuf_tensor(name, shape, F32))

        t = Part()
        t.xbcT = sb("xbcT", [P, 24, T])
        t.dtT, t.acumT = sb("dtT", [SH, T]), sb("acumT", [SH, T])
        ssm_projection_stage(k, t)
        ssd_stage(k, t)
        ssm_out_stage(k, t)


def second_projection_stage(k, t):
    nc = k.nc
    with ExitStack() as ctx:
        def sb(name, shape):
            return ctx.enter_context(nc.sbuf_tensor(name, shape, F32))

        xa = sb("a_raw", [DH, T])
        neg = sb("a_minus_abs", [DH, T])
        e = sb("a_exp_minus_abs", [DH, T])
        u = sb("a_one_plus_exp", [DH, T])
        ln = sb("a_log_one_plus", [DH, T])
        a_neg = sb("dn_exp_a_log", [DH, 1])
        ones = sb("dn_ones_row", [DH, CH])
        raw = sb("conv_raw", [P, 2, T])
        ba = find(k, "w_in_2", BA0, 8)[0]
        plan = token_rows(find(k, "w_in_2", QA0, 512) + find(k, "w_in_2", KA0, 512) + find(k, "w_in_2", VA0, 512), k.hT)
        plan += columns(find(k, "w_in_2", QKV0, 1536), k.hT) + token_rows(find(k, "w_in_2", ZB0, 512), k.hT)
        pj = Projection(k, ctx, "second_in", plan)
        tapped = Signal(ctx, nc, "dn_first_tap")
        convolved = Signal(ctx, nc, "dn_convolved")
        gates_made = ctx.enter_context(nc.semaphore("dn_gate_products"))
        absed = Signal(ctx, nc, "a_minus_abs_ready")
        exped = Signal(ctx, nc, "a_exps")
        summed = Signal(ctx, nc, "a_one_plus")
        logged = Signal(ctx, nc, "a_logs")
        sig_ok = Signal(ctx, nc, "beta_ready")
        block = ctx.enter_context(nc.Block())

        @block.sync
        def _(sp):
            k.stream(sp, ba)

        @block.tensor
        def _(pe):
            pj.run(pe)
            w = k.take(pe, ba)
            pe.wait_ge(pj.freed.sem, 28)
            for which in range(2):
                for kk in range(KD):
                    last = pe.matmul(k.bank[which][0:DH, :], w[:, kk, which * DH:(which + 1) * DH], k.hT[:, kk, :],
                                     start=(kk == 0), stop=(kk == KD - 1))
                last.then_inc(gates_made if which == 0 else k.used.sem, 1)
            k.used.n += 1

        @block.scalar
        def _(act):
            for dst in (t.qa, t.ka, t.va):
                for i in range(NT):
                    bank = pj.next(act)
                    post(act, act.activation(dst[:, i, :], bank[:], ACT.Copy), pj.freed)
            for j in range(12):
                bank = pj.next(act)
                if j >= 2:
                    act.wait_ge(convolved.sem, j - 1)
                post(act, act.activation(raw[:, j % 2, :], bank[:], ACT.Copy), pj.freed)
                post(act, act.activation(t.dT[:, j, :], raw[:, j % 2, :], ACT.Copy,
                                         scale=k.col("dn_conv_w_2", 3 * 12 + j)), tapped)
                if j > 0:
                    act.wait_ge(convolved.sem, j)
                    post(act, act.activation(t.dT[:, j - 1, :], t.dT[:, j - 1, :], ACT.Silu), k.astep)
            act.wait_ge(convolved.sem, 12)
            post(act, act.activation(t.dT[:, 11, :], t.dT[:, 11, :], ACT.Silu), k.astep)
            for i in range(NT):
                bank = pj.next(act)
                post(act, act.activation(t.zb[:, i, :], bank[:], ACT.Silu), pj.freed)
            act.wait_ge(gates_made, 1)
            post(act, act.activation(t.betaT[:], k.bank[0][0:DH, :], ACT.Sigmoid), k.astep)
            post(act, act.activation(a_neg[:], k.col("dn_a_log_2", 0, 1, DH), ACT.Exp), sig_ok)
            act.wait_ge(absed.sem, 1)
            post(act, act.activation(e[:], neg[:], ACT.Exp), exped)
            act.wait_ge(summed.sem, 1)
            post(act, act.activation(ln[:], u[:], ACT.Ln), logged)

        @block.vector
        def _(dve):
            def v(ins):
                post(dve, ins, k.vstep)

            v(dve.memset(ones[:], 1.0))
            for j in range(12):
                dve.wait_ge(tapped.sem, j + 1)
                for b in (1, 2, 3):
                    ins = dve.scalar_tensor_tensor(t.dT[:, j, b:T], raw[:, j % 2, 0:T - b],
                                                   k.col("dn_conv_w_2", (3 - b) * 12 + j), t.dT[:, j, b:T],
                                                   ALU.mult, ALU.add)
                    post(dve, ins, convolved if b == 3 else k.vstep)
            dve.wait_ge(k.used.sem, ba + 1)
            v(dve.tensor_scalar(xa[:], k.bank[1][0:DH, :], k.col("dn_dt_bias_2", 0, 1, DH), None, ALU.add))
            v(dve.tensor_scalar(neg[:], xa[:], -1.0, None, ALU.mult))
            post(dve, dve.tensor_tensor(neg[:], neg[:], xa[:], ALU.min), absed)
            dve.wait_ge(exped.sem, 1)
            post(dve, dve.tensor_scalar(u[:], e[:], 1.0, None, ALU.add), summed)
            v(dve.scalar_tensor_tensor(e[:], u[:], -1.0, e[:], ALU.add, ALU.subtract))
            v(dve.reciprocal(neg[:], u[:]))
            v(dve.scalar_tensor_tensor(e[:], e[:], -1.0, neg[:], ALU.mult, ALU.mult))
            dve.wait_ge(logged.sem, 1)
            v(dve.tensor_tensor(e[:], e[:], ln[:], ALU.add))
            v(dve.scalar_tensor_tensor(xa[:], xa[:], 0.0, e[:], ALU.max, ALU.add))
            dve.wait_ge(sig_ok.sem, 1)
            v(dve.tensor_scalar(e[:], xa[:], a_neg[:], -1.0, ALU.mult, ALU.mult))
            for c in range(T // CH):
                cs = slice(c * CH, (c + 1) * CH)
                v(dve.tensor_tensor_scan(t.gcT[:, cs], ones[:], e[:, cs], 0.0, ALU.mult, ALU.add))


def band_setup_stage(k, t):
    nc, d = k.nc, k.dram
    with ExitStack() as ctx:
        def sb(name, shape):
            return ctx.enter_context(nc.sbuf_tensor(name, shape, F32))

        sq = sb("band_squares", [P, NT * 512])
        ssum = sb("band_sums", [P, 2, NT * BH])
        rb = sb("rel_bias_padded", [BH, 384])
        first = ctx.enter_context(nc.semaphore("rel_bias_in"))
        padded = Signal(ctx, nc, "rel_bias_padded_ready")
        stored = ctx.enter_context(nc.semaphore("rel_bias_stored"))
        spread = ctx.enter_context(nc.semaphore("near_bias_in"))
        summed = Signal(ctx, nc, "band_squares_summed")
        rooted = Signal(ctx, nc, "band_roots")
        ready = Signal(ctx, nc, "band_rows_ready")
        turned = ctx.enter_context(nc.semaphore("band_turned"))
        turned_in = Signal(ctx, nc, "band_turned_in")
        flipped = ctx.enter_context(nc.semaphore("near_bias_flipped"))
        flipped_in = Signal(ctx, nc, "near_bias_flipped_in")
        block = ctx.enter_context(nc.Block())
        rel = t.rel_scratch

        @block.sync
        def _(sp):
            sp.dma_start(rb[:, 127:384], d["rel_bias_reversed"]).then_inc(first, 16)
            sp.wait_ge(padded.sem, 1)
            sp.dma_start(rel, rb[:]).then_inc(stored, 16)
            sp.wait_ge(stored, 16)
            near = bass.AP(tensor=rel.tensor, offset=0, ap=[[1, P], [384, BH], [1, 256]])
            sp.dma_start(t.near[:], near).then_inc(spread, 16)

        @block.vector
        def _(dve):
            def v(ins):
                post(dve, ins, k.vstep)

            dve.wait_ge(first, 16)
            post(dve, dve.tensor_copy(rb[:, 0:127], rb[:, 127:128].broadcast_to([BH, 127])), padded)
            for w, x in enumerate((t.qa, t.ka)):
                flat = x[:].rearrange("p t n -> p (t n)")
                v(dve.tensor_tensor(sq[:], flat, flat, ALU.mult))
                ins = dve.tensor_reduce(ssum[:, w, :], sq[:].rearrange("p (a d) -> p a d", d=BD), AX, ALU.add)
                post(dve, ins, summed)
            dve.wait_ge(rooted.sem, 1)
            v(dve.reciprocal(ssum[:], ssum[:]))
            for w, (x, gain) in enumerate(((t.qa, "attn_q_gain_2"), (t.ka, "attn_k_gain_2"))):
                x3 = x[:].rearrange("p t (h d) -> p (t h) d", h=BH)
                v(dve.tensor_tensor(x3, x3, bc(ssum[:, w, :], 2, [P, NT * BH, BD]), ALU.mult))
                post(dve, dve.tensor_tensor(x3, x3, bc(k.row(gain), 1, [P, NT * BH, BD]), ALU.mult), ready)
            dve.wait_ge(flipped_in.sem, 4)
            diag = t.near[:, :, P:2 * P]
            v(dve.tensor_tensor(diag, diag, bc(k.const("band_add"), 1, [P, BH, P]), ALU.add))

        @block.scalar
        def _(act):
            act.wait_ge(summed.sem, 2)
            post(act, act.activation(ssum[:], ssum[:], ACT.Sqrt, bias=k.const("eps"), scale=1.0 / BD), rooted)
            for n, dst in enumerate([t.qaT[:, j, :] for j in range(4)] + [t.kaT[:, j, :] for j in range(4)]):
                act.wait_ge(turned, n + 1)
                post(act, act.activation(dst, k.bank[n][:], ACT.Copy), turned_in)
            act.wait_ge(flipped, 1)
            for j in range(4):
                post(act, act.activation(t.near[:, 2 * j:2 * j + 2, :], k.bank[j][:].rearrange("p (h s) -> p h s", h=2),
                                         ACT.Copy), flipped_in)

        @block.tensor
        def _(pe):
            for w, src in enumerate((t.qa, t.ka)):
                pe.wait_ge(ready.sem, w + 1)
                for j in range(4):
                    for i in range(NT):
                        last = pe.transpose(k.bank[4 * w + j][:, i * P:(i + 1) * P], src[:, i, j * P:(j + 1) * P],
                                            k.const("ident"))
                    last.then_inc(turned, 1)
            pe.wait_ge(turned_in.sem, 4)
            pe.wait_ge(spread, 16)
            for j in range(4):
                last = pe.matmul(k.bank[j][:], k.const("flip"), t.near[:, 2 * j:2 * j + 2, :].rearrange("p h s -> p (h s)"),
                                 start=True, stop=True)
            last.then_inc(flipped, 1)


def band_attention_stage(k, t):
    nc = k.nc
    scale = float(BD) ** -0.5
    with ExitStack() as ctx:
        def sb(name, shape):
            return ctx.enter_context(nc.sbuf_tensor(name, shape, F32))

        s_at, p_at = [0, P, 3 * P, 6 * P], [0, 4 * P, 7 * P, 9 * P]
        s = sb("band_scores", [P, 2, 10 * P])
        pT = sb("band_probsT", [P, 2, 10 * P])
        top = sb("band_top", [P, 2, NT])
        den = sb("band_sum", [P, 2, NT])
        scored = ctx.enter_context(nc.semaphore("band_scores_made"))
        read = Signal(ctx, nc, "band_scores_read")
        topped = Signal(ctx, nc, "band_tops")
        exped = Signal(ctx, nc, "band_exps")
        flipped = ctx.enter_context(nc.semaphore("band_probs_flipped"))
        copied = Signal(ctx, nc, "band_probsT_copied")
        valued = ctx.enter_context(nc.semaphore("band_values_mixed"))
        normed = Signal(ctx, nc, "band_outputs_normed")
        block = ctx.enter_context(nc.Block())
        place = [(4, 0), (5, 0), (6, 0), (6, 256)]

        @block.tensor
        def _(pe):
            def scores(h):
                p0 = BD * (h % 2)
                for i in range(NT):
                    if h > 0:
                        pe.wait_ge(read.sem, NT * (h - 1) + i + 1)
                    w = (i + 1) * P
                    pe.matmul(k.bank[i][:, 0:w], t.qaT[p0:p0 + BD, h // 2, i * P:w], t.kaT[p0:p0 + BD, h // 2, 0:w],
                              start=True, stop=True).then_inc(scored, 1)

            scores(0)
            for h in range(BH):
                if h + 1 < BH:
                    scores(h + 1)
                for i in range(NT):
                    pe.wait_ge(exped.sem, NT * h + i + 1)
                    if h > 0 and i == 0:
                        pe.wait_ge(copied.sem, NT * h)
                    for j in range(i + 1):
                        b, c = place[j]
                        c += (i - j) * P
                        last = pe.transpose(k.bank[b][:, c:c + P], s[:, h % 2, s_at[i] + j * P:s_at[i] + (j + 1) * P],
                                            k.const("ident"))
                last.then_inc(flipped, 1)
                if h > 0:
                    pe.wait_ge(normed.sem, h)
                pe.wait_ge(copied.sem, NT * (h + 1))
                for i in range(NT):
                    for j in range(i + 1):
                        last = pe.matmul(k.bank[7][:, i * BD:(i + 1) * BD],
                                         pT[:, h % 2, p_at[j] + (i - j) * P:p_at[j] + (i - j + 1) * P],
                                         t.va[:, j, h * BD:(h + 1) * BD], start=(j == 0), stop=(j == i))
                last.then_inc(valued, 1)

        @block.vector
        def _(dve):
            def softmax_in(h):
                for i in range(NT):
                    w = (i + 1) * P
                    dve.wait_ge(scored, NT * h + i + 1)
                    if h >= 2:
                        dve.wait_ge(flipped, h - 1)
                    at = s_at[i]
                    if i >= 2:
                        post(dve, dve.tensor_scalar(s[:, h % 2, at:at + w - 2 * P], k.bank[i][:, 0:w - 2 * P], scale,
                                                    k.row("rel_far")[:, h:h + 1], ALU.mult, ALU.add), k.vstep)
                    nw = min(w, 2 * P)
                    post(dve, dve.scalar_tensor_tensor(s[:, h % 2, at + w - nw:at + w], k.bank[i][:, w - nw:w], scale,
                                                       t.near[:, h, 2 * P - nw:2 * P], ALU.mult, ALU.add), read)
                    post(dve, dve.tensor_reduce(top[:, h % 2, i:i + 1], s[:, h % 2, at:at + w], AX, ALU.max,
                                                negate=True), topped)

            def out(h):
                dve.wait_ge(valued, h + 1)
                post(dve, dve.reciprocal(den[:, h % 2, :], den[:, h % 2, :]), k.vstep)
                o3 = k.bank[7][:, 0:NT * BD].rearrange("p (t d) -> p t d", t=NT)
                post(dve, dve.tensor_tensor(t.oa[:, :, h * BD:(h + 1) * BD], o3, bc(den[:, h % 2, :], 2, [P, NT, BD]),
                                            ALU.mult), normed)

            softmax_in(0)
            for h in range(BH):
                if h + 1 < BH:
                    softmax_in(h + 1)
                out(h)

        @block.scalar
        def _(act):
            def exps(h):
                for i in range(NT):
                    w = (i + 1) * P
                    act.wait_ge(topped.sem, NT * h + i + 1)
                    if h >= 2 and i == 0:
                        act.wait_ge(normed.sem, h - 1)
                    post(act, act.activation(s[:, h % 2, s_at[i]:s_at[i] + w], s[:, h % 2, s_at[i]:s_at[i] + w], ACT.Exp,
                                             bias=top[:, h % 2, i:i + 1], accum_out=den[:, h % 2, i:i + 1]), exped)

            exps(0)
            for h in range(BH):
                if h + 1 < BH:
                    exps(h + 1)
                act.wait_ge(flipped, h + 1)
                if h >= 2:
                    act.wait_ge(valued, h - 1)
                for j in range(NT):
                    b, c = place[j]
                    post(act, act.activation(pT[:, h % 2, p_at[j]:p_at[j] + T - j * P], k.bank[b][:, c:c + T - j * P],
                                             ACT.Copy), copied)


def delta_setup_stage(k, t):
    nc = k.nc
    with ExitStack() as ctx:
        def sb(name, shape):
            return ctx.enter_context(nc.sbuf_tensor(name, shape, F32))

        sq = sb("dn_squares", [P, 2, T])
        rstd = sb("dn_rstd", [P, 2, T])
        last_row = sb("dn_chunk_end_rows", [P, NT, DH])
        squared = Signal(ctx, nc, "dn_squared")
        summed = ctx.enter_context(nc.semaphore("dn_squares_summed"))
        rooted = Signal(ctx, nc, "dn_roots")
        scaled = Signal(ctx, nc, "dn_columns_scaled")
        spread = ctx.enter_context(nc.semaphore("dn_sums_spread"))
        spread_in = Signal(ctx, nc, "dn_sums_in")
        turned = ctx.enter_context(nc.semaphore("dn_turned"))
        rows_in = Signal(ctx, nc, "dn_rows_in")
        expo = Signal(ctx, nc, "dn_row_exponents")
        expd = Signal(ctx, nc, "dn_row_exps")
        block = ctx.enter_context(nc.Block())

        @block.tensor
        def _(pe):
            for h in range(DH):
                sel = k.const("ident", DH, DH)[:, h:h + 1].broadcast_to([DH, P])
                pe.matmul(k.bank[h][:], sel, t.gcT[:], start=True, stop=True).then_inc(spread, 1)
            for i in range(NT):
                pe.transpose(k.bank[4][:, 8 * i:8 * i + 4], t.gcT[:, i * P:(i + 1) * P], k.const("ident", DH, DH))
                last = pe.transpose(k.bank[4][:, 8 * i + 4:8 * i + 8], t.betaT[:, i * P:(i + 1) * P],
                                    k.const("ident", DH, DH))
            last.then_inc(spread, 1)
            for j in range(8):
                pe.wait_ge(squared.sem, j + 1)
                if j >= 2:
                    pe.wait_ge(rooted.sem, j - 1)
                pe.matmul(k.bank[5 + j % 2][:], k.const("ones"), sq[:, j % 2, :], start=True, stop=True).then_inc(summed, 1)
            pe.wait_ge(scaled.sem, 8)
            pe.wait_ge(spread_in.sem, 6)
            for n in range(8):
                i, first = n % 4, 8 if n < 4 else 4
                for h in range(DH):
                    last = pe.transpose(k.bank[[0, 1, 2, 3, 7, 4, 5, 6][n]][:, h * P:(h + 1) * P],
                                        t.dT[:, first + h, i * P:(i + 1) * P], k.const("ident"))
                last.then_inc(turned, 1)

        @block.scalar
        def _(act):
            for h in range(DH):
                act.wait_ge(spread, h + 1)
                post(act, act.activation(t.gcB[:, h, :], k.bank[h][:], ACT.Copy), spread_in)
            act.wait_ge(spread, 5)
            v4 = k.bank[4][:, 0:32].rearrange("p (t x) -> p t x", t=NT)
            post(act, act.activation(t.gc_row[:], v4[:, :, 0:4], ACT.Copy), spread_in)
            post(act, act.activation(t.beta_row[:], v4[:, :, 4:8], ACT.Copy), spread_in)
            for j in range(8):
                act.wait_ge(summed, j + 1)
                if j >= 2:
                    act.wait_ge(scaled.sem, j - 1)
                post(act, act.activation(rstd[:, j % 2, :], k.bank[5 + j % 2][:], ACT.Sqrt, bias=k.const("eps")), rooted)
            for n in range(8):
                act.wait_ge(turned, n + 1)
                dst = t.v_row if n < 4 else t.k_row
                post(act, act.activation(dst[:, n % 4, :], k.bank[[0, 1, 2, 3, 7, 4, 5, 6][n]][:], ACT.Copy), rows_in)
            act.wait_ge(expo.sem, 1)
            post(act, act.activation(t.egl[:], t.egl[:], ACT.Exp), k.astep)
            post(act, act.activation(last_row[:], last_row[:], ACT.Exp), k.astep)
            post(act, act.activation(t.eg_row[:], t.gc_row[:], ACT.Exp), expd)
            post(act, act.activation(t.qgT[:], t.gcB[:], ACT.Exp), expd)

        @block.vector
        def _(dve):
            def v(ins):
                post(dve, ins, k.vstep)

            for j in range(8):
                if j == 0:
                    for jj in range(2):
                        post(dve, dve.tensor_tensor(sq[:, jj, :], t.dT[:, jj, :], t.dT[:, jj, :], ALU.mult), squared)
                dve.wait_ge(rooted.sem, j + 1)
                v(dve.reciprocal(rstd[:, j % 2, :], rstd[:, j % 2, :]))
                if j < DH:
                    post(dve, dve.scalar_tensor_tensor(t.dT[:, j, :], t.dT[:, j, :], float(P) ** -0.5, rstd[:, j % 2, :],
                                                       ALU.mult, ALU.mult), scaled)
                else:
                    post(dve, dve.tensor_tensor(t.dT[:, j, :], t.dT[:, j, :], rstd[:, j % 2, :], ALU.mult), scaled)
                if j + 2 < 8:
                    post(dve, dve.tensor_tensor(sq[:, j % 2, :], t.dT[:, j + 2, :], t.dT[:, j + 2, :], ALU.mult), squared)
            dve.wait_ge(spread_in.sem, 6)
            ends = t.gcB[:].rearrange("p h (n c) -> p h n c", c=CH)[:, :, :, CH - 1]
            v(dve.tensor_copy(t.egl[:], ends))
            for half in range(2):
                ps = slice(CH * half, CH * (half + 1))
                mine = ends.rearrange("p h (t two) -> p t h two", two=2)[ps, :, :, half]
                ins = dve.tensor_tensor(last_row[ps], mine, t.gc_row[ps], ALU.subtract)
                post(dve, ins, expo if half else k.vstep)
            dve.wait_ge(rows_in.sem, 8)
            dve.wait_ge(expd.sem, 2)
            shape = [P, NT, DH, P]

            def heads(x):
                return x[:].rearrange("p t (h d) -> p t h d", h=DH)

            v(dve.tensor_tensor(heads(t.v_row), heads(t.v_row), bc(t.beta_row[:], 3, shape), ALU.mult))
            v(dve.tensor_tensor(heads(t.kdec), heads(t.k_row), bc(last_row[:], 3, shape), ALU.mult))
            v(dve.tensor_tensor(heads(t.k_row), heads(t.k_row), bc(t.beta_row[:], 3, shape), ALU.mult))
            v(dve.tensor_tensor(heads(t.k_row), heads(t.k_row), bc(t.eg_row[:], 3, shape), ALU.mult))
            v(dve.tensor_tensor(t.qgT[:], t.qgT[:], t.dT[:, 0:DH, :], ALU.mult))


def delta_solve_stage(k, t):
    nc = k.nc
    levels = ["lvlT2", "lvlT4", "lvlT8", "lvlT16", "lvlT32"]
    with ExitStack() as ctx:
        def sb(name, shape):
            return ctx.enter_context(nc.sbuf_tensor(name, shape, F32))

        full = [P, DH, P]
        dec = sb("dn_decay", full)
        low = sb("dn_lower", full)
        lowT = sb("dn_lowerT", full)
        x = sb("dn_inverse", full)
        xT = sb("dn_inverseT", full)
        part = sb("dn_level", full)
        yy = sb("dn_level_x", full)
        products = ctx.enter_context(nc.semaphore("dn_products"))
        diff = Signal(ctx, nc, "dn_decay_exponents")
        exped = Signal(ctx, nc, "dn_decays")
        lowered = Signal(ctx, nc, "dn_lower_ready")
        flipped = ctx.enter_context(nc.semaphore("dn_lower_flipped"))
        begun = Signal(ctx, nc, "dn_level_ready")
        first = ctx.enter_context(nc.semaphore("dn_level_first"))
        first_in = Signal(ctx, nc, "dn_level_first_in")
        second = ctx.enter_context(nc.semaphore("dn_level_second"))
        inverted = Signal(ctx, nc, "dn_inverted")
        solved = ctx.enter_context(nc.semaphore("dn_solved"))
        solved_in = Signal(ctx, nc, "dn_solved_in")
        block = ctx.enter_context(nc.Block())

        def b3(i):
            return k.bank[i][:].rearrange("p (h l) -> p h l", h=DH)

        @block.tensor
        def _(pe):
            n_lvl = len(levels)
            for i in range(NT):
                ts = slice(i * P, (i + 1) * P)
                if i > 0:
                    pe.wait_ge(solved_in.sem, 2 * i)
                for h in range(DH):
                    pe.matmul(b3(0)[:, h], t.dT[:, DH + h, ts], t.dT[:, DH + h, ts], start=True, stop=True)
                for h in range(DH):
                    last = pe.matmul(b3(1)[:, h], t.dT[:, DH + h, ts], t.dT[:, h, ts], start=True, stop=True)
                last.then_inc(products, 1)
                pe.wait_ge(lowered.sem, i + 1)
                for h in range(DH):
                    last = pe.transpose(b3(2)[:, h], low[:, h], k.const("ident"))
                last.then_inc(flipped, 1)
                for m in range(n_lvl):
                    pe.wait_ge(begun.sem, n_lvl * i + m + 1)
                    for h in range(DH):
                        last = pe.matmul(b3(3)[:, h], part[:, h], x[:, h], start=True, stop=True)
                    last.then_inc(first, 1)
                    pe.wait_ge(first_in.sem, n_lvl * i + m + 1)
                    for h in range(DH):
                        pe.matmul(b3(4)[:, h], xT[:, h], yy[:, h], start=True, stop=True)
                    for h in range(DH):
                        last = pe.matmul(b3(5)[:, h], yy[:, h], xT[:, h], start=True, stop=True)
                    last.then_inc(second, 1)
                pe.wait_ge(inverted.sem, i + 1)
                for h in range(DH):
                    hs = slice(h * P, (h + 1) * P)
                    pe.matmul(b3(6)[:, h], xT[:, h], t.v_row[:, i, hs], start=True, stop=True)
                for h in range(DH):
                    hs = slice(h * P, (h + 1) * P)
                    last = pe.matmul(b3(7)[:, h], t.k_row[:, i, hs], xT[:, h], start=True, stop=True)
                last.then_inc(solved, 1)

        @block.scalar
        def _(act):
            n_lvl = len(levels)
            for i in range(NT):
                for w in range(2):
                    act.wait_ge(diff.sem, 2 * i + w + 1)
                    post(act, act.activation(dec[:], dec[:], ACT.Exp), exped)
                for m in range(n_lvl):
                    act.wait_ge(first, n_lvl * i + m + 1)
                    post(act, act.activation(yy[:], b3(3), ACT.Copy), first_in)
                act.wait_ge(solved, i + 1)
                post(act, act.activation(t.u[:, i, :], k.bank[6][:], ACT.Copy), solved_in)
                post(act, act.activation(t.wT[:, :, i * P:(i + 1) * P], b3(7), ACT.Copy), solved_in)

        @block.vector
        def _(dve):
            def v(ins):
                post(dve, ins, k.vstep)

            n_lvl = len(levels)
            for i in range(NT):
                along = t.gcB[:, :, i * P:(i + 1) * P]
                mine = bc(t.gc_row[:, i, :], 2, full)
                v(dve.tensor_tensor(dec[:], mine, along, ALU.subtract))
                post(dve, dve.tensor_scalar(dec[:], dec[:], 0.0, None, ALU.min), diff)
                dve.wait_ge(exped.sem, 2 * i + 1)
                dve.wait_ge(products, i + 1)
                v(dve.tensor_tensor(low[:], b3(0), dec[:], ALU.mult))
                v(dve.tensor_tensor(low[:], low[:], bc(t.beta_row[:, i, :], 2, full), ALU.mult))
                post(dve, dve.tensor_tensor(low[:], low[:], bc(k.const("strict64"), 1, full), ALU.mult), lowered)
                v(dve.tensor_tensor(dec[:], along, mine, ALU.subtract))
                post(dve, dve.tensor_scalar(dec[:], dec[:], 0.0, None, ALU.min), diff)
                dve.wait_ge(exped.sem, 2 * i + 2)
                v(dve.tensor_tensor(t.at[:, i], b3(1), dec[:], ALU.mult))
                v(dve.tensor_tensor(t.at[:, i], t.at[:, i], bc(k.const("upper64"), 1, full), ALU.mult))
                dve.wait_ge(flipped, i + 1)
                v(dve.tensor_copy(lowT[:], b3(2)))
                for dst, src, mask in ((x, low, "lvl1"), (xT, lowT, "lvl1T")):
                    v(dve.scalar_tensor_tensor(dst[:], src[:], -1.0, bc(k.const(mask), 1, full), ALU.mult, ALU.mult))
                    v(dve.tensor_tensor(dst[:], dst[:], bc(k.const("ident"), 1, full), ALU.add))
                for m, mask in enumerate(levels):
                    post(dve, dve.tensor_tensor(part[:], lowT[:], bc(k.const(mask), 1, full), ALU.mult), begun)
                    dve.wait_ge(second, n_lvl * i + m + 1)
                    v(dve.tensor_tensor(x[:], x[:], b3(4), ALU.subtract))
                    post(dve, dve.tensor_tensor(xT[:], xT[:], b3(5), ALU.subtract),
                         inverted if m == n_lvl - 1 else k.vstep)


def delta_scan_stage(k, t):
    nc = k.nc
    with ExitStack() as ctx:
        state = ctx.enter_context(nc.sbuf_tensor("dn_state", [P, DH, P], F32))
        vnew = ctx.enter_context(nc.sbuf_tensor("dn_v_new", [P, DH, P], F32))
        kept = Signal(ctx, nc, "dn_state_ready")
        removed = ctx.enter_context(nc.semaphore("dn_state_read"))
        v_ok = Signal(ctx, nc, "dn_v_new_ready")
        added = ctx.enter_context(nc.semaphore("dn_chunk_products"))
        stored = Signal(ctx, nc, "dn_chunk_stored")
        block = ctx.enter_context(nc.Block())

        def b3(i):
            return k.bank[i][:].rearrange("p (h l) -> p h l", h=DH)

        @block.tensor
        def _(pe):
            for n in range(T // CH):
                i, ps = n // 2, slice(CH * (n % 2), CH * (n % 2 + 1))
                cs = slice(n * CH, (n + 1) * CH)
                pe.wait_ge(kept.sem, n + 1)
                for h in range(DH):
                    last = pe.matmul(b3(0)[ps, h], t.wT[:, h, cs], state[:, h], start=True, stop=True)
                last.then_inc(removed, 1)
                if n > 0:
                    pe.wait_ge(stored.sem, n)
                pe.wait_ge(v_ok.sem, n + 1)
                for h in range(DH):
                    pe.matmul(b3(1)[ps, h], t.qgT[:, h, cs], state[:, h], start=True, stop=False)
                    pe.matmul(b3(1)[ps, h], t.at[ps, i, h, ps], vnew[ps, h], start=False, stop=True)
                for h in range(DH):
                    last = pe.matmul(b3(2)[:, h], t.kdec[ps, i, h * P:(h + 1) * P], vnew[ps, h], start=True, stop=True)
                last.then_inc(added, 1)

        @block.vector
        def _(dve):
            post(dve, dve.memset(state[:], 0.0), kept)
            for n in range(T // CH):
                i, ps = n // 2, slice(CH * (n % 2), CH * (n % 2 + 1))
                dve.wait_ge(removed, n + 1)
                u3 = t.u[ps, i, :].rearrange("p (h d) -> p h d", h=DH)
                post(dve, dve.tensor_tensor(vnew[ps], u3, b3(0)[ps], ALU.subtract), v_ok)
                dve.wait_ge(added, n + 1)
                post(dve, dve.tensor_tensor(state[:], state[:], bc(t.egl[:, :, n], 2, [P, DH, P]), ALU.mult), k.vstep)
                post(dve, dve.tensor_tensor(state[:], state[:], b3(2), ALU.add), kept)

        @block.scalar
        def _(act):
            for n in range(T // CH):
                i, ps = n // 2, slice(CH * (n % 2), CH * (n % 2 + 1))
                act.wait_ge(added, n + 1)
                post(act, act.activation(t.ob[ps, i, :], k.bank[1][ps, :], ACT.Copy), stored)


def second_out_stage(k, t):
    nc = k.nc
    with ExitStack() as ctx:
        def sb(name, shape):
            return ctx.enter_context(nc.sbuf_tensor(name, shape, F32))

        sq = sb("mix_squares", [P, NT, 512])
        ss = sb("mix_sums", [P, NT + NT * DH])
        mixT = k.hT
        plan = columns(find(k, "w_out_2", 0, 1024), mixT)
        pj = Projection(k, ctx, "second_out", plan)
        summed = Signal(ctx, nc, "mix_squares_summed")
        rooted = Signal(ctx, nc, "mix_roots")
        ready = Signal(ctx, nc, "mix_rows_ready")
        turned = ctx.enter_context(nc.semaphore("mix_turned"))
        copied = Signal(ctx, nc, "mix_columns")
        block = ctx.enter_context(nc.Block())

        @block.sync
        def _(sp):
            k.stream(sp, plan[-1][1][-1])

        @block.vector
        def _(dve):
            def v(ins):
                post(dve, ins, k.vstep)

            ob4 = t.ob[:].rearrange("p t (h d) -> p t h d", h=DH)
            v(dve.tensor_tensor(sq[:], t.oa[:], t.oa[:], ALU.mult))
            v(dve.tensor_reduce(ss[:, 0:NT], sq[:], AX, ALU.add))
            v(dve.tensor_tensor(sq[:], t.ob[:], t.ob[:], ALU.mult))
            v(dve.tensor_reduce(ss[:, NT:], sq[:].rearrange("p t (h d) -> p (t h) d", h=DH), AX, ALU.add))
            post(dve, dve.tensor_scalar(ss[:, 0:NT], ss[:, 0:NT], 0.25, None, ALU.mult), summed)
            dve.wait_ge(rooted.sem, 1)
            v(dve.reciprocal(ss[:], ss[:]))
            v(dve.tensor_tensor(t.oa[:], t.oa[:], bc(ss[:, 0:NT], 2, [P, NT, 512]), ALU.mult))
            r = ss[:, NT:].rearrange("p (t h) -> p t h", t=NT)
            v(dve.tensor_tensor(ob4, ob4, bc(r, 3, [P, NT, DH, P]), ALU.mult))
            post(dve, dve.tensor_tensor(t.ob[:], t.ob[:], t.zb[:], ALU.mult), ready)
            for j in range(8):
                bank = pj.next(dve)
                post(dve, dve.scalar_tensor_tensor(k.xT[:, j, :], bank[:], k.mod2[:, 16 + j:17 + j], k.xT[:, j, :],
                                                   ALU.mult, ALU.add), pj.freed)

        @block.scalar
        def _(act):
            act.wait_ge(summed.sem, 1)
            post(act, act.activation(ss[:], ss[:], ACT.Sqrt, bias=k.const("eps"), scale=1.0 / P), rooted)
            for j in range(8):
                gain = k.col("attn_out_gain_2", j) if j < 4 else k.col("dn_out_gain_2")
                act.wait_ge(turned, j + 1)
                post(act, act.activation(mixT[:, j, :], k.bank[j][:], ACT.Copy, scale=gain), copied)

        @block.tensor
        def _(pe):
            pe.wait_ge(ready.sem, 1)
            for j in range(8):
                src = t.oa if j < 4 else t.ob
                for i in range(NT):
                    last = pe.transpose(k.bank[j][:, i * P:(i + 1) * P], src[:, i, (j % 4) * P:(j % 4 + 1) * P],
                                        k.const("ident"))
                last.then_inc(turned, 1)
            pe.wait_ge(copied.sem, 8)
            pj.run(pe)


def second_mixer(k):
    nc = k.nc
    with ExitStack() as ctx:
        def sb(name, shape):
            return ctx.enter_context(nc.sbuf_tensor(name, shape, F32))

        t = Part()
        t.rel_scratch = nc.dram_tensor("rel_bias_scratch", (BH, 384), F32, kind="Internal").ap()
        t.zb = sb("silu_z_b", [P, NT, 512])
        t.betaT, t.gcT = sb("betaT", [DH, T]), sb("gcT", [DH, T])
        t.oa = sb("band_out", [P, NT, 512])
        t.dT = sb("delta_qkvT", [P, 12, T])
        with ExitStack() as bctx:
            def bsb(name, shape):
                return bctx.enter_context(nc.sbuf_tensor(name, shape, F32))

            t.qa, t.ka, t.va = (bsb(n, [P, NT, 512]) for n in ("band_q", "band_k", "band_v"))
            second_projection_stage(k, t)
            t.qaT, t.kaT = k.hT[:, 0:4, :], k.hT[:, 4:8, :]
            t.near = bsb("near_bias", [P, BH, 256])
            band_setup_stage(k, t)
            band_attention_stage(k, t)
        t.gcB = sb("gc_spread", [P, DH, T])
        t.gc_row, t.beta_row, t.eg_row = (sb(n, [P, NT, DH]) for n in ("gc_rows", "beta_rows", "exp_gc_rows"))
        t.egl = sb("exp_gc_chunk_end", [P, DH, T // CH])
        t.k_row, t.v_row = (sb(n, [P, NT, 512]) for n in ("dn_k_rows", "dn_v_rows"))
        t.kdec, t.qgT = k.hT[:, 0:4, :], k.hT[:, 4:8, :]
        delta_setup_stage(k, t)
        t.u = sb("dn_u", [P, NT, 512])
        t.wT = sb("dn_wT", [P, DH, T])
        t.at = sb("dn_intraT", [P, NT, DH, P])
        delta_solve_stage(k, t)
        t.ob = sb("dn_out", [P, NT, 512])
        delta_scan_stage(k, t)
        second_out_stage(k, t)


def expert_rows_stage(k, t):
    nc = k.nc
    with ExitStack() as ctx:
        turned = ctx.enter_context(nc.semaphore("rows_back_turned"))
        copied = Signal(ctx, nc, "rows_back")
        block = ctx.enter_context(nc.Block())
        jobs = [(src, dst, i, half) for src, dst in ((k.hT, t.h_row), (k.xT, t.x_row)) for i in range(NT)
                for half in range(2)]

        @block.tensor
        def _(pe):
            for n, (src, _, i, half) in enumerate(jobs):
                if n >= 8:
                    pe.wait_ge(copied.sem, n - 7)
                for j in range(4):
                    last = pe.transpose(k.bank[n % 8][:, j * P:(j + 1) * P], src[:, 4 * half + j, i * P:(i + 1) * P],
                                        k.const("ident"))
                last.then_inc(turned, 1)

        @block.scalar
        def _(act):
            for n, (_, dst, i, half) in enumerate(jobs):
                act.wait_ge(turned, n + 1)
                post(act, act.activation(dst[:, i, half * 512:(half + 1) * 512], k.bank[n % 8][:], ACT.Copy), copied)


def query_stage(k, t):
    nc, d = k.nc, k.dram
    with ExitStack() as ctx:
        def sb(name, shape):
            return ctx.enter_context(nc.sbuf_tensor(name, shape, F32))

        qT = sb("queriesT", [P, 2 * RH, T])
        sq = sb("query_squares", [P, 2, 2, T])
        keys = sb("sub_keys", [P, 2, P])
        keyT = sb("sub_keysT", [P, 2, P])
        keys_in = ctx.enter_context(nc.semaphore("sub_keys_loaded"))
        keys_turned = ctx.enter_context(nc.semaphore("sub_keys_turned"))
        keys_ok = Signal(ctx, nc, "sub_keys_ready")
        squared = Signal(ctx, nc, "queries_squared")
        summed = ctx.enter_context(nc.semaphore("query_squares_summed"))
        rooted = Signal(ctx, nc, "query_roots")
        scored = ctx.enter_context(nc.semaphore("key_scores_made"))
        plan = columns(find(k, "peer_w_query_2", 0, 2048), k.hT)
        pj = Projection(k, ctx, "queries", plan, banks=range(6))
        block = ctx.enter_context(nc.Block())

        @block.sync
        def _(sp):
            sp.dma_start(keys[:, 0, :], d["peer_sub_keys_1_2"]).then_inc(keys_in, 16)
            sp.dma_start(keys[:, 1, :], d["peer_sub_keys_2_2"]).then_inc(keys_in, 16)
            k.stream(sp, plan[-1][1][-1])

        @block.tensor
        def _(pe):
            pe.wait_ge(keys_in, 32)
            for w in range(2):
                last = pe.transpose(k.bank[7][:, w * P:(w + 1) * P], keys[:, w, :], k.const("ident"))
            last.then_inc(keys_turned, 1)

            def sums(h):
                pe.wait_ge(squared.sem, 2 * (h + 1))
                for i in range(NT):
                    for half in range(2):
                        last = pe.matmul(k.bank[6][:, i * RH + h:i * RH + h + 1],
                                         sq[:, h % 2, half, i * P:(i + 1) * P], k.const("ones", 1),
                                         start=(half == 0), stop=(half == 1))
                last.then_inc(summed, 1)

            for n in range(4):
                pj.run(pe, slice(n, n + 1))
                for h in ((2 * n - 2, 2 * n - 1) if n else ()):
                    sums(h)
            sums(6)
            sums(7)
            pe.wait_ge(pj.freed.sem, 16)
            pe.wait_ge(keys_ok.sem, 2)
            for n in range(4 * NT):
                i, quarter = n // 4, n % 4
                bank = k.bank[n % 6]
                if n >= 6:
                    pe.wait_ge(t.scores_in.sem, n - 5)
                for j in range(4):
                    b = 4 * quarter + j
                    last = pe.matmul(bank[:, j * P:(j + 1) * P], qT[:, b, i * P:(i + 1) * P], keyT[:, b % 2, :],
                                     start=True, stop=True)
                last.then_inc(scored, 1)

        @block.scalar
        def _(act):
            act.wait_ge(keys_turned, 1)
            for w in range(2):
                post(act, act.activation(keyT[:, w, :], k.bank[7][:, w * P:(w + 1) * P], ACT.Copy,
                                         scale=k.col("peer_query_gain_2", w)), keys_ok)
            for b in range(2 * RH):
                bank = pj.next(act)
                post(act, act.activation(qT[:, b, :], bank[:], ACT.Copy), pj.freed)
            act.wait_ge(summed, RH)
            post(act, act.activation(t.q_rstd[:], k.bank[6][:, 0:NT * RH], ACT.Sqrt, bias=k.const("eps"),
                                     scale=1.0 / (2 * P)), rooted)
            for n in range(4 * NT):
                i, quarter = n // 4, n % 4
                act.wait_ge(scored, n + 1)
                post(act, act.activation(t.scores[:, i, quarter * 512:(quarter + 1) * 512], k.bank[n % 6][:], ACT.Copy),
                     t.scores_in)

        @block.vector
        def _(dve):
            for b in range(2 * RH):
                h, half = b // 2, b % 2
                dve.wait_ge(pj.freed.sem, b + 1)
                if h >= 2 and half == 0:
                    dve.wait_ge(summed, h - 1)
                post(dve, dve.tensor_tensor(sq[:, h % 2, half, :], qT[:, b, :], qT[:, b, :], ALU.mult), squared)
            dve.wait_ge(rooted.sem, 1)
            post(dve, dve.reciprocal(t.q_rstd[:], t.q_rstd[:]), k.vstep)


def expert_stage(k, t):
    nc, d = k.nc, k.dram
    GR = 16
    with ExitStack() as ctx:
        def sb(name, shape, dt=F32):
            return ctx.enter_context(nc.sbuf_tensor(name, shape, dt))

        more = sb("more_expert_rows", [P, GR - 4 * SLOTS, D])
        slot = [r[:, 2 * a:2 * a + 2, :].rearrange("p a b -> p (a b)") for r in k.ring for a in range(4)]
        slot += [more[:, a, :] for a in range(GR - 4 * SLOTS)]
        diag = sb("coef_diagonals", [P, RK, P])
        experts = sb("experts", [P, NT, NSEL], I32)
        gates = sb("expert_gates", [P, NT, NSEL])
        dots = sb("expert_dots", [P, 2, RK])
        coef = sb("expert_coefs", [P, 2, RK])
        left = sb("scores_left_over", [P, RK * RK])
        vals = sb("key_values", [P, 2, RK])
        kidx = sb("key_indices", [P, 2, RK], U32)
        kidx_f = sb("key_indices_f", [P, 2, RK])
        cand = sb("pair_scores", [P, RK, RK])
        ctop = sb("pair_top", [P, RK])
        cpos = sb("pair_positions", [P, RK], U32)
        part = sb("pair_parts", [P, RK], U32)
        part_f = sb("pair_parts_f", [P, RK])
        picked = sb("key_picked", [P, 2, RK])
        gsum = sb("gate_sums", [P, 1])
        here = [ctx.enter_context(nc.semaphore(f"expert_row_in{s}")) for s in range(GR)]
        routed = Signal(ctx, nc, "unit_routed")
        soft_in = Signal(ctx, nc, "gate_exponents")
        soft_out = Signal(ctx, nc, "gate_exps")
        dotted = Signal(ctx, nc, "expert_dots_made")
        gelued = Signal(ctx, nc, "expert_gelus")
        weighed = Signal(ctx, nc, "expert_coefs_ready")
        diag_ok = Signal(ctx, nc, "coef_diagonal_ready")
        summed = ctx.enter_context(nc.semaphore("expert_row_summed"))
        written = Signal(ctx, nc, "tile_result")
        out_ok = k.output_stored
        block = ctx.enter_context(nc.Block())
        out2 = k.out[0].rearrange("(t p) d -> p t d", p=P)
        units = [(i, h) for i in range(NT) for h in range(RH)]
        N = len(units)

        order = [("down", 0, s) for s in range(RK)]
        for u in range(N):
            for s in range(RK):
                if u + 1 < N:
                    order.append(("down", u + 1, s))
                order.append(("up", u, s))
        place = {job: n for n, job in enumerate(order)}

        @block.gpsimd
        def _(pool):
            for n, (kind, u, s) in enumerate(order):
                if kind == "down" and s == 0:
                    pool.wait_ge(routed.sem, u + 1)
                if n >= GR:
                    old_kind, old_u, old_s = order[n - GR]
                    pool.wait_ge(dotted.sem if old_kind == "down" else summed, old_u * RK + old_s + 1)
                i, h = units[u]
                j = h * RK + s
                pool.indirect_dma_start(
                    out=slot[n % GR], out_offset=None, in_=d[f"peer_expert_{kind}_2"],
                    in_offset=bass.IndirectOffsetOnAxis(ap=experts[:, i, j:j + 1], axis=0),
                ).then_inc(here[n % GR], 16)

        def arrived(eng, job):
            n = place[job]
            eng.wait_ge(here[n % GR], 16 * (n // GR + 1))
            return slot[n % GR]

        @block.vector
        def _(dve):
            def v(ins):
                post(dve, ins, k.vstep)

            def top16(values, indices, source, width):
                v(dve.max(values[:, 0:8], source))
                v(dve.max_index(indices[:, 0:8], values[:, 0:8], source))
                v(dve.match_replace(left[:, 0:width], values[:, 0:8], source, -3.0e38))
                v(dve.max(values[:, 8:16], left[:, 0:width]))
                v(dve.max_index(indices[:, 8:16], values[:, 8:16], left[:, 0:width]))

            def route(u):
                i, h = units[u]
                for w in range(2):
                    b = 2 * h + w
                    top16(vals[:, w, :], kidx[:, w, :], t.scores[:, i, b * NKEY:(b + 1) * NKEY], NKEY)
                shape = [P, RK, RK]
                v(dve.tensor_tensor(cand[:], bc(vals[:, 0], 2, shape), bc(vals[:, 1], 1, shape), ALU.add))
                top16(ctop[:], cpos[:], cand[:].rearrange("p a b -> p (a b)"), RK * RK)
                v(dve.tensor_copy(kidx_f[:], kidx[:]))
                for w, (op, by) in enumerate(((ALU.logical_shift_right, 4), (ALU.bitwise_and, 15))):
                    v(dve.tensor_scalar(part[:], cpos[:], by, None, op))
                    v(dve.tensor_copy(part_f[:], part[:]))
                    v(dve.tensor_tensor(cand[:], bc(k.const("iota16"), 1, shape), bc(part_f[:], 2, shape), ALU.is_equal))
                    v(dve.tensor_tensor(cand[:], cand[:], bc(kidx_f[:, w], 1, shape), ALU.mult))
                    v(dve.tensor_reduce(picked[:, w], cand[:], AX, ALU.add))
                mine = slice(h * RK, (h + 1) * RK)
                post(dve, dve.scalar_tensor_tensor(experts[:, i, mine], picked[:, 0], float(NKEY), picked[:, 1],
                                                   ALU.mult, ALU.add), routed)
                at = i * RH + h
                post(dve, dve.tensor_scalar(gates[:, i, mine], ctop[:], ctop[:, 0:1], t.q_rstd[:, at:at + 1],
                                            ALU.subtract, ALU.mult), soft_in)

            def dot(u):
                i, _ = units[u]
                for s in range(RK):
                    row = arrived(dve, ("down", u, s))
                    if u >= 2 and s == 0:
                        dve.wait_ge(weighed.sem, u - 1)
                    post(dve, dve.tensor_tensor_reduce(row, row, t.h_row[:, i, :], 1.0, 0.0, ALU.mult, ALU.add,
                                                       dots[:, u % 2, s:s + 1]), dotted)

            def weigh(u):
                i, h = units[u]
                g = gates[:, i, h * RK:(h + 1) * RK]
                dve.wait_ge(soft_out.sem, u + 1)
                v(dve.tensor_reduce(gsum[:], g, AX, ALU.add))
                v(dve.reciprocal(gsum[:], gsum[:]))
                dve.wait_ge(gelued.sem, u + 1)
                if u >= 2:
                    dve.wait_ge(diag_ok.sem, (u - 1) * RK)
                post(dve, dve.scalar_tensor_tensor(coef[:, u % 2, :], dots[:, u % 2, :], gsum[:], g,
                                                   ALU.mult, ALU.mult), weighed)

            def finish(i):
                dve.wait_ge(summed, (i + 1) * NSEL)
                for half in range(2):
                    hs = slice(half * 512, (half + 1) * 512)
                    v(dve.tensor_tensor(t.result[:, hs], k.bank[2 * (i % 2) + half][:], k.gate2[:, hs], ALU.mult))
                post(dve, dve.tensor_tensor(t.x_row[:, i, :], t.x_row[:, i, :], t.result[:], ALU.add), written)

            route(0)
            route(1)
            for u in range(N):
                dot(u)
                weigh(u)
                if u + 2 < N:
                    route(u + 2)
                if u > 0 and units[u][1] == 0:
                    finish(units[u][0] - 1)
            finish(NT - 1)

        @block.scalar
        def _(act):
            def soft(u):
                i, h = units[u]
                act.wait_ge(soft_in.sem, u + 1)
                g = gates[:, i, h * RK:(h + 1) * RK]
                post(act, act.activation(g, g, ACT.Exp), soft_out)

            soft(0)
            soft(1)
            for u in range(N):
                act.wait_ge(dotted.sem, (u + 1) * RK)
                post(act, act.activation(dots[:, u % 2, :], dots[:, u % 2, :], ACT.Gelu), gelued)
                act.wait_ge(weighed.sem, u + 1)
                for s in range(RK):
                    if u > 0:
                        act.wait_ge(summed, (u - 1) * RK + s + 1)
                    act.activation(diag[:, s, :], k.const("ident"), ACT.Copy,
                                   scale=coef[:, u % 2, s:s + 1]).then_inc(diag_ok.sem, 1)
                    diag_ok.n += 1
                if u + 2 < N:
                    soft(u + 2)

        @block.tensor
        def _(pe):
            for u, (i, h) in enumerate(units):
                if i >= 2 and h == 0:
                    pe.wait_ge(written.sem, i - 1)
                for s in range(RK):
                    row = arrived(pe, ("up", u, s))
                    pe.wait_ge(diag_ok.sem, u * RK + s + 1)
                    for half in range(2):
                        last = pe.matmul(k.bank[2 * (i % 2) + half][:], diag[:, s, :],
                                         row[:, half * 512:(half + 1) * 512],
                                         start=(h == 0 and s == 0), stop=(h == RH - 1 and s == RK - 1))
                    last.then_inc(summed, 1)

        @block.sync
        def _(sp):
            for i in range(NT):
                sp.wait_ge(written.sem, i + 1)
                sp.dma_start(out2[:, i, :], t.x_row[:, i, :]).then_inc(out_ok, 16)
            sp.wait_ge(out_ok, 16 * NT)


def expert_branch(k):
    nc = k.nc
    with ExitStack() as ctx:
        def sb(name, shape):
            return ctx.enter_context(nc.sbuf_tensor(name, shape, F32))

        t = Part()
        t.h_row, t.x_row = sb("h_rows", [P, NT, D]), sb("x_out_rows", [P, NT, D])
        t.scores = sb("key_scores", [P, NT, 2 * RH * NKEY])
        t.q_rstd = sb("query_rstd", [P, NT * RH])
        t.scores_in = Signal(ctx, nc, "key_scores_in")
        expert_rows_stage(k, t)
        query_stage(k, t)
        t.result = k.xT[:, 0:2, :].rearrange("p a b -> p (a b)")
        expert_stage(k, t)


def recycle(nc):
    ids = sorted(set(nc.released_uncleared_semaphores))
    runs = []
    for n in ids:
        if runs and runs[-1][1] == n:
            runs[-1][1] = n + 1
        else:
            runs.append([n, n + 1])
    for first, end in runs:
        nc.gpsimd.sem_clear(range(first, end))
    nc.all_engine_barrier()


def build(nc, dram, out, upto=99):
    with ExitStack() as ctx:
        k = Kernel(nc, ctx, dram, out)
        load_stage(k)
        modulation_stage(k)
        norm_stage(k, "norm1", "norm_g", k.mod1, 0, 8)
        with nc.sbuf_tensor("merged", [P, KD, T], F32) as k.merged:
            attention_branch(k)
            if upto < 2:
                return
            recycle(nc)
            ssm_branch(k)
        recycle(nc)
        if upto < 3:
            return
        norm_stage(k, "norm2", "norm1_gain_2", k.mod2, 0, 8)
        second_mixer(k)
        if upto < 4:
            return
        recycle(nc)
        norm_stage(k, "norm3", "norm2_gain_2", k.mod2, 24, 32)
        expert_branch(k)


def _tables():
    p = np.arange(P)
    row, colm = p[:, None], p[None, :]
    same64 = (row // 64) == (colm // 64)
    m = {"ident": np.eye(P), "flip": np.eye(P)[::-1], "ones": np.ones((P, P)), "causal_add": np.where(colm <= row, 0.0, NEG),
         "s_le_l": (row <= colm), "strict64": same64 & (colm < row), "upper64": same64 & (row <= colm),
         "iota16": np.tile(np.arange(16), (P, 1)), "eps": np.full((P, 1), EPS),
         "band_add": np.where((colm // 64) <= (row // 64), 0.0, NEG)}
    f = np.float32

    def inv(n):
        return np.power(f(500000.0), -(np.arange(0, n, 2, dtype=f) / f(n))).astype(f)

    m["inv_freq"] = np.tile(np.concatenate([inv(32), inv(16)]), (P, 1))
    for size in (1, 2, 4, 8, 16, 32):
        low = ((row // (2 * size)) == (colm // (2 * size))) & (row % (2 * size) >= size) & (colm % (2 * size) < size)
        if size == 1:
            m["lvl1"], m["lvl1T"] = low, low.T
        else:
            m[f"lvlT{size}"] = low.T
    return np.concatenate([np.asarray(m[n], f).reshape(P, w) for n, w in CONSTS], axis=1)


_DIRECT = ["x", "positions", "ada_w", "w_in", "w_branch_att", "w_branch_ssm", "w_out", "w_ada_2", "w_in_2",
           "w_out_2", "attn_rel_bias_2", "peer_w_query_2", "peer_sub_keys_1_2", "peer_sub_keys_2_2",
           "peer_expert_down_2", "peer_expert_up_2"]


def _layout(inputs):
    a = {n: np.asarray(v) for n, v in inputs.items()}
    out = {"consts": _tables()}
    for n in _DIRECT:
        v = a[n]
        out[n] = np.ascontiguousarray(v[0] if v.ndim == 3 else v)
    for n in ("peer_sub_keys_1_2", "peer_sub_keys_2_2", "peer_expert_down_2", "peer_expert_up_2", "attn_rel_bias_2"):
        out[n] = np.ascontiguousarray(a[n][0])

    out["positions"] = np.ascontiguousarray(a["positions"].reshape(NT, P).T)

    out["rel_bias_reversed"] = np.ascontiguousarray(out.pop("attn_rel_bias_2")[:, ::-1])

    def columns_of(n, w):
        if n in ("conv_w", "dn_conv_w_2"):
            v = a[n][0]
            return v.reshape(4, -1, P).transpose(2, 0, 1).reshape(P, w)
        v = a[n].reshape(-1)
        if v.size < P:
            full = np.zeros(P, v.dtype)
            full[:v.size] = v
            v = full
        return v.reshape(w, P).T

    out["cols"] = np.ascontiguousarray(np.concatenate([columns_of(n, w) for n, w in COLS], axis=1))
    rows = {n: a[n].reshape(-1) for n, _ in ROWS if n in a}
    rows["gate2_b"] = a["b_ada_2"].reshape(-1)[5 * D:6 * D]
    rows["rel_far"] = a["attn_rel_bias_2"][0][:, 256]
    out["rows"] = np.ascontiguousarray(np.concatenate([rows[n] for n, _ in ROWS])[None, :])
    return out


def kernel(**inputs):
    import concourse.bacc as _bacc
    from concourse.bass_utils import run_bass_kernel_spmd as _run

    nc = _bacc.Bacc("TRN2", target_bir_lowering=False, num_devices=1)
    arrays = _layout(inputs)
    dram = {n: nc.dram_tensor(f"in_{n}", a.shape, mybir.dt.from_np(a.dtype), kind="ExternalInput").ap()
            for n, a in arrays.items()}
    out = nc.dram_tensor("out", (1, T, D), F32, kind="ExternalOutput").ap()
    build(nc, dram, out)
    r = _run(nc, [{f"in_{n}": a for n, a in arrays.items()}], core_ids=[0])
    return r.results[0]["out"]
```

```python
from contextlib import ExitStack

import concourse.bass as bass
from concourse import mybir
import numpy as np

F32 = mybir.dt.float32
I32 = mybir.dt.int32
U32 = mybir.dt.uint32
ALU = mybir.AluOpType
ACT = mybir.ActivationFunctionType
AX = mybir.AxisListType.X

P = 128
D = 1024
KD = D // P
T = 512
NT = T // P
EPS = 1e-6
NEG = -1.0e30
SLOTS = 3
TWO_PI = 2.0 * np.pi

Q0, KV0, ZA0, IX0 = 0, 1024, 1536, 2560
ZS0, XBC0, DT0, GA0, GS0 = 2884, 4932, 8004, 8036, 9060
IDX_COLS = 4 * 64 + 64 + 4
AH, AKV, IH = 8, 2, 4
TOPK = 128
SH, SG, SP_ = 32, 4, 64
QA0, KA0, VA0, QKV0, ZB0, BA0 = 0, 512, 1024, 1536, 3072, 3584
BH, BD = 8, 64
DH, CH = 4, 64
RH, RK, NKEY = 8, 16, 128
NSEL = RH * RK

COLS = [("c", 8), ("c_2", 8), ("ada_b", 24), ("norm_g", 8), ("conv_b", 24), ("conv_w", 96),
        ("ssm_norm_g", 16), ("b_ada_2", 48), ("norm1_gain_2", 8), ("dn_conv_w_2", 48),
        ("attn_out_gain_2", 4), ("dn_out_gain_2", 1), ("norm2_gain_2", 8), ("peer_query_gain_2", 2),
        ("dt_bias", 1), ("a_log", 1), ("dn_dt_bias_2", 1), ("dn_a_log_2", 1)]
ROWS = [("q_norm_g", 128), ("k_norm_g", 128), ("idx_k_ln_g", 64), ("idx_k_ln_b", 64), ("d_skip", 32),
        ("attn_q_gain_2", 64), ("attn_k_gain_2", 64), ("gate2_b", 1024), ("rel_far", 8)]
CONSTS = [("ident", 128), ("ones", 128), ("causal_add", 128), ("s_le_l", 128), ("strict64", 128),
          ("upper64", 128), ("inv_freq", 24), ("iota16", 16), ("eps", 1), ("band_add", 128),
          ("lvl1", 128), ("lvl1T", 128), ("lvlT2", 128), ("lvlT4", 128), ("lvlT8", 128),
          ("lvlT16", 128), ("lvlT32", 128), ("flip", 128)]


def offsets(table):
    at, out = 0, {}
    for name, n in table:
        out[name] = (at, n)
        at += n
    return out, at


COL_AT, NCOL = offsets(COLS)
ROW_AT, NROW = offsets(ROWS)
CONST_AT, NCONST = offsets(CONSTS)


class Signal:

    def __init__(self, ctx, nc, name):
        self.sem = ctx.enter_context(nc.semaphore(name))
        self.n = 0


def post(eng, ins, sig):
    ins.then_inc(sig.sem, 1)
    sig.n += 1
    eng.wait_ge(sig.sem, sig.n)


class Kernel:

    def __init__(self, nc, ctx, dram, out):
        self.nc, self.ctx, self.dram, self.out = nc, ctx, dram, out
        sb = self.keep
        self.consts = sb("consts", [P, NCONST])
        self.cols = sb("cols", [P, NCOL])
        self.rows = sb("rows", [P, NROW])
        self.xT = sb("xT", [P, KD, T])
        self.hT = sb("hT", [P, KD, T])
        self.mod1 = sb("mod1", [P, 24])
        self.mod2 = sb("mod2", [P, 48])
        self.gate2 = sb("gate2", [P, D])
        self.ring = [sb(f"ring{i}", [P, KD, 512]) for i in range(SLOTS)]
        self.bank = [ctx.enter_context(nc.psum_tensor(f"bank{i}", [P, 512], F32)) for i in range(8)]
        self.vstep = Signal(ctx, nc, "vector_step")
        self.astep = Signal(ctx, nc, "scalar_step")
        self.gstep = Signal(ctx, nc, "gpsimd_step")
        self.loaded = [ctx.enter_context(nc.semaphore(f"weights_loaded{i}")) for i in range(SLOTS)]
        self.used = Signal(ctx, nc, "weights_used")
        self.output_stored = ctx.enter_context(nc.semaphore("output_stored"))
        self.issued = 0
        self.chunks = self.weight_chunks()
        self.modulation = Modulation(self)

    def keep(self, name, shape, dt=F32):
        return self.ctx.enter_context(self.nc.sbuf_tensor(name, shape, dt))

    def const(self, name, n=None, p=P):
        at, w = CONST_AT[name]
        return self.consts[0:p, at:at + (n or w)]

    def col(self, name, i=0, n=1, p=P):
        at, _ = COL_AT[name]
        return self.cols[0:p, at + i:at + i + n]

    def row(self, name, p=P):
        at, w = ROW_AT[name]
        return self.rows[0:p, at:at + w]

    def weight_chunks(self):
        d = self.dram

        def cut(name, c0, n, k0=0):
            w = d[name][k0:k0 + D, :]
            return [(name, c, k0, w[:, c:min(c + 512, c0 + n)].rearrange("(k p) n -> p k n", p=P), min(512, c0 + n - c))
                    for c in range(c0, c0 + n, 512)]

        out = cut("ada_w", 0, 3072)
        out += cut("w_in", Q0, 1024) + cut("w_in", KV0, 512) + cut("w_in", IX0, IDX_COLS)
        out += cut("w_in", ZA0, 1024)
        out += cut("w_ada_2", 0, 6144)
        out += cut("w_in", GA0, 1024) + cut("w_branch_att", 0, 1024)
        out += cut("w_in", DT0, 32) + cut("w_in", XBC0, 3072) + cut("w_in", ZS0, 2048)
        out += cut("w_in", GS0, 1024)
        for c in (0, 512):
            out += cut("w_branch_ssm", c, 512) + cut("w_branch_ssm", c, 512, D)
        out += cut("w_out", 0, 1024)
        out += cut("w_in_2", BA0, 8)
        out += cut("w_in_2", QA0, 512) + cut("w_in_2", KA0, 512) + cut("w_in_2", VA0, 512)
        out += cut("w_in_2", QKV0, 1536) + cut("w_in_2", ZB0, 512)
        out += cut("w_out_2", 0, 1024) + cut("peer_w_query_2", 0, 2048)
        return out

    def stream(self, sp, last):
        upto = min(len(self.chunks), last + SLOTS)
        for g in range(self.issued, upto):
            if g >= SLOTS:
                sp.wait_ge(self.used.sem, g - SLOTS + 1)
            n = self.chunks[g][4]
            sp.dma_start(self.ring[g % SLOTS][:, :, 0:n], self.chunks[g][3]).then_inc(self.loaded[g % SLOTS], 16)
        self.issued = max(self.issued, upto)

    def take(self, pe, g):
        pe.wait_ge(self.loaded[g % SLOTS], 16 * (g // SLOTS + 1))
        return self.ring[g % SLOTS]


class Modulation:

    def __init__(self, k):
        self.k = k
        self.silu_c = k.keep("silu_c", [P, 2, 8])
        self.gs = [find(k, "ada_w", 0, 3072), find(k, "w_ada_2", 0, 6144)]
        self.steps = [(which, i, g) for which in range(2) for i, g in enumerate(self.gs[which])]
        self.row_in = k.ctx.enter_context(k.nc.semaphore("mod_row_copied"))
        self.turned = k.ctx.enter_context(k.nc.semaphore("mod_row_turned"))
        self.columns_in = k.ctx.enter_context(k.nc.semaphore("mod_columns_copied"))

    def rows_buffer(self, ctx, name):
        self.rows = ctx.enter_context(self.k.nc.sbuf_tensor(name, [1, 2, 512], F32))

    def multiply(self, pe, n):
        which, _, g = self.steps[n]
        w = self.k.take(pe, g)
        if n > 1:
            pe.wait_ge(self.row_in, n - 1)
        for kk in range(KD):
            last = pe.matmul(self.k.bank[6 + n % 2][0:1, :], self.silu_c[:, which, kk:kk + 1], w[:, kk, :],
                             start=(kk == 0), stop=(kk == KD - 1))
        last.then_inc(self.k.used.sem, 1)
        self.k.used.n += 1

    def turn(self, pe, n):
        pe.wait_ge(self.row_in, n + 1)
        if n > 0:
            pe.wait_ge(self.columns_in, n)
        for b in range(4):
            last = pe.matmul(self.k.bank[5][:, b:b + 1], self.rows[:, n % 2, b * P:(b + 1) * P],
                             self.k.const("ones", 1, 1), start=True, stop=True)
        last.then_inc(self.turned, 1)

    def copy_row(self, act, n):
        act.wait_ge(self.k.used.sem, self.steps[n][2] + 1)
        if n > 1:
            act.wait_ge(self.turned, n - 1)
        act.activation(self.rows[:, n % 2, :], self.k.bank[6 + n % 2][0:1, :], ACT.Copy).then_inc(self.row_in, 1)

    def copy_columns(self, act, n):
        which, i, _ = self.steps[n]
        act.wait_ge(self.turned, n + 1)
        dst = (self.k.mod1, self.k.mod2)[which][:, 4 * i:4 * i + 4]
        act.activation(dst, self.k.bank[5][:, 0:4], ACT.Copy).then_inc(self.columns_in, 1)

    def on_tensor(self, pe, steps):
        for n in steps:
            self.multiply(pe, n)
            if n > steps[0]:
                self.turn(pe, n - 1)
        self.turn(pe, steps[-1])

    def on_scalar(self, act, steps):
        for n in steps:
            self.copy_row(act, n)
            if n > steps[0]:
                self.copy_columns(act, n - 1)
        self.copy_columns(act, steps[-1])


def load_stage(k):
    nc, d, m = k.nc, k.dram, k.modulation
    with ExitStack() as ctx:
        x = ctx.enter_context(nc.sbuf_tensor("x_rows", [P, NT, D], F32))
        m.rows_buffer(ctx, "mod1_rows")
        small = ctx.enter_context(nc.semaphore("small_loaded"))
        x_in = ctx.enter_context(nc.semaphore("x_loaded"))
        turned = ctx.enter_context(nc.semaphore("x_turned"))
        x_copied = ctx.enter_context(nc.semaphore("x_columns_copied"))
        silu = ctx.enter_context(nc.semaphore("silu_c_ready"))
        block = ctx.enter_context(nc.Block())
        steps = range(len(m.gs[0]))
        half = len(steps) // 2
        banks = 5

        @block.sync
        def _(sp):
            sp.dma_start(k.consts[:], d["consts"]).then_inc(small, 16)
            k.stream(sp, -1)
            sp.dma_start(x[:], d["x"].rearrange("(t p) d -> p t d", p=P)).then_inc(x_in, 16)
            k.stream(sp, m.gs[0][-1])

        @block.scalar
        def _(act):
            act.dma_start(k.cols[:], d["cols"]).then_inc(small, 16)
            act.dma_start(k.rows[:], d["rows"].to_broadcast([P, NROW])).then_inc(small, 16)
            act.wait_ge(small, 48)
            act.activation(m.silu_c[:, 0, :], k.col("c", 0, 8), ACT.Silu).then_inc(silu, 1)
            act.activation(m.silu_c[:, 1, :], k.col("c_2", 0, 8), ACT.Silu).then_inc(silu, 1)
            m.on_scalar(act, steps[:half])
            m.on_scalar(act, steps[half:])

        @block.tensor
        def _(pe):
            pe.wait_ge(small, 48)
            pe.wait_ge(silu, 2)
            m.on_tensor(pe, steps[:half])
            pe.wait_ge(x_in, 16)
            for i in range(KD):
                if i >= banks:
                    pe.wait_ge(x_copied, i - banks + 1)
                for t in range(NT):
                    last = nc.tensor.transpose(k.bank[i % banks][:, t * P:(t + 1) * P], x[:, t, i * P:(i + 1) * P],
                                               k.const("ident"))
                last.then_inc(turned, 1)
            m.on_tensor(pe, steps[half:])

        @block.vector
        def _(dve):
            for i in range(KD):
                dve.wait_ge(turned, i + 1)
                dve.tensor_copy(k.xT[:, i, :], k.bank[i % banks][:]).then_inc(x_copied, 1)
            dve.wait_ge(x_copied, KD)
            dve.wait_ge(small, 48)
            dve.wait_ge(m.columns_in, len(steps))
            post(dve, dve.tensor_tensor(k.mod1[:], k.mod1[:], k.col("ada_b", 0, 24), ALU.add), k.vstep)


def norm_stage(k, name, gain, mod, shift, scale):
    nc = k.nc
    act_squares, pool_scales = (1, 3, 5, 7), (2, 4, 7)
    with ExitStack() as ctx:
        sq = ctx.enter_context(nc.sbuf_tensor(f"{name}_squares", [P, KD, T], F32))
        rstd = ctx.enter_context(nc.sbuf_tensor(f"{name}_rstd", [P, T], F32))
        gs = ctx.enter_context(nc.sbuf_tensor(f"{name}_gain", [P, KD], F32))
        squared = Signal(ctx, nc, f"{name}_squared_by_vector")
        squared_a = Signal(ctx, nc, f"{name}_squared_by_scalar")
        summed = ctx.enter_context(nc.semaphore(f"{name}_summed"))
        rooted = Signal(ctx, nc, f"{name}_rooted")
        inverted = Signal(ctx, nc, f"{name}_rstd_ready")
        scaled = Signal(ctx, nc, f"{name}_scaled_by_vector")
        scaled_p = Signal(ctx, nc, f"{name}_scaled_by_gpsimd")
        block = ctx.enter_context(nc.Block())

        @block.vector
        def _(dve):
            for i in range(KD):
                if i not in act_squares:
                    dve.tensor_tensor(sq[:, i, :], k.xT[:, i, :], k.xT[:, i, :], ALU.mult).then_inc(squared.sem, 1)
            post(dve, dve.tensor_scalar(gs[:], mod[:, scale:scale + KD], 1.0, None, ALU.add), k.vstep)
            post(dve, dve.tensor_tensor(gs[:], gs[:], k.col(gain, 0, KD), ALU.mult), k.vstep)
            dve.wait_ge(rooted.sem, 1)
            post(dve, dve.reciprocal(rstd[:], rstd[:]), inverted)
            for i in range(KD):
                if i not in pool_scales:
                    dve.tensor_tensor(k.hT[:, i, :], k.xT[:, i, :], rstd[:], ALU.mult).then_inc(scaled.sem, 1)

        @block.gpsimd
        def _(pool):
            pool.wait_ge(inverted.sem, 1)
            for i in pool_scales:
                pool.tensor_tensor(k.hT[:, i, :], k.xT[:, i, :], rstd[:], ALU.mult).then_inc(scaled_p.sem, 1)

        @block.tensor
        def _(pe):
            for i in range(KD):
                if i in act_squares:
                    pe.wait_ge(squared_a.sem, act_squares.index(i) + 1)
                else:
                    pe.wait_ge(squared.sem, i // 2 + 1)
                last = pe.matmul(k.bank[0][:], k.const("ones"), sq[:, i, :], start=(i == 0), stop=(i == KD - 1))
            last.then_inc(summed, 1)

        @block.scalar
        def _(act):
            for i in act_squares:
                act.activation(sq[:, i, :], k.xT[:, i, :], ACT.Square).then_inc(squared_a.sem, 1)
            act.wait_ge(summed, 1)
            post(act, act.activation(rstd[:], k.bank[0][:], ACT.Sqrt, bias=k.const("eps"), scale=1.0 / D), rooted)
            by_vector = 0
            for i in range(KD):
                if i in pool_scales:
                    act.wait_ge(scaled_p.sem, pool_scales.index(i) + 1)
                else:
                    by_vector += 1
                    act.wait_ge(scaled.sem, by_vector)
                last = act.activation(k.hT[:, i, :], k.hT[:, i, :], ACT.Identity, bias=mod[:, shift + i:shift + i + 1],
                                      scale=gs[:, i:i + 1])
            post(act, last, k.astep)


class Projection:

    def __init__(self, k, ctx, name, plan, banks=range(8)):
        self.k, self.banks, self.plan = k, list(banks), plan
        self.done = ctx.enter_context(k.nc.semaphore(f"{name}_product"))
        self.freed = Signal(ctx, k.nc, f"{name}_freed")
        self.made = self.taken = 0
        self.there = []
        count = 0
        for kind, gs, _, _ in plan:
            outs = NT if kind == "rows" else max(1, k.chunks[gs[-1]][4] // P)
            for i in range(outs):
                if i == outs - 1:
                    self.there.append((k.used.sem, gs[-1] + 1))
                else:
                    count += 1
                    self.there.append((self.done, count))

    def _bank(self, pe):
        n = len(self.banks)
        if self.made >= n:
            pe.wait_ge(self.freed.sem, self.made - n + 1)
        self.made += 1
        return self.k.bank[self.banks[(self.made - 1) % n]]

    def run(self, pe, items=None):
        k = self.k
        for kind, gs, fixed, part in (self.plan if items is None else self.plan[items]):
            outs = NT if kind == "rows" else max(1, k.chunks[gs[-1]][4] // P)
            held = [None] * outs
            for which, g in enumerate(gs):
                w = k.take(pe, g)
                n = k.chunks[g][4]
                wide = min(n, P)
                for i in range(outs):
                    if which == 0:
                        held[i] = self._bank(pe)
                    for kk in range(KD):
                        flags = dict(start=(which == 0 and kk == 0), stop=(which == len(gs) - 1 and kk == KD - 1))
                        if kind == "rows":
                            last = pe.matmul(held[i][:, 0:n], fixed[:, kk, i * P:(i + 1) * P], w[:, kk, 0:n], **flags)
                        else:
                            last = pe.matmul(held[i][0:wide, :], w[:, kk, i * P:i * P + wide],
                                             fixed[:, which * KD + kk, :], **flags)
                    if i == outs - 1:
                        last.then_inc(k.used.sem, 1)
                        k.used.n += 1
                    elif which == len(gs) - 1:
                        last.then_inc(self.done, 1)

    def next(self, eng):
        sem, value = self.there[self.taken]
        eng.wait_ge(sem, value)
        self.taken += 1
        return self.k.bank[self.banks[(self.taken - 1) % len(self.banks)]]


def columns(gs, rhs):
    return [("columns", (g,), rhs, None) for g in gs]


def token_rows(gs, lhs):
    return [("rows", (g,), lhs, None) for g in gs]


def find(k, name, c0, n, k0=0):
    return [g for g, (w, c, kk, _, _) in enumerate(k.chunks) if w == name and c0 <= c < c0 + n and kk == k0]


def attention_projection_stage(k, t):
    nc = k.nc
    with ExitStack() as ctx:
        plan = token_rows(find(k, "w_in", Q0, 1024) + find(k, "w_in", KV0, 512) + find(k, "w_in", IX0, IDX_COLS), k.hT)
        plan += columns(find(k, "w_in", ZA0, 1024), k.hT)
        pj = Projection(k, ctx, "attention_in", plan)
        block = ctx.enter_context(nc.Block())

        @block.sync
        def _(sp):
            k.stream(sp, plan[-1][1][-1])

        @block.tensor
        def _(pe):
            pj.run(pe)

        @block.scalar
        def _(act):
            for c, (dst, c0, n) in enumerate([(t.q, 0, 512), (t.q, 512, 512), (t.kv, 0, 512), (t.ix, 0, IDX_COLS)]):
                for i in range(NT):
                    bank = pj.next(act)
                    post(act, act.activation(dst[:, i, c0:c0 + n], bank[:, 0:n], ACT.Copy), pj.freed)
            for j in range(8):
                bank = pj.next(act)
                post(act, act.activation(t.zT[:, j, :], bank[:], ACT.Silu), pj.freed)


def bc(ap, axis, shape):
    return ap.unsqueeze(axis).broadcast_to(shape)


def rotate(k, dve, x, cos, sin, tmp, half, heads):
    shape = [P, NT, heads, half]
    x1, x2 = x[:, :, :, 0:half], x[:, :, :, half:2 * half]
    c, s = bc(cos, 2, shape), bc(sin, 2, shape)
    a, b, e, f = (tmp[:, i, 0:NT * heads * half].rearrange("p (t h d) -> p t h d", t=NT, h=heads) for i in range(4))
    post(dve, dve.tensor_tensor(a, x1, c, ALU.mult), k.vstep)
    post(dve, dve.tensor_tensor(b, x2, s, ALU.mult), k.vstep)
    post(dve, dve.tensor_tensor(e, x2, c, ALU.mult), k.vstep)
    post(dve, dve.tensor_tensor(f, x1, s, ALU.mult), k.vstep)
    post(dve, dve.tensor_tensor(x1, a, b, ALU.subtract), k.vstep)
    post(dve, dve.tensor_tensor(x2, e, f, ALU.add), k.vstep)


def attention_rotary_stage(k, t):
    nc, d = k.nc, k.dram
    with ExitStack() as ctx:
        def sb(name, shape, dt=F32):
            return ctx.enter_context(nc.sbuf_tensor(name, shape, dt))

        pos = sb("positions", [P, NT], I32)
        posf = sb("positions_f", [P, NT])
        ang = sb("angle", [P, NT, 24])
        turns = sb("turns", [P, NT, 24])
        red = sb("angle_reduced", [P, 2, NT, 24])
        trig = sb("sin_cos", [P, 2, NT, 24])
        sq = k.merged[:].rearrange("p k t -> p (k t)")
        ssum = sb("head_sums", [P, 44])
        rstd = sb("head_rstd", [P, 44])
        mean = sb("idx_mean", [P, NT])
        tmp = sb("rope_products", [P, 4, NT * AH * 16])
        kdup = sb("idx_k_twice", [P, NT, 2, 64])
        m = k.modulation
        m.rows_buffer(ctx, "mod2_rows_a")
        first = len(m.gs[0])
        steps = range(first, first + len(m.gs[1]) // 2)
        pos_in = ctx.enter_context(nc.semaphore("positions_loaded"))
        reduced = Signal(ctx, nc, "angles_reduced")
        trig_ok = Signal(ctx, nc, "trig_ready")
        summed = Signal(ctx, nc, "head_squares_summed")
        rooted = Signal(ctx, nc, "head_roots")
        ready = Signal(ctx, nc, "rows_rotated")
        turned = ctx.enter_context(nc.semaphore("rows_turned"))
        block = ctx.enter_context(nc.Block())
        q4 = t.q[:].rearrange("p t (h d) -> p t h d", h=AH)
        k4 = t.kv[:, :, 0:256].rearrange("p t (h d) -> p t h d", h=AKV)
        qi4 = t.ix[:, :, 0:256].rearrange("p t (h d) -> p t h d", h=IH)
        ki = t.ix[:, :, 256:320]

        @block.sync
        def _(sp):
            sp.dma_start(pos[:], d["positions"]).then_inc(pos_in, 16)
            k.stream(sp, m.steps[steps[-1]][2])

        @block.vector
        def _(dve):
            def v(ins):
                post(dve, ins, k.vstep)

            dve.wait_ge(pos_in, 16)
            v(dve.tensor_copy(posf[:], pos[:]))
            v(dve.tensor_tensor(ang[:], bc(posf[:], 2, [P, NT, 24]), bc(k.const("inv_freq"), 1, [P, NT, 24]), ALU.mult))
            magic = 12582912.0
            hi, mid, lo = 6.28125, 0.0019340515136718750, 1.2556659146e-06
            hi_mid_lo = (hi, mid, lo)
            for w, quarter in ((0, 0.0), (1, 0.25)):
                v(dve.tensor_scalar(turns[:], ang[:], 1.0 / TWO_PI, quarter, ALU.mult, ALU.add))
                v(dve.tensor_scalar(turns[:], turns[:], magic, None, ALU.add))
                v(dve.tensor_scalar(turns[:], turns[:], magic, None, ALU.subtract))
                src = ang[:]
                for part in hi_mid_lo:
                    v(dve.scalar_tensor_tensor(red[:, w], turns[:], -part, src, ALU.mult, ALU.add))
                    src = red[:, w]
                if quarter:
                    v(dve.tensor_scalar(red[:, w], red[:, w], TWO_PI / 4, None, ALU.add))
                v(dve.tensor_scalar(red[:, w], red[:, w], 3.1415925, None, ALU.min))
                ins = dve.tensor_scalar(red[:, w], red[:, w], -3.1415925, None, ALU.max)
                post(dve, ins, reduced)

            v(dve.tensor_tensor(sq, t.q[:].rearrange("p t n -> p (t n)"), t.q[:].rearrange("p t n -> p (t n)"), ALU.mult))
            v(dve.tensor_reduce(ssum[:, 0:32], sq.rearrange("p (a d) -> p a d", d=P), AX, ALU.add))
            ksq = sq[:, 0:1024].rearrange("p (t h d) -> p t h d", t=NT, h=AKV)
            v(dve.tensor_tensor(ksq, k4, k4, ALU.mult))
            v(dve.tensor_reduce(ssum[:, 32:40], sq[:, 0:1024].rearrange("p (a d) -> p a d", d=P), AX, ALU.add))
            v(dve.tensor_reduce(mean[:], ki, AX, ALU.add))
            v(dve.tensor_scalar(mean[:], mean[:], 1.0 / 64, None, ALU.mult))
            v(dve.tensor_tensor(ki, ki, bc(mean[:], 2, [P, NT, 64]), ALU.subtract))
            kisq = sq[:, 0:256].rearrange("p (t d) -> p t d", t=NT)
            v(dve.tensor_tensor(kisq, ki, ki, ALU.mult))
            v(dve.tensor_reduce(ssum[:, 40:44], kisq, AX, ALU.add))
            post(dve, dve.tensor_scalar(ssum[:, 40:44], ssum[:, 40:44], 2.0, None, ALU.mult), summed)
            dve.wait_ge(rooted.sem, 1)
            v(dve.reciprocal(rstd[:], rstd[:]))
            for x4, at, heads, gain in ((q4, 0, AH, "q_norm_g"), (k4, 32, AKV, "k_norm_g")):
                r = rstd[:, at:at + NT * heads].rearrange("p (t h) -> p t h", t=NT)
                v(dve.tensor_tensor(x4, x4, bc(r, 3, [P, NT, heads, P]), ALU.mult))
                g = k.row(gain).unsqueeze(1).unsqueeze(1).broadcast_to([P, NT, heads, P])
                v(dve.tensor_tensor(x4, x4, g, ALU.mult))
            v(dve.tensor_tensor(ki, ki, bc(rstd[:, 40:44], 2, [P, NT, 64]), ALU.mult))
            v(dve.tensor_tensor(ki, ki, bc(k.row("idx_k_ln_g"), 1, [P, NT, 64]), ALU.mult))
            v(dve.tensor_tensor(ki, ki, bc(k.row("idx_k_ln_b"), 1, [P, NT, 64]), ALU.add))
            v(dve.tensor_scalar(t.ix[:, :, 320:324], t.ix[:, :, 320:324], 0.125 * 0.5, None, ALU.mult))
            dve.wait_ge(trig_ok.sem, 2)
            sa, ca = trig[:, 0, :, 0:16], trig[:, 1, :, 0:16]
            si, ci = trig[:, 0, :, 16:24], trig[:, 1, :, 16:24]
            rotate(k, dve, q4, ca, sa, tmp, 16, AH)
            rotate(k, dve, k4, ca, sa, tmp, 16, AKV)
            rotate(k, dve, qi4, ci, si, tmp, 8, IH)
            rotate(k, dve, ki.unsqueeze(2), ci, si, tmp, 8, 1)
            post(dve, dve.tensor_copy(kdup[:], bc(ki, 2, [P, NT, 2, 64])), ready)

        @block.scalar
        def _(act):
            for w in range(2):
                act.wait_ge(reduced.sem, w + 1)
                post(act, act.activation(trig[:, w], red[:, w], ACT.Sin), trig_ok)
            m.on_scalar(act, steps[:2])
            act.wait_ge(summed.sem, 1)
            post(act, act.activation(rstd[:], ssum[:], ACT.Sqrt, bias=k.const("eps"), scale=1.0 / P), rooted)
            m.on_scalar(act, steps[2:])
            for n, dst in enumerate([t.qT[:, h, :] for h in range(AH)] + [t.kT[:, h, :] for h in range(AKV)]
                                    + [t.qiT[:, h, :] for h in range(2)] + [t.kiT[:]]):
                act.wait_ge(turned, n + 1)
                post(act, act.activation(dst, k.bank[n % 8][:], ACT.Copy), k.astep)
                if n == 0:
                    t.turn_base = k.astep.n - 1

        @block.tensor
        def _(pe):
            srcs = [t.q[:, :, h * P:(h + 1) * P] for h in range(AH)]
            srcs += [t.kv[:, :, h * P:(h + 1) * P] for h in range(AKV)]
            srcs += [t.ix[:, :, h * P:(h + 1) * P] for h in range(2)]
            srcs += [kdup[:].rearrange("p t a d -> p t (a d)")]
            m.on_tensor(pe, steps[:2])
            m.on_tensor(pe, steps[2:])
            pe.wait_ge(ready.sem, 1)
            pe.wait_ge(m.columns_in, steps[-1] + 1)
            for n, src in enumerate(srcs):
                if n >= 8:
                    pe.wait_ge(k.astep.sem, t.turn_base + n - 7)
                for i in range(NT):
                    last = pe.transpose(k.bank[n % 8][:, i * P:(i + 1) * P], src[:, i, :], k.const("ident"))
                last.then_inc(turned, 1)


def selection_stage(k, t):
    nc = k.nc
    with ExitStack() as ctx:
        def sb(name, shape):
            return ctx.enter_context(nc.sbuf_tensor(name, shape, F32))

        relu = sb("relu_logits", [P, IH, T])
        score = sb("index_scores", [P, T])
        work = sb("scores_left", [P, T])
        m8 = sb("best8", [P, 8])
        eq = sb("tied", [P, T])
        seen = sb("ties_so_far", [P, T])
        need = sb("ties_to_keep", [P, 1])
        ones = sb("ones_wide", [P, T])
        m = k.modulation
        m.rows_buffer(ctx, "mod2_rows_b")
        first = len(m.gs[0]) + len(m.gs[1]) // 2
        steps = [range(first + 2 * i, first + 2 * i + 2) for i in range(3)]
        spread = ctx.enter_context(nc.semaphore("gate2_spread"))
        logits = ctx.enter_context(nc.semaphore("index_logits"))
        rect = Signal(ctx, nc, "index_relu")
        summed = Signal(ctx, nc, "index_scores_summed")
        block = ctx.enter_context(nc.Block())

        @block.sync
        def _(sp):
            k.stream(sp, m.gs[1][-1])

        @block.tensor
        def _(pe):
            for i in range(1, NT):
                w = (i + 1) * P
                if i > 1:
                    pe.wait_ge(rect.sem, IH * (i - 1))
                for h in range(IH):
                    p0 = 64 * (h % 2)
                    pe.matmul(k.bank[h][:, 0:w], t.qiT[p0:p0 + 64, h // 2, i * P:(i + 1) * P],
                              t.kiT[p0:p0 + 64, 0:w], start=True, stop=True).then_inc(logits, 1)
                m.on_tensor(pe, steps[i - 1])
            for half in range(2):
                last = pe.matmul(k.bank[4 + 2 * half][:], k.const("ones", P, 1), m.rows[:, half, :],
                                 start=True, stop=True)
            last.then_inc(spread, 1)

        @block.scalar
        def _(act):
            for i in range(1, NT):
                w = (i + 1) * P
                if i > 1:
                    act.wait_ge(summed.sem, i - 1)
                for h in range(IH):
                    act.wait_ge(logits, IH * (i - 1) + h + 1)
                    post(act, act.activation(relu[:, h, 0:w], k.bank[h][:, 0:w], ACT.Relu), rect)
                m.on_scalar(act, steps[i - 1])

        @block.vector
        def _(dve):
            def v(ins):
                post(dve, ins, k.vstep)

            v(dve.memset(ones[:], 1.0))
            v(dve.memset(t.madd[:], NEG))
            v(dve.tensor_copy(t.madd[:, 0, 0:P], k.const("causal_add")))
            for i in range(1, NT):
                w = (i + 1) * P
                for h in range(IH):
                    dve.wait_ge(rect.sem, IH * (i - 1) + h + 1)
                    wh = t.ix[:, i, 320 + h:321 + h]
                    if h == 0:
                        v(dve.tensor_scalar(score[:, 0:w], relu[:, h, 0:w], wh, None, ALU.mult))
                    else:
                        ins = dve.scalar_tensor_tensor(score[:, 0:w], relu[:, h, 0:w], wh, score[:, 0:w],
                                                       ALU.mult, ALU.add)
                        post(dve, ins, summed if h == IH - 1 else k.vstep)
                v(dve.tensor_tensor(score[:, w - P:w], score[:, w - P:w], k.const("causal_add"), ALU.add))
                for r in range(TOPK // 8):
                    src = score if r == 0 else work
                    v(dve.max(m8[:], src[:, 0:w]))
                    if r < TOPK // 8 - 1:
                        v(dve.match_replace(work[:, 0:w], m8[:], src[:, 0:w], -3.0e38))
                keep = t.madd[:, i, 0:w]
                v(dve.tensor_scalar(eq[:, 0:w], score[:, 0:w], m8[:, 7:8], None, ALU.is_equal))
                v(dve.tensor_scalar(keep, score[:, 0:w], m8[:, 7:8], None, ALU.is_gt))
                v(dve.tensor_reduce(need[:], keep, AX, ALU.add))
                v(dve.tensor_scalar(need[:], need[:], -1.0, float(TOPK), ALU.mult, ALU.add))
                v(dve.tensor_tensor_scan(seen[:, 0:w], ones[:, 0:w], eq[:, 0:w], 0.0, ALU.mult, ALU.add))
                v(dve.scalar_tensor_tensor(eq[:, 0:w], seen[:, 0:w], need[:], eq[:, 0:w], ALU.is_le, ALU.mult))
                v(dve.tensor_tensor(keep, keep, eq[:, 0:w], ALU.add))
                v(dve.tensor_scalar(keep, keep, 1.0, -NEG, ALU.subtract, ALU.mult))
            dve.wait_ge(m.columns_in, len(m.steps))
            v(dve.tensor_tensor(k.mod2[:], k.mod2[:], k.col("b_ada_2", 0, 48), ALU.add))
            dve.wait_ge(spread, 1)
            at, _w = ROW_AT["gate2_b"]
            for half in range(2):
                v(dve.tensor_tensor(k.gate2[:, half * 512:(half + 1) * 512], k.bank[4 + 2 * half][:],
                                    k.rows[:, at + half * 512:at + (half + 1) * 512], ALU.add))


def attention_stage(k, t):
    nc = k.nc
    scale = float(P) ** -0.5
    with ExitStack() as ctx:
        def sb(name, shape):
            return ctx.enter_context(nc.sbuf_tensor(name, shape, F32))

        s_at, p_at = [0, P, 3 * P, 6 * P], [0, 4 * P, 7 * P, 9 * P]
        s = sb("scores", [P, 2, 10 * P])
        pT = sb("probsT", [P, 2, 10 * P])
        top = sb("row_top", [P, 2, NT])
        den = sb("row_sum", [P, 2, NT])
        scored = ctx.enter_context(nc.semaphore("scores_made"))
        read = Signal(ctx, nc, "scores_read")
        topped = Signal(ctx, nc, "row_tops")
        exped = Signal(ctx, nc, "exps_made")
        normed = Signal(ctx, nc, "probs_normed")
        flipped = ctx.enter_context(nc.semaphore("probs_flipped"))
        copied = Signal(ctx, nc, "probsT_copied")
        valued = ctx.enter_context(nc.semaphore("values_mixed"))
        gated = Signal(ctx, nc, "outputs_gated")
        block = ctx.enter_context(nc.Block())
        place = [(4, 0), (5, 0), (6, 0), (6, 256)]

        @block.tensor
        def _(pe):
            def scores(h):
                for i in range(NT):
                    if h > 0:
                        pe.wait_ge(read.sem, NT * (h - 1) + i + 1)
                    w = (i + 1) * P
                    pe.matmul(k.bank[i][:, 0:w], t.qT[:, h, i * P:w], t.kT[:, h // 4, 0:w],
                              start=True, stop=True).then_inc(scored, 1)

            scores(0)
            scores(1)
            for h in range(AH):
                for i in range(NT):
                    pe.wait_ge(normed.sem, NT * h + i + 1)
                    if h > 0 and i == 0:
                        pe.wait_ge(copied.sem, NT * h)
                    for j in range(i + 1):
                        b, c = place[j]
                        c += (i - j) * P
                        last = pe.transpose(k.bank[b][:, c:c + P], s[:, h % 2, s_at[i] + j * P:s_at[i] + (j + 1) * P], k.const("ident"))
                last.then_inc(flipped, 1)
                if h + 2 < AH:
                    scores(h + 2)
                if h > 0:
                    pe.wait_ge(gated.sem, h)
                for j in range(NT):
                    pe.wait_ge(copied.sem, NT * h + j + 1)
                    v = t.kv[:, j, 256 + (h // 4) * P:256 + (h // 4 + 1) * P]
                    last = pe.matmul(k.bank[7][:, j * P:T], v, pT[:, h % 2, p_at[j]:p_at[j] + T - j * P], start=(j == 0), stop=(j == NT - 1))
                last.then_inc(valued, 1)

        @block.vector
        def _(dve):
            def softmax_in(h):
                for i in range(NT):
                    w = (i + 1) * P
                    dve.wait_ge(scored, NT * h + i + 1)
                    if h >= 2:
                        dve.wait_ge(flipped, h - 1)
                    post(dve, dve.scalar_tensor_tensor(s[:, h % 2, s_at[i]:s_at[i] + w], k.bank[i][:, 0:w], scale,
                                                       t.madd[:, i, 0:w], ALU.mult, ALU.add), read)
                    post(dve, dve.tensor_reduce(top[:, h % 2, i:i + 1], s[:, h % 2, s_at[i]:s_at[i] + w], AX, ALU.max, negate=True), topped)

            def softmax_out(h):
                dve.wait_ge(exped.sem, NT * (h + 1))
                post(dve, dve.reciprocal(den[:, h % 2, :], den[:, h % 2, :]), k.vstep)
                for i in range(NT):
                    w = (i + 1) * P
                    post(dve, dve.tensor_scalar(s[:, h % 2, s_at[i]:s_at[i] + w], s[:, h % 2, s_at[i]:s_at[i] + w], den[:, h % 2, i:i + 1],
                                                None, ALU.mult), normed)

            def gate(h):
                dve.wait_ge(valued, h + 1)
                post(dve, dve.tensor_tensor(t.oT[:, h, :], k.bank[7][:], t.zT[:, h, :], ALU.mult), gated)

            softmax_in(0)
            softmax_in(1)
            for h in range(AH):
                softmax_out(h)
                if h > 0:
                    gate(h - 1)
                if h + 2 < AH:
                    softmax_in(h + 2)
            gate(AH - 1)

        @block.scalar
        def _(act):
            def exps(h):
                for i in range(NT):
                    w = (i + 1) * P
                    act.wait_ge(topped.sem, NT * h + i + 1)
                    if h >= 2 and i == 0:
                        act.wait_ge(normed.sem, NT * (h - 1))
                    post(act, act.activation(s[:, h % 2, s_at[i]:s_at[i] + w], s[:, h % 2, s_at[i]:s_at[i] + w], ACT.Exp,
                                             bias=top[:, h % 2, i:i + 1], accum_out=den[:, h % 2, i:i + 1]), exped)

            exps(0)
            exps(1)
            for h in range(AH):
                act.wait_ge(flipped, h + 1)
                if h >= 2:
                    act.wait_ge(valued, h - 1)
                for j in range(NT):
                    b, c = place[j]
                    post(act, act.activation(pT[:, h % 2, p_at[j]:p_at[j] + T - j * P], k.bank[b][:, c:c + T - j * P], ACT.Copy), copied)
                if h + 2 < AH:
                    exps(h + 2)


def attention_out_stage(k, t):
    nc = k.nc
    with ExitStack() as ctx:
        plan = columns(find(k, "w_in", GA0, 1024), k.hT) + columns(find(k, "w_branch_att", 0, 1024), t.oT)
        pj = Projection(k, ctx, "attention_out", plan)
        block = ctx.enter_context(nc.Block())

        @block.sync
        def _(sp):
            k.stream(sp, plan[-1][1][-1])

        @block.tensor
        def _(pe):
            pj.run(pe)

        @block.scalar
        def _(act):
            for j in range(8):
                bank = pj.next(act)
                post(act, act.activation(t.merged[:, j, :], bank[:], ACT.Sigmoid), pj.freed)

        @block.vector
        def _(dve):
            pj.taken = 8
            dve.wait_ge(pj.freed.sem, 8)
            for j in range(8):
                bank = pj.next(dve)
                post(dve, dve.tensor_tensor(t.merged[:, j, :], bank[:], t.merged[:, j, :], ALU.mult), pj.freed)


class Part:
    pass


def attention_branch(k):
    with ExitStack() as ctx:
        def sb(name, shape):
            return ctx.enter_context(k.nc.sbuf_tensor(name, shape, F32))

        t = Part()
        t.merged = k.merged
        t.zT = sb("silu_zT", [P, 8, T])
        t.kv = sb("k_v_rows", [P, NT, 512])
        t.ix = sb("index_rows", [P, NT, IDX_COLS])
        t.kT, t.qiT, t.kiT = sb("kT", [P, AKV, T]), sb("index_qT", [P, 2, T]), sb("index_kT", [P, T])
        t.qT = sb("qT", [P, AH, T])
        with k.nc.sbuf_tensor("q_rows", [P, NT, D], F32) as t.q:
            attention_projection_stage(k, t)
            attention_rotary_stage(k, t)
        t.madd = sb("selected_add", [P, NT, T])
        selection_stage(k, t)
        t.oT = t.zT
        attention_stage(k, t)
        attention_out_stage(k, t)


def ssm_projection_stage(k, t):
    nc = k.nc
    with ExitStack() as ctx:
        def sb(name, shape):
            return ctx.enter_context(nc.sbuf_tensor(name, shape, F32))

        neg = sb("minus_abs", [SH, T])
        e = sb("exp_minus_abs", [SH, T])
        u = sb("one_plus_exp", [SH, T])
        ln = sb("log_one_plus", [SH, T])
        a_neg = sb("exp_a_log", [SH, 1])
        ones = sb("ones_row", [SH, P])
        dt_plan = columns(find(k, "w_in", DT0, 32), k.hT)
        plan = dt_plan + columns(find(k, "w_in", XBC0, 3072), k.hT)
        pj = Projection(k, ctx, "ssm_in", plan)
        first_tap = Signal(ctx, nc, "conv_first_tap")
        convolved = Signal(ctx, nc, "convolved")
        absed = Signal(ctx, nc, "dt_minus_abs")
        exped = Signal(ctx, nc, "dt_exps")
        summed = Signal(ctx, nc, "dt_one_plus")
        logged = Signal(ctx, nc, "dt_logs")
        block = ctx.enter_context(nc.Block())

        @block.sync
        def _(sp):
            k.stream(sp, plan[-1][1][-1])

        @block.tensor
        def _(pe):
            pj.run(pe)

        @block.scalar
        def _(act):
            post(act, act.activation(a_neg[:], k.col("a_log", 0, 1, SH), ACT.Exp), k.astep)
            a_done = k.astep.n
            t.a_done = a_done
            act.wait_ge(absed.sem, 1)
            post(act, act.activation(e[:], neg[:], ACT.Exp), exped)
            act.wait_ge(summed.sem, 1)
            post(act, act.activation(ln[:], u[:], ACT.Ln), logged)
            for j in range(24):
                sem, value = pj.there[j + 1]
                act.wait_ge(sem, value)
                post(act, act.activation(t.xbcT[:, j, :], k.bank[(j + 1) % 8][:], ACT.Identity,
                                         bias=k.col("conv_b", j), scale=k.col("conv_w", 3 * 24 + j)), first_tap)
                if j > 0:
                    act.wait_ge(convolved.sem, j)
                    post(act, act.activation(t.xbcT[:, j - 1, :], t.xbcT[:, j - 1, :], ACT.Silu), k.astep)
            act.wait_ge(convolved.sem, 24)
            post(act, act.activation(t.xbcT[:, 23, :], t.xbcT[:, 23, :], ACT.Silu), k.astep)

        @block.vector
        def _(dve):
            def v(ins):
                post(dve, ins, k.vstep)

            v(dve.memset(ones[:], 1.0))
            bank = pj.next(dve)
            v(dve.tensor_scalar(t.dtT[:], bank[0:SH, :], k.col("dt_bias", 0, 1, SH), None, ALU.add))
            dve.sem_inc(pj.freed.sem, 1)
            pj.freed.n += 1
            v(dve.tensor_scalar(neg[:], t.dtT[:], -1.0, None, ALU.mult))
            post(dve, dve.tensor_tensor(neg[:], neg[:], t.dtT[:], ALU.min), absed)
            dve.wait_ge(exped.sem, 1)
            post(dve, dve.tensor_scalar(u[:], e[:], 1.0, None, ALU.add), summed)
            v(dve.scalar_tensor_tensor(e[:], u[:], -1.0, e[:], ALU.add, ALU.subtract))
            v(dve.reciprocal(neg[:], u[:]))
            v(dve.scalar_tensor_tensor(e[:], e[:], -1.0, neg[:], ALU.mult, ALU.mult))
            dve.wait_ge(logged.sem, 1)
            v(dve.tensor_tensor(e[:], e[:], ln[:], ALU.add))
            v(dve.scalar_tensor_tensor(t.dtT[:], t.dtT[:], 0.0, e[:], ALU.max, ALU.add))
            dve.wait_ge(k.astep.sem, t.a_done)
            v(dve.tensor_scalar(e[:], t.dtT[:], a_neg[:], -1.0, ALU.mult, ALU.mult))
            for c in range(NT):
                cs = slice(c * P, (c + 1) * P)
                v(dve.tensor_tensor_scan(t.acumT[:, cs], ones[:], e[:, cs], 0.0, ALU.mult, ALU.add))
            for j in range(24):
                bank = pj.next(dve)
                dve.wait_ge(first_tap.sem, j + 1)
                for back in (1, 2, 3):
                    ins = dve.scalar_tensor_tensor(t.xbcT[:, j, back:T], bank[:, 0:T - back],
                                                   k.col("conv_w", (3 - back) * 24 + j), t.xbcT[:, j, back:T],
                                                   ALU.mult, ALU.add)
                    post(dve, ins, convolved if back == 3 else k.vstep)
                dve.sem_inc(pj.freed.sem, 1)
                pj.freed.n += 1


def ssd_stage(k, t):
    nc = k.nc
    HG = SH // SG
    with ExitStack() as ctx:
        def sb(name, shape):
            return ctx.enter_context(nc.sbuf_tensor(name, shape, F32))

        z = sb("silu_z_rows", [P, NT, 512])
        dt_row = sb("dt_rows", [P, NT, SH])
        ac_row = sb("acum_rows", [P, NT, SH])
        ea_row = sb("exp_acum_rows", [P, NT, SH])
        xs = sb("xs_rows", [P, 512])
        cbm = sb("cb_causal", [P, P])
        squares = ctx.enter_context(nc.sbuf_tensor("y_squares", [P, 512], mybir.dt.bfloat16))
        state = sb("state", [P, HG, SP_])
        b_row = sb("b_rows", [P, 2, P])
        xdt = sb("xs_dt", [P, 2, HG, SP_])
        xdec = sb("xs_dt_decay", [P, 2, HG, SP_])
        skip = sb("xs_skip", [P, HG, SP_])
        dec = sb("decay", [P, 2, HG, P])
        ends = sb("end_decays", [P, 2, 2, HG])
        y = sb("y_rows", [P, 2, 512])
        ss = sb("group_squares", [P, 2])
        diag = sb("rstd_diagonal", [P, 2, P])
        z_chunks = find(k, "w_in", ZS0, 2048)
        z_made = ctx.enter_context(nc.semaphore("z_product"))
        z_in = Signal(ctx, nc, "silu_z_ready")
        smalls = ctx.enter_context(nc.semaphore("dt_acum_turned"))
        small_in = Signal(ctx, nc, "dt_acum_rows")
        turned = ctx.enter_context(nc.semaphore("unit_turned"))
        bcast = ctx.enter_context(nc.semaphore("acum_spread"))
        rows_in = Signal(ctx, nc, "unit_rows")
        subbed = Signal(ctx, nc, "decay_exponents")
        exped = Signal(ctx, nc, "decays_made")
        scaled = Signal(ctx, nc, "xs_scaled")
        weighted = Signal(ctx, nc, "decay_weighted")
        side = Signal(ctx, nc, "skip_and_decayed")
        multiplied = ctx.enter_context(nc.semaphore("unit_products"))
        faded = Signal(ctx, nc, "state_faded")
        stated = Signal(ctx, nc, "state_updated")
        summed = Signal(ctx, nc, "unit_summed")
        gated = Signal(ctx, nc, "unit_gated")
        rooted = Signal(ctx, nc, "unit_root")
        normed = Signal(ctx, nc, "unit_rstd_diagonal")
        back = ctx.enter_context(nc.semaphore("unit_turned_back"))
        stored = Signal(ctx, nc, "unit_stored")
        block = ctx.enter_context(nc.Block())
        units = [(g, c) for g in range(SG) for c in range(NT)]
        last_unit = len(units) - 1
        full, tall = [P, HG, P], [P, HG, SP_]

        def fades(n):
            return n + 1 - (n + 1) // NT

        def z_there(n):
            g, c = units[n]
            return (k.used.sem, z_chunks[g] + 1) if c == NT - 1 else (z_made, n + 1 - g)


        @block.sync
        def _(sp):
            k.stream(sp, z_chunks[-1])

        @block.tensor
        def _(pe):
            def z_product(n):
                g, c = units[n]
                w = k.take(pe, z_chunks[g])
                if n > 0:
                    pe.wait_ge(z_in.sem, n)
                if n > 3:
                    pe.wait_ge(stored.sem, n - 3)
                for kk in range(KD):
                    last = pe.matmul(k.bank[7][:], k.hT[:, kk, c * P:(c + 1) * P], w[:, kk, :],
                                     start=(kk == 0), stop=(kk == KD - 1))
                sem, _ = z_there(n)
                last.then_inc(sem, 1)
                k.used.n += c == NT - 1

            def front(n):
                g, c = units[n]
                cs = slice(c * P, (c + 1) * P)
                if n > 0:
                    pe.wait_ge(weighted.sem, n)
                for h in range(HG):
                    sel = k.const("ident", SH, SH)[:, g * HG + h:g * HG + h + 1].broadcast_to([SH, P])
                    last = pe.matmul(k.bank[4 + h // 4][:, (h % 4) * P:(h % 4 + 1) * P], sel, t.acumT[:, cs],
                                     start=True, stop=True)
                last.then_inc(bcast, 1)
                for j in range(4):
                    pe.transpose(k.bank[0][:, j * P:(j + 1) * P], t.xbcT[:, 4 * g + j, cs], k.const("ident"))
                pe.transpose(k.bank[1][:, 0:P], t.xbcT[:, 16 + g, cs], k.const("ident"))
                pe.matmul(k.bank[1][:, P:2 * P], t.xbcT[:, 16 + g, cs], t.xbcT[:, 20 + g, cs],
                          start=True, stop=True).then_inc(turned, 1)

            def products(n):
                g, c = units[n]
                i = n % 2
                pe.wait_ge(weighted.sem, n + 1)
                pe.wait_ge(side.sem, n + 1)
                if n > 0:
                    pe.wait_ge(summed.sem, n)
                    pe.wait_ge(stated.sem, n)
                for h in range(HG):
                    out = k.bank[2][:, h * SP_:(h + 1) * SP_]
                    pe.matmul(out, dec[:, i, h, :], xdt[:, i, h, :], start=True, stop=False)
                    pe.matmul(out, k.const("ident"), skip[:, h, :], start=False, stop=True)
                pe.matmul(k.bank[3][:], t.xbcT[:, 20 + g, c * P:(c + 1) * P], state[:].rearrange("p h d -> p (h d)"),
                          start=True, stop=True)
                pe.matmul(k.bank[6][:], b_row[:, i, :], xdec[:, i].rearrange("p h d -> p (h d)"),
                          start=True, stop=True).then_inc(multiplied, 1)

            def turn_back(n):
                pe.wait_ge(normed.sem, n + 1)
                pe.wait_ge(z_in.sem, min(n + 4, len(units)))
                if n > 0:
                    pe.wait_ge(stored.sem, n)
                for j in range(4):
                    last = pe.matmul(k.bank[7][:, j * P:(j + 1) * P], y[:, n % 2, j * P:(j + 1) * P],
                                     diag[:, n % 2, :], start=True, stop=True)
                last.then_inc(back, 1)

            for c in range(NT):
                pe.transpose(k.bank[4][:, c * 64:c * 64 + SH], t.dtT[:, c * P:(c + 1) * P], k.const("ident", SH, SH))
                last = pe.transpose(k.bank[4][:, c * 64 + SH:c * 64 + 64], t.acumT[:, c * P:(c + 1) * P],
                                    k.const("ident", SH, SH))
            last.then_inc(smalls, 1)
            pe.wait_ge(small_in.sem, 2)
            z_product(0)
            front(0)
            z_product(1)
            for n in range(len(units)):
                if n < last_unit:
                    front(n + 1)
                if n > 1:
                    turn_back(n - 2)
                products(n)
                if n + 2 <= last_unit:
                    z_product(n + 2)
            turn_back(last_unit - 1)
            turn_back(last_unit)

        @block.scalar
        def _(act):
            def a(ins):
                post(act, ins, k.astep)

            def silu_z(n):
                act.wait_ge(*z_there(n))
                if n >= NT:
                    act.wait_ge(gated.sem, n - NT + 1)
                post(act, act.activation(z[:, n % NT, :], k.bank[7][:], ACT.Silu), z_in)

            def front(n):
                act.wait_ge(turned, n + 1)
                if n > 1:
                    act.wait_ge(multiplied, n - 1)
                a(act.activation(b_row[:, n % 2, :], k.bank[1][:, 0:P], ACT.Copy))
                if n > 0:
                    act.wait_ge(side.sem, n)
                post(act, act.activation(xs[:], k.bank[0][:], ACT.Copy), rows_in)
                act.wait_ge(subbed.sem, n + 1)
                a(act.activation(ends[:, n % 2], ends[:, n % 2], ACT.Exp))
                post(act, act.activation(dec[:, n % 2], dec[:, n % 2], ACT.Exp), exped)

            def root(n):
                act.wait_ge(gated.sem, n + 1)
                if n > 1:
                    act.wait_ge(normed.sem, n - 1)
                mine = ss[:, n % 2:n % 2 + 1]
                a(act.activation(squares[:], y[:, n % 2, :], ACT.Square, accum_out=mine))
                a(act.activation(mine, mine, ACT.Ln, bias=k.const("eps"), scale=1.0 / 512))
                post(act, act.activation(mine, mine, ACT.Exp, scale=-0.5), rooted)

            def store(n):
                g, c = units[n]
                act.wait_ge(back, n + 1)
                for j in range(4):
                    ins = act.activation(t.xbcT[:, 4 * g + j, c * P:(c + 1) * P], k.bank[7][:, j * P:(j + 1) * P],
                                         ACT.Copy, scale=k.col("ssm_norm_g", 4 * g + j))
                    if j == 3:
                        post(act, ins, stored)

            act.wait_ge(smalls, 1)
            v4 = k.bank[4][:, 0:256].rearrange("p (c x) -> p c x", c=NT)
            a(act.activation(dt_row[:], v4[:, :, 0:SH], ACT.Copy))
            post(act, act.activation(ac_row[:], v4[:, :, SH:64], ACT.Copy), small_in)
            post(act, act.activation(ea_row[:], v4[:, :, SH:64], ACT.Exp), small_in)
            silu_z(0)
            front(0)
            silu_z(1)
            for n in range(len(units)):
                if n < last_unit:
                    front(n + 1)
                if n > 1:
                    store(n - 2)
                if n > 0:
                    root(n - 1)
                if n + 2 <= last_unit:
                    silu_z(n + 2)
            root(last_unit)
            store(last_unit - 1)
            store(last_unit)

        @block.vector
        def _(dve):
            def v(ins):
                post(dve, ins, k.vstep)

            def front(n):
                g, c = units[n]
                i, hs = n % 2, slice(g * HG, (g + 1) * HG)
                dve.wait_ge(bcast, n + 1)
                if n > 1:
                    dve.wait_ge(multiplied, n - 1)
                    dve.wait_ge(faded.sem, fades(n - 2))
                spread = [k.bank[4 + b][:].rearrange("p (h l) -> p h l", h=4) for b in range(2)]
                for b in range(2):
                    last = dve.tensor_copy(ends[:, i, 1, 4 * b:4 * b + 4], spread[b][:, :, P - 1])
                v(last)
                v(dve.tensor_tensor(ends[:, i, 0, :], ends[:, i, 1, :], ac_row[:, c, hs], ALU.subtract))
                for h in range(HG):
                    last = dve.tensor_scalar(dec[:, i, h, :], spread[h // 4][:, h % 4, :],
                                             ac_row[:, c, g * HG + h:g * HG + h + 1], 0.0, ALU.subtract, ALU.min)
                post(dve, last, subbed)
                dve.wait_ge(rows_in.sem, n + 1)
                dve.tensor_tensor(cbm[:], k.bank[1][:, P:2 * P], k.const("s_le_l"), ALU.mult)
                x3 = xs[:].rearrange("p (h d) -> p h d", h=HG)
                post(dve, dve.tensor_tensor(xdt[:, i], x3, bc(dt_row[:, c, hs], 2, tall), ALU.mult), scaled)
                dve.wait_ge(exped.sem, n + 1)
                post(dve, dve.tensor_tensor(dec[:, i], dec[:, i], bc(cbm[:], 1, full), ALU.mult), weighted)

            def sums(n):
                g, c = units[n]
                dve.wait_ge(multiplied, n + 1)
                if c == NT - 1:
                    post(dve, dve.memset(state[:], 0.0), stated)
                else:
                    dve.wait_ge(faded.sem, fades(n))
                    s3 = k.bank[6][:].rearrange("p (h d) -> p h d", h=HG)
                    post(dve, dve.tensor_tensor(state[:], state[:], s3, ALU.add), stated)
                if n > 1:
                    dve.wait_ge(back, n - 1)
                off = k.bank[3][:].rearrange("p (h d) -> p h d", h=HG)
                y3 = y[:, n % 2].rearrange("p (h d) -> p h d", h=HG)
                v(dve.tensor_tensor(y3, off, bc(ea_row[:, c, g * HG:(g + 1) * HG], 2, tall), ALU.mult))
                post(dve, dve.tensor_tensor(y[:, n % 2], y[:, n % 2], k.bank[2][:], ALU.add), summed)

            def norm(n):
                dve.wait_ge(rooted.sem, n + 1)
                if n > 1:
                    dve.wait_ge(back, n - 1)
                post(dve, dve.tensor_scalar(diag[:, n % 2, :], k.const("ident"), ss[:, n % 2:n % 2 + 1], None,
                                            ALU.mult), normed)

            dve.wait_ge(small_in.sem, 2)
            v(dve.memset(state[:], 0.0))
            front(0)
            for n in range(len(units)):
                if n < last_unit:
                    front(n + 1)
                sums(n)
                if n > 0:
                    norm(n - 1)
            norm(last_unit)

        @block.gpsimd
        def _(pool):
            def p(ins):
                post(pool, ins, k.gstep)

            def front(n):
                g, c = units[n]
                i, hs = n % 2, slice(g * HG, (g + 1) * HG)
                pool.wait_ge(rows_in.sem, n + 1)
                if n > 0:
                    pool.wait_ge(multiplied, n)
                x3 = xs[:].rearrange("p (h d) -> p h d", h=HG)
                pool.tensor_tensor(skip[:], x3, bc(k.row("d_skip")[:, hs], 2, tall), ALU.mult)
                pool.wait_ge(scaled.sem, n + 1)
                pool.wait_ge(exped.sem, n + 1)
                post(pool, pool.tensor_tensor(xdec[:, i], xdt[:, i], bc(ends[:, i, 0, :], 2, tall), ALU.mult), side)

            def fade(n):
                pool.wait_ge(multiplied, n + 1)
                if n > 0:
                    pool.wait_ge(stated.sem, n)
                post(pool, pool.tensor_tensor(state[:], state[:], bc(ends[:, n % 2, 1, :], 2, tall), ALU.mult), faded)

            def gate(n):
                pool.wait_ge(summed.sem, n + 1)
                pool.wait_ge(z_in.sem, n + 1)
                post(pool, pool.tensor_tensor(y[:, n % 2], y[:, n % 2], z[:, units[n][1], :], ALU.mult), gated)

            front(0)
            for n in range(len(units)):
                if n < last_unit:
                    front(n + 1)
                if units[n][1] < NT - 1:
                    fade(n)
                gate(n)


def ssm_out_stage(k, t):
    nc = k.nc
    with ExitStack() as ctx:
        sig = ctx.enter_context(nc.sbuf_tensor("ssm_gate", [P, 8, T], F32))
        term = ctx.enter_context(nc.sbuf_tensor("ssm_term", [P, T], F32))
        plan = columns(find(k, "w_in", GS0, 1024), k.hT)
        for c in (0, 512):
            pair = (find(k, "w_branch_ssm", c, 512)[0], find(k, "w_branch_ssm", c, 512, D)[0])
            plan.append(("columns", pair, t.xbcT, None))
        n_branch = len(plan)
        plan += columns(find(k, "w_out", 0, 1024), k.merged)
        pj = Projection(k, ctx, "ssm_out", plan)
        merged = Signal(ctx, nc, "branches_merged")
        block = ctx.enter_context(nc.Block())

        @block.sync
        def _(sp):
            k.stream(sp, plan[-1][1][-1])

        @block.tensor
        def _(pe):
            pj.run(pe, slice(0, n_branch))
            pe.wait_ge(merged.sem, 8)
            pj.run(pe, slice(n_branch, None))

        @block.scalar
        def _(act):
            for j in range(8):
                bank = pj.next(act)
                post(act, act.activation(sig[:, j, :], bank[:], ACT.Sigmoid), pj.freed)

        @block.vector
        def _(dve):
            dve.wait_ge(pj.freed.sem, 8)
            for j in range(8):
                bank = pj.next(dve)
                post(dve, dve.tensor_tensor(term[:], bank[:], sig[:, j, :], ALU.mult), pj.freed)
                post(dve, dve.tensor_tensor(k.merged[:, j, :], k.merged[:, j, :], term[:], ALU.add), merged)
            for j in range(8):
                bank = pj.next(dve)
                post(dve, dve.scalar_tensor_tensor(k.xT[:, j, :], bank[:], k.mod1[:, 16 + j:17 + j], k.xT[:, j, :],
                                                   ALU.mult, ALU.add), pj.freed)


def ssm_branch(k):
    with ExitStack() as ctx:
        def sb(name, shape):
            return ctx.enter_context(k.nc.sbuf_tensor(name, shape, F32))

        t = Part()
        t.xbcT = sb("xbcT", [P, 24, T])
        t.dtT, t.acumT = sb("dtT", [SH, T]), sb("acumT", [SH, T])
        ssm_projection_stage(k, t)
        ssd_stage(k, t)
        ssm_out_stage(k, t)


def second_projection_stage(k, t):
    nc, d = k.nc, k.dram
    with ExitStack() as ctx:
        def sb(name, shape):
            return ctx.enter_context(nc.sbuf_tensor(name, shape, F32))

        xa = sb("a_raw", [DH, T])
        neg = sb("a_minus_abs", [DH, T])
        e = sb("a_exp_minus_abs", [DH, T])
        u = sb("a_one_plus_exp", [DH, T])
        ln = sb("a_log_one_plus", [DH, T])
        a_neg = sb("dn_exp_a_log", [DH, 1])
        ones = sb("dn_ones_row", [DH, CH])
        raw = sb("conv_raw", [P, 2, T])
        sq = sb("band_squares", [P, NT * 512])
        ssum = sb("band_sums", [P, 2, NT * BH])
        rb = sb("rel_bias_padded", [BH, 384])
        bias_in = ctx.enter_context(nc.semaphore("rel_bias_in"))
        padded = Signal(ctx, nc, "rel_bias_padded_ready")
        stored = ctx.enter_context(nc.semaphore("rel_bias_stored"))
        squares_summed = Signal(ctx, nc, "band_squares_summed")
        rooted = Signal(ctx, nc, "band_roots")
        ba = find(k, "w_in_2", BA0, 8)[0]
        plan = token_rows(find(k, "w_in_2", QA0, 512) + find(k, "w_in_2", KA0, 512) + find(k, "w_in_2", VA0, 512), k.hT)
        plan += columns(find(k, "w_in_2", QKV0, 1536), k.hT) + token_rows(find(k, "w_in_2", ZB0, 512), k.hT)
        pj = Projection(k, ctx, "second_in", plan, banks=range(2, 8))
        tapped = Signal(ctx, nc, "dn_first_tap")
        convolved = Signal(ctx, nc, "dn_convolved")
        gates_made = ctx.enter_context(nc.semaphore("dn_gate_products"))
        absed = Signal(ctx, nc, "a_minus_abs_ready")
        exped = Signal(ctx, nc, "a_exps")
        summed = Signal(ctx, nc, "a_one_plus")
        logged = Signal(ctx, nc, "a_logs")
        sig_ok = Signal(ctx, nc, "beta_ready")
        block = ctx.enter_context(nc.Block())

        @block.sync
        def _(sp):
            sp.dma_start(rb[:, 127:384], d["rel_bias_reversed"]).then_inc(bias_in, 16)
            k.stream(sp, plan[-1][1][-1])
            sp.wait_ge(padded.sem, 1)
            rel = t.rel_scratch
            sp.dma_start(rel, rb[:]).then_inc(stored, 16)
            sp.wait_ge(stored, 16)
            near = bass.AP(tensor=rel.tensor, offset=0, ap=[[1, P], [384, BH], [1, 256]])
            sp.dma_start(t.near[:], near).then_inc(t.near_in, 16)

        @block.tensor
        def _(pe):
            w = k.take(pe, ba)
            for which in range(2):
                for kk in range(KD):
                    last = pe.matmul(k.bank[which][0:DH, :], w[:, kk, which * DH:(which + 1) * DH], k.hT[:, kk, :],
                                     start=(kk == 0), stop=(kk == KD - 1))
                last.then_inc(gates_made if which == 0 else k.used.sem, 1)
            k.used.n += 1
            pj.run(pe)

        @block.scalar
        def _(act):
            act.wait_ge(gates_made, 1)
            post(act, act.activation(t.betaT[:], k.bank[0][0:DH, :], ACT.Sigmoid), k.astep)
            post(act, act.activation(a_neg[:], k.col("dn_a_log_2", 0, 1, DH), ACT.Exp), sig_ok)
            act.wait_ge(absed.sem, 1)
            post(act, act.activation(e[:], neg[:], ACT.Exp), exped)
            act.wait_ge(summed.sem, 1)
            post(act, act.activation(ln[:], u[:], ACT.Ln), logged)
            for dst in (t.qa, t.ka, t.va):
                for i in range(NT):
                    bank = pj.next(act)
                    post(act, act.activation(dst[:, i, :], bank[:], ACT.Copy), pj.freed)
                if dst is t.ka:
                    act.wait_ge(squares_summed.sem, 2)
                    post(act, act.activation(ssum[:], ssum[:], ACT.Sqrt, bias=k.const("eps"), scale=1.0 / BD), rooted)
            for j in range(12):
                bank = pj.next(act)
                if j >= 2:
                    act.wait_ge(convolved.sem, j - 1)
                post(act, act.activation(raw[:, j % 2, :], bank[:], ACT.Copy), pj.freed)
                post(act, act.activation(t.dT[:, j, :], raw[:, j % 2, :], ACT.Copy,
                                         scale=k.col("dn_conv_w_2", 3 * 12 + j)), tapped)
                if j > 0:
                    act.wait_ge(convolved.sem, j)
                    post(act, act.activation(t.dT[:, j - 1, :], t.dT[:, j - 1, :], ACT.Silu), k.astep)
            act.wait_ge(convolved.sem, 12)
            post(act, act.activation(t.dT[:, 11, :], t.dT[:, 11, :], ACT.Silu), k.astep)
            for i in range(NT):
                bank = pj.next(act)
                post(act, act.activation(t.zb[:, i, :], bank[:], ACT.Silu), pj.freed)

        @block.vector
        def _(dve):
            def v(ins):
                post(dve, ins, k.vstep)

            v(dve.memset(ones[:], 1.0))
            dve.wait_ge(bias_in, 16)
            post(dve, dve.tensor_copy(rb[:, 0:127], rb[:, 127:128].broadcast_to([BH, 127])), padded)
            dve.wait_ge(k.used.sem, ba + 1)
            v(dve.tensor_scalar(xa[:], k.bank[1][0:DH, :], k.col("dn_dt_bias_2", 0, 1, DH), None, ALU.add))
            v(dve.tensor_scalar(neg[:], xa[:], -1.0, None, ALU.mult))
            post(dve, dve.tensor_tensor(neg[:], neg[:], xa[:], ALU.min), absed)
            dve.wait_ge(exped.sem, 1)
            post(dve, dve.tensor_scalar(u[:], e[:], 1.0, None, ALU.add), summed)
            v(dve.scalar_tensor_tensor(e[:], u[:], -1.0, e[:], ALU.add, ALU.subtract))
            v(dve.reciprocal(neg[:], u[:]))
            v(dve.scalar_tensor_tensor(e[:], e[:], -1.0, neg[:], ALU.mult, ALU.mult))
            dve.wait_ge(logged.sem, 1)
            v(dve.tensor_tensor(e[:], e[:], ln[:], ALU.add))
            v(dve.scalar_tensor_tensor(xa[:], xa[:], 0.0, e[:], ALU.max, ALU.add))
            dve.wait_ge(sig_ok.sem, 1)
            v(dve.tensor_scalar(e[:], xa[:], a_neg[:], -1.0, ALU.mult, ALU.mult))
            for c in range(T // CH):
                cs = slice(c * CH, (c + 1) * CH)
                v(dve.tensor_tensor_scan(t.gcT[:, cs], ones[:], e[:, cs], 0.0, ALU.mult, ALU.add))
            for w, x in enumerate((t.qa, t.ka)):
                dve.wait_ge(pj.freed.sem, NT * (w + 1))
                flat = x[:].rearrange("p t n -> p (t n)")
                v(dve.tensor_tensor(sq[:], flat, flat, ALU.mult))
                ins = dve.tensor_reduce(ssum[:, w, :], sq[:].rearrange("p (a d) -> p a d", d=BD), AX, ALU.add)
                post(dve, ins, squares_summed)
            dve.wait_ge(rooted.sem, 1)
            v(dve.reciprocal(ssum[:], ssum[:]))
            for w, (x, gain) in enumerate(((t.qa, "attn_q_gain_2"), (t.ka, "attn_k_gain_2"))):
                x3 = x[:].rearrange("p t (h d) -> p (t h) d", h=BH)
                v(dve.tensor_tensor(x3, x3, bc(ssum[:, w, :], 2, [P, NT * BH, BD]), ALU.mult))
                v(dve.tensor_tensor(x3, x3, bc(k.row(gain), 1, [P, NT * BH, BD]), ALU.mult))
            for j in range(12):
                dve.wait_ge(tapped.sem, j + 1)
                for b in (1, 2, 3):
                    ins = dve.scalar_tensor_tensor(t.dT[:, j, b:T], raw[:, j % 2, 0:T - b],
                                                   k.col("dn_conv_w_2", (3 - b) * 12 + j), t.dT[:, j, b:T],
                                                   ALU.mult, ALU.add)
                    post(dve, ins, convolved if b == 3 else k.vstep)


def band_setup_stage(k, t):
    nc = k.nc
    with ExitStack() as ctx:
        turned = ctx.enter_context(nc.semaphore("band_turned"))
        turned_in = Signal(ctx, nc, "band_turned_in")
        flipped = ctx.enter_context(nc.semaphore("near_bias_flipped"))
        flipped_in = Signal(ctx, nc, "near_bias_flipped_in")
        block = ctx.enter_context(nc.Block())

        @block.tensor
        def _(pe):
            for n in range(8):
                src = (t.qa, t.ka)[n // 4]
                for i in range(NT):
                    last = pe.transpose(k.bank[n][:, i * P:(i + 1) * P], src[:, i, (n % 4) * P:(n % 4 + 1) * P],
                                        k.const("ident"))
                last.then_inc(turned, 1)
            pe.wait_ge(turned_in.sem, 4)
            pe.wait_ge(t.near_in, 16)
            for j in range(4):
                last = pe.matmul(k.bank[j][:], k.const("flip"), t.near[:, 2 * j:2 * j + 2, :].rearrange("p h s -> p (h s)"),
                                 start=True, stop=True)
            last.then_inc(flipped, 1)

        @block.scalar
        def _(act):
            for n in range(8):
                dst = (t.qaT, t.kaT)[n // 4][:, n % 4, :]
                act.wait_ge(turned, n + 1)
                act.activation(dst, k.bank[n][:], ACT.Copy).then_inc(turned_in.sem, 1)
            turned_in.n += 8
            act.wait_ge(turned_in.sem, 8)

        @block.vector
        def _(dve):
            dve.wait_ge(flipped, 1)
            for j in range(4):
                mine = t.near[:, 2 * j:2 * j + 2, :]
                post(dve, dve.tensor_copy(mine, k.bank[j][:].rearrange("p (h s) -> p h s", h=2)), flipped_in)
            diag = t.near[:, :, P:2 * P]
            post(dve, dve.tensor_tensor(diag, diag, bc(k.const("band_add"), 1, [P, BH, P]), ALU.add), k.vstep)


def band_attention_stage(k, t):
    nc = k.nc
    scale = float(BD) ** -0.5
    with ExitStack() as ctx:
        def sb(name, shape):
            return ctx.enter_context(nc.sbuf_tensor(name, shape, F32))

        s_at, p_at = [0, P, 3 * P, 6 * P], [0, 4 * P, 7 * P, 9 * P]
        s = sb("band_scores", [P, 2, 10 * P])
        pT = sb("band_probsT", [P, 2, 10 * P])
        top = sb("band_top", [P, 2, NT])
        den = sb("band_sum", [P, 2, NT])
        scored = ctx.enter_context(nc.semaphore("band_scores_made"))
        read = Signal(ctx, nc, "band_scores_read")
        topped = Signal(ctx, nc, "band_tops")
        exped = Signal(ctx, nc, "band_exps")
        flipped = ctx.enter_context(nc.semaphore("band_probs_flipped"))
        copied = Signal(ctx, nc, "band_probsT_copied")
        valued = ctx.enter_context(nc.semaphore("band_values_mixed"))
        normed = Signal(ctx, nc, "band_outputs_normed")
        block = ctx.enter_context(nc.Block())
        place = [(4, 0), (5, 0), (6, 0), (6, 256)]

        @block.tensor
        def _(pe):
            def scores(h):
                p0 = BD * (h % 2)
                for i in range(NT):
                    if h > 0:
                        pe.wait_ge(read.sem, NT * (h - 1) + i + 1)
                    w = (i + 1) * P
                    pe.matmul(k.bank[i][:, 0:w], t.qaT[p0:p0 + BD, h // 2, i * P:w], t.kaT[p0:p0 + BD, h // 2, 0:w],
                              start=True, stop=True).then_inc(scored, 1)

            scores(0)
            scores(1)
            for h in range(BH):
                for i in range(NT):
                    pe.wait_ge(exped.sem, NT * h + i + 1)
                    if h > 0 and i == 0:
                        pe.wait_ge(copied.sem, NT * h)
                    for j in range(i + 1):
                        b, c = place[j]
                        c += (i - j) * P
                        last = pe.transpose(k.bank[b][:, c:c + P], s[:, h % 2, s_at[i] + j * P:s_at[i] + (j + 1) * P],
                                            k.const("ident"))
                last.then_inc(flipped, 1)
                if h + 2 < BH:
                    scores(h + 2)
                if h > 0:
                    pe.wait_ge(normed.sem, h)
                pe.wait_ge(copied.sem, NT * (h + 1))
                for i in range(NT):
                    for j in range(i + 1):
                        last = pe.matmul(k.bank[7][:, i * BD:(i + 1) * BD],
                                         pT[:, h % 2, p_at[j] + (i - j) * P:p_at[j] + (i - j + 1) * P],
                                         t.va[:, j, h * BD:(h + 1) * BD], start=(j == 0), stop=(j == i))
                last.then_inc(valued, 1)

        @block.vector
        def _(dve):
            def softmax_in(h):
                for i in range(NT):
                    w = (i + 1) * P
                    dve.wait_ge(scored, NT * h + i + 1)
                    if h >= 2:
                        dve.wait_ge(flipped, h - 1)
                    at = s_at[i]
                    if i >= 2:
                        post(dve, dve.tensor_scalar(s[:, h % 2, at:at + w - 2 * P], k.bank[i][:, 0:w - 2 * P], scale,
                                                    k.row("rel_far")[:, h:h + 1], ALU.mult, ALU.add), k.vstep)
                    nw = min(w, 2 * P)
                    post(dve, dve.scalar_tensor_tensor(s[:, h % 2, at + w - nw:at + w], k.bank[i][:, w - nw:w], scale,
                                                       t.near[:, h, 2 * P - nw:2 * P], ALU.mult, ALU.add), read)
                    post(dve, dve.tensor_reduce(top[:, h % 2, i:i + 1], s[:, h % 2, at:at + w], AX, ALU.max,
                                                negate=True), topped)

            def out(h):
                dve.wait_ge(valued, h + 1)
                post(dve, dve.reciprocal(den[:, h % 2, :], den[:, h % 2, :]), k.vstep)
                o3 = k.bank[7][:, 0:NT * BD].rearrange("p (t d) -> p t d", t=NT)
                post(dve, dve.tensor_tensor(t.oa[:, :, h * BD:(h + 1) * BD], o3, bc(den[:, h % 2, :], 2, [P, NT, BD]),
                                            ALU.mult), normed)

            softmax_in(0)
            softmax_in(1)
            for h in range(BH):
                if h + 2 < BH:
                    softmax_in(h + 2)
                out(h)

        @block.scalar
        def _(act):
            def exps(h):
                for i in range(NT):
                    w = (i + 1) * P
                    act.wait_ge(topped.sem, NT * h + i + 1)
                    if h >= 2 and i == 0:
                        act.wait_ge(normed.sem, h - 1)
                    post(act, act.activation(s[:, h % 2, s_at[i]:s_at[i] + w], s[:, h % 2, s_at[i]:s_at[i] + w], ACT.Exp,
                                             bias=top[:, h % 2, i:i + 1], accum_out=den[:, h % 2, i:i + 1]), exped)

            exps(0)
            exps(1)
            for h in range(BH):
                act.wait_ge(flipped, h + 1)
                if h >= 2:
                    act.wait_ge(valued, h - 1)
                for j in range(NT):
                    b, c = place[j]
                    post(act, act.activation(pT[:, h % 2, p_at[j]:p_at[j] + T - j * P], k.bank[b][:, c:c + T - j * P],
                                             ACT.Copy), copied)
                if h + 2 < BH:
                    exps(h + 2)


def delta_setup_stage(k, t):
    nc = k.nc
    with ExitStack() as ctx:
        def sb(name, shape):
            return ctx.enter_context(nc.sbuf_tensor(name, shape, F32))

        sq = sb("dn_squares", [P, 2, T])
        rstd = sb("dn_rstd", [P, 2, T])
        last_row = sb("dn_chunk_end_rows", [P, NT, DH])
        squared = Signal(ctx, nc, "dn_squared")
        summed = ctx.enter_context(nc.semaphore("dn_squares_summed"))
        rooted = Signal(ctx, nc, "dn_roots")
        scaled = Signal(ctx, nc, "dn_columns_scaled")
        spread = ctx.enter_context(nc.semaphore("dn_sums_spread"))
        spread_in = Signal(ctx, nc, "dn_sums_in")
        turned = ctx.enter_context(nc.semaphore("dn_turned"))
        rows_in = Signal(ctx, nc, "dn_rows_in")
        expo = Signal(ctx, nc, "dn_row_exponents")
        expd = Signal(ctx, nc, "dn_row_exps")
        block = ctx.enter_context(nc.Block())
        shape = [P, NT, DH, P]

        def heads(x):
            return x[:].rearrange("p t (h d) -> p t h d", h=DH)

        @block.tensor
        def _(pe):
            for h in range(DH):
                sel = k.const("ident", DH, DH)[:, h:h + 1].broadcast_to([DH, P])
                pe.matmul(k.bank[h][:], sel, t.gcT[:], start=True, stop=True).then_inc(spread, 1)
            for i in range(NT):
                pe.transpose(k.bank[4][:, 8 * i:8 * i + 4], t.gcT[:, i * P:(i + 1) * P], k.const("ident", DH, DH))
                last = pe.transpose(k.bank[4][:, 8 * i + 4:8 * i + 8], t.betaT[:, i * P:(i + 1) * P],
                                    k.const("ident", DH, DH))
            last.then_inc(spread, 1)

            def rows(n, bank, block):
                for h in range(DH):
                    last = pe.transpose(k.bank[bank][:, h * P:(h + 1) * P],
                                        t.dT[:, block + h, (n % 4) * P:(n % 4 + 1) * P], k.const("ident"))
                last.then_inc(turned, 1)

            pe.wait_ge(spread_in.sem, 6)
            for n in range(4):
                rows(n, n, 8)
            for j in range(8):
                pe.wait_ge(squared.sem, j + 1)
                if j >= 2:
                    pe.wait_ge(rooted.sem, j - 1)
                pe.matmul(k.bank[5 + j % 2][:], k.const("ones"), sq[:, j % 2, :], start=True, stop=True).then_inc(summed, 1)
            pe.wait_ge(scaled.sem, 8)
            for n in range(4, 8):
                rows(n, n, 4)

        @block.scalar
        def _(act):
            for h in range(DH):
                act.wait_ge(spread, h + 1)
                post(act, act.activation(t.gcB[:, h, :], k.bank[h][:], ACT.Copy), spread_in)
            act.wait_ge(spread, 5)
            v4 = k.bank[4][:, 0:32].rearrange("p (t x) -> p t x", t=NT)
            post(act, act.activation(t.gc_row[:], v4[:, :, 0:4], ACT.Copy), spread_in)
            post(act, act.activation(t.beta_row[:], v4[:, :, 4:8], ACT.Copy), spread_in)
            act.wait_ge(expo.sem, 1)
            post(act, act.activation(t.egl[:], t.egl[:], ACT.Exp), k.astep)
            post(act, act.activation(last_row[:], last_row[:], ACT.Exp), k.astep)
            post(act, act.activation(t.eg_row[:], t.gc_row[:], ACT.Exp), expd)
            post(act, act.activation(t.qgT[:], t.gcB[:], ACT.Exp), expd)

            def rows(n):
                act.wait_ge(turned, n + 1)
                dst = t.v_row if n < 4 else t.k_row
                post(act, act.activation(dst[:, n % 4, :], k.bank[n][:], ACT.Copy), rows_in)

            for j in range(8):
                act.wait_ge(summed, j + 1)
                if j >= 2:
                    act.wait_ge(scaled.sem, j - 1)
                post(act, act.activation(rstd[:, j % 2, :], k.bank[5 + j % 2][:], ACT.Sqrt, bias=k.const("eps")), rooted)
                if j < 4:
                    rows(j)
            for n in range(4, 8):
                rows(n)

        @block.vector
        def _(dve):
            def v(ins):
                post(dve, ins, k.vstep)

            dve.wait_ge(spread_in.sem, 6)
            ends = t.gcB[:].rearrange("p h (n c) -> p h n c", c=CH)[:, :, :, CH - 1]
            v(dve.tensor_copy(t.egl[:], ends))
            for half in range(2):
                ps = slice(CH * half, CH * (half + 1))
                mine = ends.rearrange("p h (t two) -> p t h two", two=2)[ps, :, :, half]
                ins = dve.tensor_tensor(last_row[ps], mine, t.gc_row[ps], ALU.subtract)
                post(dve, ins, expo if half else k.vstep)
            for j in range(8):
                dve.wait_ge(rooted.sem, j + 1)
                v(dve.reciprocal(rstd[:, j % 2, :], rstd[:, j % 2, :]))
                if j < DH:
                    post(dve, dve.scalar_tensor_tensor(t.dT[:, j, :], t.dT[:, j, :], float(P) ** -0.5, rstd[:, j % 2, :],
                                                       ALU.mult, ALU.mult), scaled)
                else:
                    post(dve, dve.tensor_tensor(t.dT[:, j, :], t.dT[:, j, :], rstd[:, j % 2, :], ALU.mult), scaled)
            dve.wait_ge(rows_in.sem, 8)
            dve.wait_ge(expd.sem, 2)
            v(dve.tensor_tensor(heads(t.kdec), heads(t.k_row), bc(last_row[:], 3, shape), ALU.mult))
            v(dve.tensor_tensor(heads(t.k_row), heads(t.k_row), bc(t.beta_row[:], 3, shape), ALU.mult))
            v(dve.tensor_tensor(heads(t.k_row), heads(t.k_row), bc(t.eg_row[:], 3, shape), ALU.mult))

        @block.gpsimd
        def _(pool):
            for j in range(8):
                if j >= 2:
                    pool.wait_ge(summed, j - 1)
                post(pool, pool.tensor_tensor(sq[:, j % 2, :], t.dT[:, j, :], t.dT[:, j, :], ALU.mult), squared)
            pool.wait_ge(rows_in.sem, 4)
            post(pool, pool.tensor_tensor(heads(t.v_row), heads(t.v_row), bc(t.beta_row[:], 3, shape), ALU.mult), k.gstep)
            pool.wait_ge(scaled.sem, 8)
            pool.wait_ge(expd.sem, 2)
            post(pool, pool.tensor_tensor(t.qgT[:], t.qgT[:], t.dT[:, 0:DH, :], ALU.mult), k.gstep)


def delta_solve_stage(k, t):
    nc = k.nc
    levels = ["lvlT2", "lvlT4", "lvlT8", "lvlT16", "lvlT32"]
    n_lvl = len(levels)
    full = [P, DH, P]

    with ExitStack() as ctx:
        class Lane:

            def __init__(self, a):
                def sb(name, spare=None):
                    if a == 1 and spare is not None:
                        return t.dT[:, 2 * DH + spare, :].rearrange("p (h l) -> p h l", h=DH)
                    return ctx.enter_context(nc.sbuf_tensor(f"{name}{a}", full, F32))

                def sem(name):
                    return ctx.enter_context(nc.semaphore(f"{name}{a}"))

                self.dec, self.low, self.lowT = sb("dn_decay"), sb("dn_lower"), sb("dn_lowerT", 0)
                self.x, self.xT = sb("dn_inverse", 1), sb("dn_inverseT", 2)
                self.part, self.yy = self.dec, sb("dn_level_x", 3)
                self.products, self.flipped, self.solved = sem("dn_products"), sem("dn_lower_flipped"), sem("dn_solved")
                self.first, self.second = sem("dn_level_first"), sem("dn_level_second")
                self.diff = Signal(ctx, nc, f"dn_decay_exponents{a}")
                self.exped = Signal(ctx, nc, f"dn_decays{a}")
                self.lowered = Signal(ctx, nc, f"dn_lower_ready{a}")
                self.begun = Signal(ctx, nc, f"dn_level_ready{a}")
                self.first_in = Signal(ctx, nc, f"dn_level_first_in{a}")
                self.inverted = Signal(ctx, nc, f"dn_inverted{a}")
                self.solved_in = Signal(ctx, nc, f"dn_solved_in{a}")
                self.bank = [k.bank[4 * a + j][:].rearrange("p (h l) -> p h l", h=DH) for j in range(4)]

        lanes = [Lane(0), Lane(1)]
        block = ctx.enter_context(nc.Block())
        pairs = range(NT // 2)

        @block.tensor
        def _(pe):
            for r in pairs:
                for a, lane in enumerate(lanes):
                    i = 2 * r + a
                    ts = slice(i * P, (i + 1) * P)
                    if r > 0:
                        pe.wait_ge(lane.solved_in.sem, 2 * r)
                    for h in range(DH):
                        pe.matmul(lane.bank[0][:, h], t.dT[:, DH + h, ts], t.dT[:, DH + h, ts], start=True, stop=True)
                    for h in range(DH):
                        last = pe.matmul(lane.bank[1][:, h], t.dT[:, DH + h, ts], t.dT[:, h, ts], start=True, stop=True)
                    last.then_inc(lane.products, 1)
                for lane in lanes:
                    pe.wait_ge(lane.lowered.sem, r + 1)
                    for h in range(DH):
                        last = pe.transpose(lane.bank[2][:, h], lane.low[:, h], k.const("ident"))
                    last.then_inc(lane.flipped, 1)
                for m in range(n_lvl):
                    for lane in lanes:
                        pe.wait_ge(lane.begun.sem, n_lvl * r + m + 1)
                        for h in range(DH):
                            last = pe.matmul(lane.bank[3][:, h], lane.part[:, h], lane.x[:, h], start=True, stop=True)
                        last.then_inc(lane.first, 1)
                    for lane in lanes:
                        pe.wait_ge(lane.first_in.sem, n_lvl * r + m + 1)
                        for h in range(DH):
                            pe.matmul(lane.bank[0][:, h], lane.xT[:, h], lane.yy[:, h], start=True, stop=True)
                        for h in range(DH):
                            last = pe.matmul(lane.bank[1][:, h], lane.yy[:, h], lane.xT[:, h], start=True, stop=True)
                        last.then_inc(lane.second, 1)
                for a, lane in enumerate(lanes):
                    i = 2 * r + a
                    pe.wait_ge(lane.inverted.sem, r + 1)
                    for h in range(DH):
                        hs = slice(h * P, (h + 1) * P)
                        pe.matmul(lane.bank[2][:, h], lane.xT[:, h], t.v_row[:, i, hs], start=True, stop=True)
                    for h in range(DH):
                        hs = slice(h * P, (h + 1) * P)
                        last = pe.matmul(lane.bank[3][:, h], t.k_row[:, i, hs], lane.xT[:, h], start=True, stop=True)
                    last.then_inc(lane.solved, 1)

        @block.scalar
        def _(act):
            for r in pairs:
                for w in range(2):
                    for lane in lanes:
                        act.wait_ge(lane.diff.sem, 2 * r + w + 1)
                        post(act, act.activation(lane.dec[:], lane.dec[:], ACT.Exp), lane.exped)
                for m in range(n_lvl):
                    for lane in lanes:
                        act.wait_ge(lane.first, n_lvl * r + m + 1)
                        post(act, act.activation(lane.yy[:], lane.bank[3], ACT.Copy), lane.first_in)
                for a, lane in enumerate(lanes):
                    i = 2 * r + a
                    act.wait_ge(lane.solved, r + 1)
                    u3 = t.u[:, i, :].rearrange("p (h d) -> p h d", h=DH)
                    post(act, act.activation(u3, lane.bank[2], ACT.Copy), lane.solved_in)
                    post(act, act.activation(t.wT[:, :, i * P:(i + 1) * P], lane.bank[3], ACT.Copy), lane.solved_in)

        @block.vector
        def _(dve):
            def v(ins):
                post(dve, ins, k.vstep)

            for r in pairs:
                operands = [(lane, 2 * r + a, t.gcB[:, :, (2 * r + a) * P:(2 * r + a + 1) * P],
                             bc(t.gc_row[:, 2 * r + a, :], 2, full)) for a, lane in enumerate(lanes)]
                for lane, i, along, mine in operands:
                    v(dve.tensor_tensor(lane.dec[:], mine, along, ALU.subtract))
                    post(dve, dve.tensor_scalar(lane.dec[:], lane.dec[:], 0.0, None, ALU.min), lane.diff)
                for lane, i, along, mine in operands:
                    low = lane.low
                    dve.wait_ge(lane.exped.sem, 2 * r + 1)
                    dve.wait_ge(lane.products, r + 1)
                    v(dve.tensor_tensor(low[:], lane.bank[0], lane.dec[:], ALU.mult))
                    v(dve.tensor_tensor(low[:], low[:], bc(t.beta_row[:, i, :], 2, full), ALU.mult))
                    post(dve, dve.tensor_tensor(low[:], low[:], bc(k.const("strict64"), 1, full), ALU.mult), lane.lowered)
                    v(dve.tensor_tensor(lane.dec[:], along, mine, ALU.subtract))
                    post(dve, dve.tensor_scalar(lane.dec[:], lane.dec[:], 0.0, None, ALU.min), lane.diff)
                for lane, i, along, mine in operands:
                    dve.wait_ge(lane.exped.sem, 2 * r + 2)
                    v(dve.tensor_tensor(t.at[:, i], lane.bank[1], lane.dec[:], ALU.mult))
                    v(dve.tensor_tensor(t.at[:, i], t.at[:, i], bc(k.const("upper64"), 1, full), ALU.mult))
                    dve.wait_ge(lane.flipped, r + 1)
                    v(dve.tensor_copy(lane.lowT[:], lane.bank[2]))
                    for dst, src, mask in ((lane.x, lane.low, "lvl1"), (lane.xT, lane.lowT, "lvl1T")):
                        v(dve.scalar_tensor_tensor(dst[:], src[:], -1.0, bc(k.const(mask), 1, full), ALU.mult, ALU.mult))
                        v(dve.tensor_tensor(dst[:], dst[:], bc(k.const("ident"), 1, full), ALU.add))
                    post(dve, dve.tensor_tensor(lane.part[:], lane.lowT[:], bc(k.const(levels[0]), 1, full), ALU.mult),
                         lane.begun)
                for m in range(n_lvl):
                    for lane in lanes:
                        dve.wait_ge(lane.second, n_lvl * r + m + 1)
                        last_level = m == n_lvl - 1
                        dve.tensor_tensor(lane.x[:], lane.x[:], lane.bank[0], ALU.subtract)
                        post(dve, dve.tensor_tensor(lane.xT[:], lane.xT[:], lane.bank[1], ALU.subtract),
                             lane.inverted if last_level else k.vstep)
                        if not last_level:
                            mask = bc(k.const(levels[m + 1]), 1, full)
                            post(dve, dve.tensor_tensor(lane.part[:], lane.lowT[:], mask, ALU.mult), lane.begun)


def delta_scan_stage(k, t):
    nc = k.nc
    with ExitStack() as ctx:
        state = ctx.enter_context(nc.sbuf_tensor("dn_state", [P, DH, P], F32))
        vnew = ctx.enter_context(nc.sbuf_tensor("dn_v_new", [P, DH, P], F32))
        kept = Signal(ctx, nc, "dn_state_ready")
        removed = ctx.enter_context(nc.semaphore("dn_state_read"))
        v_ok = Signal(ctx, nc, "dn_v_new_ready")
        added = ctx.enter_context(nc.semaphore("dn_chunk_products"))
        stored = Signal(ctx, nc, "dn_chunk_stored")
        block = ctx.enter_context(nc.Block())

        def b3(i):
            return k.bank[i][:].rearrange("p (h l) -> p h l", h=DH)

        @block.tensor
        def _(pe):
            for n in range(T // CH):
                i, ps = n // 2, slice(CH * (n % 2), CH * (n % 2 + 1))
                cs = slice(n * CH, (n + 1) * CH)
                pe.wait_ge(kept.sem, n + 1)
                for h in range(DH):
                    last = pe.matmul(b3(0)[ps, h], t.wT[:, h, cs], state[:, h], start=True, stop=True)
                last.then_inc(removed, 1)
                if n > 0:
                    pe.wait_ge(stored.sem, n)
                pe.wait_ge(v_ok.sem, n + 1)
                for h in range(DH):
                    pe.matmul(b3(1)[ps, h], t.qgT[:, h, cs], state[:, h], start=True, stop=False)
                    pe.matmul(b3(1)[ps, h], t.at[ps, i, h, ps], vnew[ps, h], start=False, stop=True)
                for h in range(DH):
                    last = pe.matmul(b3(2)[:, h], t.kdec[ps, i, h * P:(h + 1) * P], vnew[ps, h], start=True, stop=True)
                last.then_inc(added, 1)

        @block.vector
        def _(dve):
            post(dve, dve.memset(state[:], 0.0), kept)
            for n in range(T // CH):
                i, ps = n // 2, slice(CH * (n % 2), CH * (n % 2 + 1))
                dve.wait_ge(removed, n + 1)
                u3 = t.u[ps, i, :].rearrange("p (h d) -> p h d", h=DH)
                post(dve, dve.tensor_tensor(vnew[ps], u3, b3(0)[ps], ALU.subtract), v_ok)
                dve.wait_ge(added, n + 1)
                post(dve, dve.tensor_tensor(state[:], state[:], bc(t.egl[:, :, n], 2, [P, DH, P]), ALU.mult), k.vstep)
                post(dve, dve.tensor_tensor(state[:], state[:], b3(2), ALU.add), kept)

        @block.scalar
        def _(act):
            for n in range(T // CH):
                i, ps = n // 2, slice(CH * (n % 2), CH * (n % 2 + 1))
                act.wait_ge(added, n + 1)
                post(act, act.activation(t.ob[ps, i, :], k.bank[1][ps, :], ACT.Copy), stored)


def second_out_stage(k, t):
    nc = k.nc
    with ExitStack() as ctx:
        def sb(name, shape):
            return ctx.enter_context(nc.sbuf_tensor(name, shape, F32))

        sq = sb("mix_squares", [P, NT, 512])
        ss = sb("mix_sums", [P, NT + NT * DH])
        mixT = k.hT
        plan = columns(find(k, "w_out_2", 0, 1024), mixT)
        pj = Projection(k, ctx, "second_out", plan)
        summed = Signal(ctx, nc, "mix_squares_summed")
        rooted = Signal(ctx, nc, "mix_roots")
        inverted = Signal(ctx, nc, "mix_rstd_ready")
        band_ready = Signal(ctx, nc, "band_rows_normed")
        ready = Signal(ctx, nc, "mix_rows_ready")
        turned = ctx.enter_context(nc.semaphore("mix_turned"))
        copied = Signal(ctx, nc, "mix_columns")
        block = ctx.enter_context(nc.Block())

        @block.sync
        def _(sp):
            k.stream(sp, plan[-1][1][-1])

        @block.vector
        def _(dve):
            def v(ins):
                post(dve, ins, k.vstep)

            ob4 = t.ob[:].rearrange("p t (h d) -> p t h d", h=DH)
            v(dve.tensor_tensor(sq[:], t.oa[:], t.oa[:], ALU.mult))
            v(dve.tensor_reduce(ss[:, 0:NT], sq[:], AX, ALU.add))
            v(dve.tensor_tensor(sq[:], t.ob[:], t.ob[:], ALU.mult))
            v(dve.tensor_reduce(ss[:, NT:], sq[:].rearrange("p t (h d) -> p (t h) d", h=DH), AX, ALU.add))
            post(dve, dve.tensor_scalar(ss[:, 0:NT], ss[:, 0:NT], 0.25, None, ALU.mult), summed)
            dve.wait_ge(rooted.sem, 1)
            post(dve, dve.reciprocal(ss[:], ss[:]), inverted)
            r = ss[:, NT:].rearrange("p (t h) -> p t h", t=NT)
            v(dve.tensor_tensor(ob4, ob4, bc(r, 3, [P, NT, DH, P]), ALU.mult))
            post(dve, dve.tensor_tensor(t.ob[:], t.ob[:], t.zb[:], ALU.mult), ready)
            for j in range(8):
                bank = pj.next(dve)
                post(dve, dve.scalar_tensor_tensor(k.xT[:, j, :], bank[:], k.mod2[:, 16 + j:17 + j], k.xT[:, j, :],
                                                   ALU.mult, ALU.add), pj.freed)

        @block.gpsimd
        def _(pool):
            pool.wait_ge(inverted.sem, 1)
            post(pool, pool.tensor_tensor(t.oa[:], t.oa[:], bc(ss[:, 0:NT], 2, [P, NT, 512]), ALU.mult), band_ready)

        @block.scalar
        def _(act):
            act.wait_ge(summed.sem, 1)
            post(act, act.activation(ss[:], ss[:], ACT.Sqrt, bias=k.const("eps"), scale=1.0 / P), rooted)
            for n, j in enumerate((4, 5, 6, 7, 0, 1, 2, 3)):
                gain = k.col("attn_out_gain_2", j) if j < 4 else k.col("dn_out_gain_2")
                act.wait_ge(turned, n + 1)
                post(act, act.activation(mixT[:, j, :], k.bank[j][:], ACT.Copy, scale=gain), copied)

        @block.tensor
        def _(pe):
            for j in (4, 5, 6, 7, 0, 1, 2, 3):
                src = t.oa if j < 4 else t.ob
                pe.wait_ge(band_ready.sem if j < 4 else ready.sem, 1)
                for i in range(NT):
                    last = pe.transpose(k.bank[j][:, i * P:(i + 1) * P], src[:, i, (j % 4) * P:(j % 4 + 1) * P],
                                        k.const("ident"))
                last.then_inc(turned, 1)
            pe.wait_ge(copied.sem, 8)
            pj.run(pe)


def second_mixer(k):
    nc = k.nc
    with ExitStack() as ctx:
        def sb(name, shape):
            return ctx.enter_context(nc.sbuf_tensor(name, shape, F32))

        t = Part()
        t.rel_scratch = nc.dram_tensor("rel_bias_scratch", (BH, 384), F32, kind="Internal").ap()
        t.zb = sb("silu_z_b", [P, NT, 512])
        t.betaT, t.gcT = sb("betaT", [DH, T]), sb("gcT", [DH, T])
        t.oa = sb("band_out", [P, NT, 512])
        t.dT = sb("delta_qkvT", [P, 12, T])
        with ExitStack() as bctx:
            def bsb(name, shape):
                return bctx.enter_context(nc.sbuf_tensor(name, shape, F32))

            t.qa, t.ka, t.va = (bsb(n, [P, NT, 512]) for n in ("band_q", "band_k", "band_v"))
            t.near = bsb("near_bias", [P, BH, 256])
            t.near_in = bctx.enter_context(nc.semaphore("near_bias_in"))
            second_projection_stage(k, t)
            t.qaT, t.kaT = k.hT[:, 0:4, :], k.hT[:, 4:8, :]
            band_setup_stage(k, t)
            band_attention_stage(k, t)
        t.gcB = sb("gc_spread", [P, DH, T])
        t.gc_row, t.beta_row, t.eg_row = (sb(n, [P, NT, DH]) for n in ("gc_rows", "beta_rows", "exp_gc_rows"))
        t.egl = sb("exp_gc_chunk_end", [P, DH, T // CH])
        t.k_row, t.v_row = (sb(n, [P, NT, 512]) for n in ("dn_k_rows", "dn_v_rows"))
        t.kdec, t.qgT = k.hT[:, 0:4, :], k.hT[:, 4:8, :]
        delta_setup_stage(k, t)
        t.u = sb("dn_u", [P, NT, 512])
        t.wT = sb("dn_wT", [P, DH, T])
        t.at = sb("dn_intraT", [P, NT, DH, P])
        delta_solve_stage(k, t)
        t.ob = sb("dn_out", [P, NT, 512])
        delta_scan_stage(k, t)
        second_out_stage(k, t)


def expert_rows_stage(k, t):
    nc = k.nc
    with ExitStack() as ctx:
        turned = ctx.enter_context(nc.semaphore("rows_back_turned"))
        copied = [Signal(ctx, nc, "rows_back_even"), Signal(ctx, nc, "rows_back_odd")]
        block = ctx.enter_context(nc.Block())
        jobs = [(src, dst, i, half) for src, dst in ((k.hT, t.h_row), (k.xT, t.x_row)) for i in range(NT)
                for half in range(2)]

        @block.tensor
        def _(pe):
            for n, (src, _, i, half) in enumerate(jobs):
                if n >= 8:
                    pe.wait_ge(copied[n % 2].sem, (n - 8) // 2 + 1)
                for j in range(4):
                    last = pe.transpose(k.bank[n % 8][:, j * P:(j + 1) * P], src[:, 4 * half + j, i * P:(i + 1) * P],
                                        k.const("ident"))
                last.then_inc(turned, 1)

        @block.scalar
        def _(act):
            for n, (_, dst, i, half) in list(enumerate(jobs))[0::2]:
                act.wait_ge(turned, n + 1)
                act.activation(dst[:, i, half * 512:(half + 1) * 512], k.bank[n % 8][:], ACT.Copy).then_inc(copied[0].sem, 1)

        @block.vector
        def _(dve):
            for n, (_, dst, i, half) in list(enumerate(jobs))[1::2]:
                dve.wait_ge(turned, n + 1)
                dve.tensor_copy(dst[:, i, half * 512:(half + 1) * 512], k.bank[n % 8][:]).then_inc(copied[1].sem, 1)


def query_stage(k, t):
    nc, d = k.nc, k.dram
    with ExitStack() as ctx:
        def sb(name, shape):
            return ctx.enter_context(nc.sbuf_tensor(name, shape, F32))

        qT = sb("queriesT", [P, 2 * RH, T])
        sq = sb("query_squares", [P, 2, 2, T])
        keys = sb("sub_keys", [P, 2, P])
        keyT = sb("sub_keysT", [P, 2, P])
        keys_in = ctx.enter_context(nc.semaphore("sub_keys_loaded"))
        keys_turned = ctx.enter_context(nc.semaphore("sub_keys_turned"))
        keys_ok = Signal(ctx, nc, "sub_keys_ready")
        squared = Signal(ctx, nc, "queries_squared")
        summed = ctx.enter_context(nc.semaphore("query_squares_summed"))
        rooted = Signal(ctx, nc, "query_roots")
        scored = ctx.enter_context(nc.semaphore("key_scores_made"))
        plan = columns(find(k, "peer_w_query_2", 0, 2048), k.hT)
        pj = Projection(k, ctx, "queries", plan, banks=range(6))
        block = ctx.enter_context(nc.Block())

        @block.sync
        def _(sp):
            sp.dma_start(keys[:, 0, :], d["peer_sub_keys_1_2"]).then_inc(keys_in, 16)
            sp.dma_start(keys[:, 1, :], d["peer_sub_keys_2_2"]).then_inc(keys_in, 16)
            k.stream(sp, plan[-1][1][-1])

        @block.tensor
        def _(pe):
            def sums(h):
                pe.wait_ge(squared.sem, 2 * (h + 1))
                for i in range(NT):
                    for half in range(2):
                        last = pe.matmul(k.bank[6][:, i * RH + h:i * RH + h + 1],
                                         sq[:, h % 2, half, i * P:(i + 1) * P], k.const("ones", 1),
                                         start=(half == 0), stop=(half == 1))
                last.then_inc(summed, 1)

            for n in range(4):
                pj.run(pe, slice(n, n + 1))
                if n == 0:
                    pe.wait_ge(keys_in, 32)
                    for w in range(2):
                        last = pe.transpose(k.bank[7][:, w * P:(w + 1) * P], keys[:, w, :], k.const("ident"))
                    last.then_inc(keys_turned, 1)
                for h in ((2 * n - 2, 2 * n - 1) if n else ()):
                    sums(h)
            sums(6)
            sums(7)
            pe.wait_ge(pj.freed.sem, 16)
            pe.wait_ge(keys_ok.sem, 2)
            for n in range(4 * NT):
                i, quarter = n // 4, n % 4
                bank = k.bank[n % 6]
                if n >= 6:
                    pe.wait_ge(t.scores_in.sem, n - 5)
                for j in range(4):
                    b = 4 * quarter + j
                    last = pe.matmul(bank[:, j * P:(j + 1) * P], qT[:, b, i * P:(i + 1) * P], keyT[:, b % 2, :],
                                     start=True, stop=True)
                last.then_inc(scored, 1)

        @block.scalar
        def _(act):
            for b in range(2 * RH):
                bank = pj.next(act)
                post(act, act.activation(qT[:, b, :], bank[:], ACT.Copy), pj.freed)
            act.wait_ge(keys_turned, 1)
            for w in range(2):
                post(act, act.activation(keyT[:, w, :], k.bank[7][:, w * P:(w + 1) * P], ACT.Copy,
                                         scale=k.col("peer_query_gain_2", w)), keys_ok)
            act.wait_ge(summed, RH)
            post(act, act.activation(t.q_rstd[:], k.bank[6][:, 0:NT * RH], ACT.Sqrt, bias=k.const("eps"),
                                     scale=1.0 / (2 * P)), rooted)
            for n in range(4 * NT):
                i, quarter = n // 4, n % 4
                act.wait_ge(scored, n + 1)
                post(act, act.activation(t.scores[:, i, quarter * 512:(quarter + 1) * 512], k.bank[n % 6][:], ACT.Copy),
                     t.scores_in)

        @block.vector
        def _(dve):
            for b in range(2 * RH):
                h, half = b // 2, b % 2
                dve.wait_ge(pj.freed.sem, b + 1)
                if h >= 2 and half == 0:
                    dve.wait_ge(summed, h - 1)
                post(dve, dve.tensor_tensor(sq[:, h % 2, half, :], qT[:, b, :], qT[:, b, :], ALU.mult), squared)
            dve.wait_ge(rooted.sem, 1)
            post(dve, dve.reciprocal(t.q_rstd[:], t.q_rstd[:]), k.vstep)


def expert_stage(k, t):
    nc, d = k.nc, k.dram
    GR = 16
    with ExitStack() as ctx:
        def sb(name, shape, dt=F32):
            return ctx.enter_context(nc.sbuf_tensor(name, shape, dt))

        more = sb("more_expert_rows", [P, GR - 4 * SLOTS, D])
        slot = [r[:, 2 * a:2 * a + 2, :].rearrange("p a b -> p (a b)") for r in k.ring for a in range(4)]
        slot += [more[:, a, :] for a in range(GR - 4 * SLOTS)]
        diag = sb("coef_diagonals", [P, RK, P])
        experts = sb("experts", [P, NT, NSEL], I32)
        gates = sb("expert_gates", [P, NT, NSEL])
        dots = sb("expert_dots", [P, 2, RK])
        coef = sb("expert_coefs", [P, 2, RK])
        left = sb("scores_left_over", [P, RK * RK])
        vals = sb("key_values", [P, 2, RK])
        kidx = sb("key_indices", [P, 2, RK], U32)
        kidx_f = sb("key_indices_f", [P, 2, RK])
        cand = sb("pair_scores", [P, RK, RK])
        ctop = sb("pair_top", [P, RK])
        cpos = sb("pair_positions", [P, RK], U32)
        part = sb("pair_parts", [P, RK], U32)
        part_f = sb("pair_parts_f", [P, RK])
        picked = sb("key_picked", [P, 2, RK])
        gsum = sb("gate_sums", [P, 1])
        here = [ctx.enter_context(nc.semaphore(f"expert_row_in{s}")) for s in range(GR)]
        routed = Signal(ctx, nc, "unit_routed")
        soft_in = Signal(ctx, nc, "gate_exponents")
        soft_out = Signal(ctx, nc, "gate_exps")
        dotted = Signal(ctx, nc, "expert_dots_made")
        gelued = Signal(ctx, nc, "expert_gelus")
        weighed = Signal(ctx, nc, "expert_coefs_ready")
        diag_ok = Signal(ctx, nc, "coef_diagonal_ready")
        summed = ctx.enter_context(nc.semaphore("expert_row_summed"))
        written = Signal(ctx, nc, "tile_result")
        out_ok = k.output_stored
        block = ctx.enter_context(nc.Block())
        out2 = k.out[0].rearrange("(t p) d -> p t d", p=P)
        units = [(i, h) for i in range(NT) for h in range(RH)]
        N = len(units)

        order = [("down", 0, s) for s in range(RK)]
        for u in range(N):
            for s in range(RK):
                if u + 1 < N:
                    order.append(("down", u + 1, s))
                order.append(("up", u, s))
        place = {job: n for n, job in enumerate(order)}

        @block.gpsimd
        def _(pool):
            for n, (kind, u, s) in enumerate(order):
                if kind == "down" and s == 0:
                    pool.wait_ge(routed.sem, u + 1)
                if n >= GR:
                    old_kind, old_u, old_s = order[n - GR]
                    pool.wait_ge(dotted.sem if old_kind == "down" else summed, old_u * RK + old_s + 1)
                i, h = units[u]
                j = h * RK + s
                pool.indirect_dma_start(
                    out=slot[n % GR], out_offset=None, in_=d[f"peer_expert_{kind}_2"],
                    in_offset=bass.IndirectOffsetOnAxis(ap=experts[:, i, j:j + 1], axis=0),
                ).then_inc(here[n % GR], 16)

        def arrived(eng, job):
            n = place[job]
            eng.wait_ge(here[n % GR], 16 * (n // GR + 1))
            return slot[n % GR]

        @block.vector
        def _(dve):
            def v(ins):
                post(dve, ins, k.vstep)

            def top16(values, indices, source, width):
                v(dve.max(values[:, 0:8], source))
                v(dve.max_index(indices[:, 0:8], values[:, 0:8], source))
                v(dve.match_replace(left[:, 0:width], values[:, 0:8], source, -3.0e38))
                v(dve.max(values[:, 8:16], left[:, 0:width]))
                v(dve.max_index(indices[:, 8:16], values[:, 8:16], left[:, 0:width]))

            def route(u):
                i, h = units[u]
                for w in range(2):
                    b = 2 * h + w
                    top16(vals[:, w, :], kidx[:, w, :], t.scores[:, i, b * NKEY:(b + 1) * NKEY], NKEY)
                shape = [P, RK, RK]
                v(dve.tensor_tensor(cand[:], bc(vals[:, 0], 2, shape), bc(vals[:, 1], 1, shape), ALU.add))
                top16(ctop[:], cpos[:], cand[:].rearrange("p a b -> p (a b)"), RK * RK)
                v(dve.tensor_copy(kidx_f[:], kidx[:]))
                for w, (op, by) in enumerate(((ALU.logical_shift_right, 4), (ALU.bitwise_and, 15))):
                    v(dve.tensor_scalar(part[:], cpos[:], by, None, op))
                    v(dve.tensor_copy(part_f[:], part[:]))
                    v(dve.tensor_tensor(cand[:], bc(k.const("iota16"), 1, shape), bc(part_f[:], 2, shape), ALU.is_equal))
                    v(dve.tensor_tensor(cand[:], cand[:], bc(kidx_f[:, w], 1, shape), ALU.mult))
                    v(dve.tensor_reduce(picked[:, w], cand[:], AX, ALU.add))
                mine = slice(h * RK, (h + 1) * RK)
                post(dve, dve.scalar_tensor_tensor(experts[:, i, mine], picked[:, 0], float(NKEY), picked[:, 1],
                                                   ALU.mult, ALU.add), routed)
                at = i * RH + h
                post(dve, dve.tensor_scalar(gates[:, i, mine], ctop[:], ctop[:, 0:1], t.q_rstd[:, at:at + 1],
                                            ALU.subtract, ALU.mult), soft_in)

            def dot(u):
                i, _ = units[u]
                for s in range(RK):
                    row = arrived(dve, ("down", u, s))
                    if u >= 2 and s == 0:
                        dve.wait_ge(weighed.sem, u - 1)
                    post(dve, dve.tensor_tensor_reduce(row, row, t.h_row[:, i, :], 1.0, 0.0, ALU.mult, ALU.add,
                                                       dots[:, u % 2, s:s + 1]), dotted)

            def weigh(u):
                i, h = units[u]
                g = gates[:, i, h * RK:(h + 1) * RK]
                dve.wait_ge(soft_out.sem, u + 1)
                v(dve.tensor_reduce(gsum[:], g, AX, ALU.add))
                v(dve.reciprocal(gsum[:], gsum[:]))
                dve.wait_ge(gelued.sem, u + 1)
                if u >= 2:
                    dve.wait_ge(diag_ok.sem, (u - 1) * RK)
                post(dve, dve.scalar_tensor_tensor(coef[:, u % 2, :], dots[:, u % 2, :], gsum[:], g,
                                                   ALU.mult, ALU.mult), weighed)

            def finish(i):
                dve.wait_ge(summed, (i + 1) * NSEL)
                for half in range(2):
                    hs = slice(half * 512, (half + 1) * 512)
                    v(dve.tensor_tensor(t.result[:, hs], k.bank[2 * (i % 2) + half][:], k.gate2[:, hs], ALU.mult))
                post(dve, dve.tensor_tensor(t.x_row[:, i, :], t.x_row[:, i, :], t.result[:], ALU.add), written)

            route(0)
            route(1)
            for u in range(N):
                dot(u)
                weigh(u)
                if u + 2 < N:
                    route(u + 2)
                if u > 0 and units[u][1] == 0:
                    finish(units[u][0] - 1)
            finish(NT - 1)

        @block.scalar
        def _(act):
            def soft(u):
                i, h = units[u]
                act.wait_ge(soft_in.sem, u + 1)
                g = gates[:, i, h * RK:(h + 1) * RK]
                post(act, act.activation(g, g, ACT.Exp), soft_out)

            soft(0)
            soft(1)
            for u in range(N):
                act.wait_ge(dotted.sem, (u + 1) * RK)
                post(act, act.activation(dots[:, u % 2, :], dots[:, u % 2, :], ACT.Gelu), gelued)
                act.wait_ge(weighed.sem, u + 1)
                for s in range(RK):
                    if u > 0:
                        act.wait_ge(summed, (u - 1) * RK + s + 1)
                    act.activation(diag[:, s, :], k.const("ident"), ACT.Copy,
                                   scale=coef[:, u % 2, s:s + 1]).then_inc(diag_ok.sem, 1)
                    diag_ok.n += 1
                if u + 2 < N:
                    soft(u + 2)

        @block.tensor
        def _(pe):
            for u, (i, h) in enumerate(units):
                if i >= 2 and h == 0:
                    pe.wait_ge(written.sem, i - 1)
                for s in range(RK):
                    row = arrived(pe, ("up", u, s))
                    pe.wait_ge(diag_ok.sem, u * RK + s + 1)
                    for half in range(2):
                        last = pe.matmul(k.bank[2 * (i % 2) + half][:], diag[:, s, :],
                                         row[:, half * 512:(half + 1) * 512],
                                         start=(h == 0 and s == 0), stop=(h == RH - 1 and s == RK - 1))
                    last.then_inc(summed, 1)

        @block.sync
        def _(sp):
            for i in range(NT):
                sp.wait_ge(written.sem, i + 1)
                sp.dma_start(out2[:, i, :], t.x_row[:, i, :]).then_inc(out_ok, 16)
            sp.wait_ge(out_ok, 16 * NT)


def expert_branch(k):
    nc = k.nc
    with ExitStack() as ctx:
        def sb(name, shape):
            return ctx.enter_context(nc.sbuf_tensor(name, shape, F32))

        t = Part()
        t.h_row, t.x_row = sb("h_rows", [P, NT, D]), sb("x_out_rows", [P, NT, D])
        t.scores = sb("key_scores", [P, NT, 2 * RH * NKEY])
        t.q_rstd = sb("query_rstd", [P, NT * RH])
        t.scores_in = Signal(ctx, nc, "key_scores_in")
        expert_rows_stage(k, t)
        query_stage(k, t)
        t.result = k.xT[:, 0:2, :].rearrange("p a b -> p (a b)")
        expert_stage(k, t)


def recycle(nc):
    ids = sorted(set(nc.released_uncleared_semaphores))
    runs = []
    for n in ids:
        if runs and runs[-1][1] == n:
            runs[-1][1] = n + 1
        else:
            runs.append([n, n + 1])
    for first, end in runs:
        nc.gpsimd.sem_clear(range(first, end))
    nc.all_engine_barrier()


def build(nc, dram, out):
    with ExitStack() as ctx:
        k = Kernel(nc, ctx, dram, out)
        load_stage(k)
        norm_stage(k, "norm1", "norm_g", k.mod1, 0, 8)
        with nc.sbuf_tensor("merged", [P, KD, T], F32) as k.merged:
            attention_branch(k)
            recycle(nc)
            ssm_branch(k)
        recycle(nc)
        norm_stage(k, "norm2", "norm1_gain_2", k.mod2, 0, 8)
        second_mixer(k)
        recycle(nc)
        norm_stage(k, "norm3", "norm2_gain_2", k.mod2, 24, 32)
        expert_branch(k)


def _tables():
    p = np.arange(P)
    row, colm = p[:, None], p[None, :]
    same64 = (row // 64) == (colm // 64)
    m = {"ident": np.eye(P), "flip": np.eye(P)[::-1], "ones": np.ones((P, P)), "causal_add": np.where(colm <= row, 0.0, NEG),
         "s_le_l": (row <= colm), "strict64": same64 & (colm < row), "upper64": same64 & (row <= colm),
         "iota16": np.tile(np.arange(16), (P, 1)), "eps": np.full((P, 1), EPS),
         "band_add": np.where((colm // 64) <= (row // 64), 0.0, NEG)}
    f = np.float32

    def inv(n):
        return np.power(f(500000.0), -(np.arange(0, n, 2, dtype=f) / f(n))).astype(f)

    m["inv_freq"] = np.tile(np.concatenate([inv(32), inv(16)]), (P, 1))
    for size in (1, 2, 4, 8, 16, 32):
        low = ((row // (2 * size)) == (colm // (2 * size))) & (row % (2 * size) >= size) & (colm % (2 * size) < size)
        if size == 1:
            m["lvl1"], m["lvl1T"] = low, low.T
        else:
            m[f"lvlT{size}"] = low.T
    return np.concatenate([np.asarray(m[n], f).reshape(P, w) for n, w in CONSTS], axis=1)


_DIRECT = ["x", "positions", "ada_w", "w_in", "w_branch_att", "w_branch_ssm", "w_out", "w_ada_2", "w_in_2",
           "w_out_2", "attn_rel_bias_2", "peer_w_query_2", "peer_sub_keys_1_2", "peer_sub_keys_2_2",
           "peer_expert_down_2", "peer_expert_up_2"]


def _layout(inputs):
    a = {n: np.asarray(v) for n, v in inputs.items()}
    out = {"consts": _tables()}
    for n in _DIRECT:
        v = a[n]
        out[n] = np.ascontiguousarray(v[0] if v.ndim == 3 else v)
    for n in ("peer_sub_keys_1_2", "peer_sub_keys_2_2", "peer_expert_down_2", "peer_expert_up_2", "attn_rel_bias_2"):
        out[n] = np.ascontiguousarray(a[n][0])

    out["positions"] = np.ascontiguousarray(a["positions"].reshape(NT, P).T)

    out["rel_bias_reversed"] = np.ascontiguousarray(out.pop("attn_rel_bias_2")[:, ::-1])

    def columns_of(n, w):
        if n in ("conv_w", "dn_conv_w_2"):
            v = a[n][0]
            return v.reshape(4, -1, P).transpose(2, 0, 1).reshape(P, w)
        v = a[n].reshape(-1)
        if v.size < P:
            full = np.zeros(P, v.dtype)
            full[:v.size] = v
            v = full
        return v.reshape(w, P).T

    out["cols"] = np.ascontiguousarray(np.concatenate([columns_of(n, w) for n, w in COLS], axis=1))
    rows = {n: a[n].reshape(-1) for n, _ in ROWS if n in a}
    rows["gate2_b"] = a["b_ada_2"].reshape(-1)[5 * D:6 * D]
    rows["rel_far"] = a["attn_rel_bias_2"][0][:, 256]
    out["rows"] = np.ascontiguousarray(np.concatenate([rows[n] for n, _ in ROWS])[None, :])
    return out


def kernel(**inputs):
    import concourse.bacc as _bacc
    from concourse.bass_utils import run_bass_kernel_spmd as _run

    nc = _bacc.Bacc("TRN2", target_bir_lowering=False, num_devices=1)
    arrays = _layout(inputs)
    dram = {n: nc.dram_tensor(f"in_{n}", a.shape, mybir.dt.from_np(a.dtype), kind="ExternalInput").ap()
            for n, a in arrays.items()}
    out = nc.dram_tensor("out", (1, T, D), F32, kind="ExternalOutput").ap()
    build(nc, dram, out)
    r = _run(nc, [{f"in_{n}": a for n, a in arrays.items()}], core_ids=[0])
    return r.results[0]["out"]
```
